# Optimizing a Trainium2 kernel written in Bass

```python
import jax, jax.numpy as jnp
from jax import lax
import numpy as np
import math
import jax
import jax.numpy as jnp

D_MODEL = 1024
BATCH = 1
SEQ = 256
DEPTH = 1

N_META = 16
BLOCK = 128
LEAD_PAD = BLOCK - N_META
SB_HEAD_DIM = 64
SB_WIDTH = D_MODEL // 2
SB_HEADS = SB_WIDTH // SB_HEAD_DIM
HG_HEAD_DIM = 128
HG_WIDTH = D_MODEL - SB_WIDTH
HG_HEADS = HG_WIDTH // HG_HEAD_DIM
MIX_WIDTH = SB_WIDTH + HG_WIDTH
IN_SPLITS = [SB_WIDTH, SB_WIDTH, SB_WIDTH, HG_WIDTH, HG_WIDTH, HG_WIDTH, HG_WIDTH]
IN_PROJ_WIDTH = sum(IN_SPLITS)
N_GROUPS = 4
EXPERTS_PER_GROUP = 8
N_EXPERTS = N_GROUPS * EXPERTS_PER_GROUP
TOP_K_IN_GROUP = 2
EXPERT_FF = D_MODEL // 2
MOE_BLOCK = 128
EPS = 1e-6


def rmsnorm(x, gain):
    xf = x.astype(jnp.float32)
    y = xf * lax.rsqrt(jnp.mean(xf * xf, axis=-1, keepdims=True) + EPS)
    return (y * gain.astype(jnp.float32)).astype(x.dtype)

def split_heads(t, n_heads, head_dim):
    b, l, _ = t.shape
    return t.reshape(b, l, n_heads, head_dim).transpose(0, 2, 1, 3)

def merge_heads_norm(o, gain):
    b, h, l, d = o.shape
    o = rmsnorm(o.transpose(0, 2, 1, 3), gain.reshape(h, d))
    return o.reshape(b, l, h * d)

def stick_breaking_attention(q, k, v):
    L = q.shape[2]
    scale = SB_HEAD_DIM ** -0.5
    outs = []
    for blk in range(L // BLOCK):
        t0 = blk * BLOCK
        t1 = t0 + BLOCK
        z = jnp.einsum('bhtd,bhsd->bhts', q[:, :, t0:t1], k[:, :, :t1]).astype(jnp.float32) * scale
        t_pos = jnp.arange(t0, t1)[:, None]
        s_pos = jnp.arange(t1)[None, :]
        valid = (s_pos < t_pos) & (s_pos >= LEAD_PAD)
        log_beta = jax.nn.log_sigmoid(z)
        log_keep = jnp.where(valid, jax.nn.log_sigmoid(-z), 0.0)
        log_tail = lax.cumsum(log_keep, axis=3, reverse=True) - log_keep
        w = jnp.where(valid, jnp.exp(log_beta + log_tail), 0.0)
        outs.append(jnp.einsum('bhts,bhsd->bhtd', w.astype(v.dtype), v[:, :, :t1]))
    return jnp.concatenate(outs, axis=2)

def hgrn2_chunked(q, k, v, log_f):
    b, h, L, dk = q.shape
    dv = v.shape[-1]
    nc = L // BLOCK

    def to_chunks(t):
        return jnp.moveaxis(t.reshape(b, h, nc, BLOCK, t.shape[-1]), 2, 0)

    causal = jnp.tril(jnp.ones((BLOCK, BLOCK), bool))[:, :, None]

    def step(state, inp):
        qc, kc, vc, gc = inp
        bc = jnp.cumsum(gc, axis=2)
        diff = bc[:, :, :, None, :] - bc[:, :, None, :, :]
        decay = jnp.exp(jnp.where(causal, diff, -jnp.inf))
        scores = jnp.einsum('bhtd,bhsd,bhtsd->bhts', qc, kc, decay)
        o = jnp.einsum('bhts,bhsv->bhtv', scores, vc) + jnp.einsum('bhtd,bhdv->bhtv', qc * jnp.exp(bc), state)
        b_last = bc[:, :, -1, :]
        state = jnp.exp(b_last)[..., None] * state + jnp.einsum(
            'bhsd,bhsv->bhdv', kc * jnp.exp(b_last[:, :, None, :] - bc), vc)
        return state, o

    s0 = jnp.zeros((b, h, dk, dv), jnp.float32)
    _, o = lax.scan(step, s0, (to_chunks(q), to_chunks(k), to_chunks(v), to_chunks(log_f)))
    return jnp.moveaxis(o, 0, 2).reshape(b, h, L, dv)

def hierarchical_moe(x2, w_rg, b_rg, w_re, b_re, w_gate, w_up, w_down):
    n_tok = x2.shape[0]
    grp_probs = jax.nn.softmax(jnp.dot(x2, w_rg).astype(jnp.float32) + b_rg.astype(jnp.float32), axis=-1)
    grp = jnp.argmax(grp_probs, axis=-1)
    p_grp = jnp.max(grp_probs, axis=-1)
    exp_logits = (jnp.dot(x2, w_re).astype(jnp.float32) + b_re.astype(jnp.float32)).reshape(
        n_tok, N_GROUPS, EXPERTS_PER_GROUP)
    in_grp = exp_logits[jnp.arange(n_tok), grp]
    top_val, top_idx = lax.top_k(in_grp, TOP_K_IN_GROUP)
    gate = jax.nn.softmax(top_val, axis=-1) * p_grp[:, None]
    expert_id = (grp[:, None] * EXPERTS_PER_GROUP + top_idx).reshape(-1).astype(jnp.int32)
    gate_flat = gate.reshape(-1)
    token_id = jnp.repeat(jnp.arange(n_tok, dtype=jnp.int32), TOP_K_IN_GROUP)
    n_assign = n_tok * TOP_K_IN_GROUP
    n_slots = -(-n_assign // MOE_BLOCK) * MOE_BLOCK + N_EXPERTS * MOE_BLOCK
    n_blocks = n_slots // MOE_BLOCK
    counts = jnp.zeros((N_EXPERTS,), jnp.int32).at[expert_id].add(1)
    padded = (counts + MOE_BLOCK - 1) // MOE_BLOCK * MOE_BLOCK
    padded_end = jnp.cumsum(padded)
    padded_start = padded_end - padded
    start = jnp.cumsum(counts) - counts
    order = jnp.argsort(expert_id)
    sorted_e = expert_id[order]
    dest = padded_start[sorted_e] + jnp.arange(n_assign, dtype=jnp.int32) - start[sorted_e]
    slot_tok = jnp.zeros((n_slots,), jnp.int32).at[dest].set(token_id[order])
    slot_gate = jnp.zeros((n_slots,), jnp.float32).at[dest].set(gate_flat[order])
    block_e = jnp.clip(jnp.searchsorted(padded_end, jnp.arange(n_blocks, dtype=jnp.int32) * MOE_BLOCK,
                                        side='right'), 0, N_EXPERTS - 1)

    def run_block(args):
        tok, g, e = args
        xb = x2[tok]
        hb = jax.nn.silu(xb @ w_gate[e]) * (xb @ w_up[e])
        return (hb @ w_down[e]) * g[:, None].astype(x2.dtype)

    y_blocks = lax.map(run_block, (slot_tok.reshape(n_blocks, MOE_BLOCK),
                                   slot_gate.reshape(n_blocks, MOE_BLOCK), block_e))
    return jnp.zeros_like(x2).at[slot_tok].add(y_blocks.reshape(n_slots, -1))

def first_inputs(seed: int = 0) -> dict:
    key = jax.random.key(seed)
    ks = jax.random.split(key, 18)
    f32 = jnp.float32

    def nrm(k, shape, scale):
        return jax.random.normal(k, shape, f32) * scale

    return {
        'x': nrm(ks[0], (BATCH, SEQ, D_MODEL), 1.0),
        'meta_tokens': nrm(ks[1], (N_META, D_MODEL), 1.0),
        'lb_logits': nrm(ks[2], (DEPTH + 1, HG_WIDTH), 0.1).at[-1].add(2.0),
        'g_mix': 1.0 + nrm(ks[3], (DEPTH, D_MODEL), 0.02),
        'w_in': nrm(ks[4], (DEPTH, D_MODEL, IN_PROJ_WIDTH), D_MODEL ** -0.5),
        'sb_gain': 1.0 + nrm(ks[5], (DEPTH, SB_WIDTH), 0.02),
        'hg_gain': 1.0 + nrm(ks[6], (DEPTH, HG_WIDTH), 0.02),
        'w_out': nrm(ks[7], (DEPTH, MIX_WIDTH, D_MODEL), MIX_WIDTH ** -0.5),
        'g_ffn': 1.0 + nrm(ks[8], (DEPTH, D_MODEL), 0.02),
        'w_router_group': nrm(ks[9], (DEPTH, D_MODEL, N_GROUPS), D_MODEL ** -0.5),
        'b_router_group': nrm(ks[10], (DEPTH, N_GROUPS), 0.01),
        'w_router_expert': nrm(ks[11], (DEPTH, D_MODEL, N_EXPERTS), D_MODEL ** -0.5),
        'b_router_expert': nrm(ks[12], (DEPTH, N_EXPERTS), 0.01),
        'w_expert_gate': nrm(ks[13], (DEPTH, N_EXPERTS, D_MODEL, EXPERT_FF), D_MODEL ** -0.5),
        'w_expert_up': nrm(ks[14], (DEPTH, N_EXPERTS, D_MODEL, EXPERT_FF), D_MODEL ** -0.5),
        'w_expert_down': nrm(ks[15], (DEPTH, N_EXPERTS, EXPERT_FF, D_MODEL), EXPERT_FF ** -0.5),
        'g_final': 1.0 + nrm(ks[16], (D_MODEL,), 0.02),
    }

def first_block(x, meta_tokens, lb_logits, g_mix, w_in, sb_gain, hg_gain, w_out, g_ffn,
              w_router_group, b_router_group, w_router_expert, b_router_expert,
              w_expert_gate, w_expert_up, w_expert_down, g_final):
    b = x.shape[0]
    lead = jnp.zeros((b, LEAD_PAD, D_MODEL), x.dtype)
    meta = jnp.broadcast_to(meta_tokens.astype(x.dtype)[None], (b, N_META, D_MODEL))
    h = jnp.concatenate([lead, meta, x], axis=1)
    L = h.shape[1]
    real = (jnp.arange(L) >= LEAD_PAD)[None, :, None]
    lower_bounds = jnp.cumsum(jax.nn.softmax(lb_logits.astype(jnp.float32), axis=0), axis=0)
    split_idx = np.cumsum(IN_SPLITS)[:-1].tolist()

    for layer in range(DEPTH):
        a = rmsnorm(h, g_mix[layer])
        proj = jnp.einsum('bld,de->ble', a, w_in[layer])
        sb_q, sb_k, sb_v, hg_q, hg_f, hg_i, hg_g = jnp.split(proj, split_idx, axis=-1)

        o_sb = stick_breaking_attention(split_heads(sb_q, SB_HEADS, SB_HEAD_DIM),
                                        split_heads(sb_k, SB_HEADS, SB_HEAD_DIM),
                                        split_heads(sb_v, SB_HEADS, SB_HEAD_DIM))
        o_sb = merge_heads_norm(o_sb, sb_gain[layer]).astype(proj.dtype)

        lb = lower_bounds[layer]
        f_pre = hg_f.astype(jnp.float32)
        log_f = jnp.log(lb + (1.0 - lb) * jax.nn.sigmoid(f_pre))
        k_in = jnp.where(real, (1.0 - lb) * jax.nn.sigmoid(-f_pre), 0.0)
        q_in = jax.nn.silu(hg_q.astype(jnp.float32))
        o_hg = hgrn2_chunked(split_heads(q_in, HG_HEADS, HG_HEAD_DIM),
                             split_heads(k_in, HG_HEADS, HG_HEAD_DIM),
                             split_heads(hg_i.astype(jnp.float32), HG_HEADS, HG_HEAD_DIM),
                             split_heads(log_f, HG_HEADS, HG_HEAD_DIM))
        o_hg = (merge_heads_norm(o_hg, hg_gain[layer]) * jax.nn.silu(hg_g.astype(jnp.float32))).astype(proj.dtype)

        mixed = jnp.concatenate([o_sb, o_hg], axis=-1)
        h = h + jnp.einsum('ble,ed->bld', mixed, w_out[layer])

        m = rmsnorm(h[:, LEAD_PAD:], g_ffn[layer])
        n_pos = m.shape[1]
        y = hierarchical_moe(m.reshape(b * n_pos, D_MODEL), w_router_group[layer], b_router_group[layer],
                             w_router_expert[layer], b_router_expert[layer], w_expert_gate[layer],
                             w_expert_up[layer], w_expert_down[layer])
        h = h + jnp.pad(y.reshape(b, n_pos, D_MODEL), ((0, 0), (LEAD_PAD, 0), (0, 0)))

    out = rmsnorm(h[:, BLOCK:], g_final)
    return out


DEPTH_2 = 2

N_MEM = 256
HEAD_DIM = 64
MAIN_W = 3 * D_MODEL // 4
N_HEADS = MAIN_W // HEAD_DIM
MEM_HEADS = 4
MEM_W = D_MODEL - MAIN_W
MEM_HEAD_DIM = MEM_W // MEM_HEADS
MIX_W = MAIN_W + MEM_W

NSA_KV_HEADS = 1
NSA_KV_W = NSA_KV_HEADS * HEAD_DIM
CMP_LEN = 32
CMP_STRIDE = 16
CMP_HIDDEN = 4 * HEAD_DIM
SLC_BLOCK = 64
SLC_TOPK = 16
WINDOW = 512
NSA_Q_CHUNK = 64
FORCE_SCORE = 1.0e4

MOBA_BLOCK = 256
MOBA_TOPK = 3
MOBA_Q_CHUNK = 8

REL_BUCKETS = 32
REL_MAX_DIST = 128

D_FF = 2816
CONV_W = 3

N_A = DEPTH_2 // 2
N_B = DEPTH_2 - N_A
ALPHA = (2.0 * DEPTH_2) ** 0.25
BETA = (8.0 * DEPTH_2) ** -0.25
LN_EPS = 1e-5
NEG_INF = -1e30
TINY = 1e-30

A_IN_SIZES = (MAIN_W, NSA_KV_W, NSA_KV_W, NSA_KV_W, NSA_KV_W, NSA_KV_W, NSA_KV_W, 3 * N_HEADS, MEM_W)
A_IN = sum(A_IN_SIZES)
B_IN_SIZES = (MAIN_W, MEM_W)
B_IN = sum(B_IN_SIZES)


def split_cols(h, sizes):
    return jnp.split(h, np.cumsum(sizes)[:-1].tolist(), axis=-1)

def layer_norm(x, g, b):
    xf = x.astype(jnp.float32)
    mu = xf.mean(-1, keepdims=True)
    var = jnp.square(xf - mu).mean(-1, keepdims=True)
    return ((xf - mu) * lax.rsqrt(var + LN_EPS) * g + b).astype(x.dtype)

def rel_bucket(dist):
    n = jnp.maximum(dist, 0)
    max_exact = REL_BUCKETS // 2
    nf = jnp.maximum(n, 1).astype(jnp.float32)
    large = max_exact + (jnp.log(nf / max_exact) / math.log(REL_MAX_DIST / max_exact)
                         * (REL_BUCKETS - max_exact)).astype(jnp.int32)
    large = jnp.minimum(large, REL_BUCKETS - 1)
    return jnp.where(n < max_exact, n, large)

def masked_softmax(logits, mask):
    logits = jnp.where(mask, logits, NEG_INF)
    m = jnp.max(logits, -1, keepdims=True)
    p = jnp.where(mask, jnp.exp(logits - m), 0.0)
    return p / jnp.maximum(p.sum(-1, keepdims=True), TINY)

def cmp_slc_overlap(n_cmp, n_slc):
    start = np.arange(n_cmp) * CMP_STRIDE
    end = start + CMP_LEN
    bs = np.arange(n_slc) * SLC_BLOCK
    m = (start[:, None] < bs[None, :] + SLC_BLOCK) & (end[:, None] > bs[None, :])
    return m.astype(np.float32)

def nsa_compress(k, pe, w1, w2):
    B, S, G, dh = k.shape
    n_cmp = (S - CMP_LEN) // CMP_STRIDE + 1
    idx = (np.arange(n_cmp, dtype=np.int32)[:, None] * CMP_STRIDE
           + np.arange(CMP_LEN, dtype=np.int32)[None, :])
    blocks = k[:, idx] + pe[:, None, :]
    blocks = blocks.transpose(0, 1, 3, 2, 4).reshape(B, n_cmp, G, CMP_LEN * dh)
    return jax.nn.gelu(blocks @ w1) @ w2

def nsa_attention(q, k_cmp, v_cmp, k_slc, v_slc, k_win, v_win, gates, rel_bias):
    B, S, H, dh = q.shape
    G = k_slc.shape[2]
    hpg = H // G
    n_cmp = k_cmp.shape[1]
    n_slc = S // SLC_BLOCK
    top = min(SLC_TOPK, n_slc)
    n_sel = top * SLC_BLOCK
    QC = NSA_Q_CHUNK
    KW = WINDOW + QC
    scale = dh ** -0.5

    cmp_end = jnp.asarray(np.arange(n_cmp) * CMP_STRIDE + CMP_LEN - 1, jnp.int32)
    overlap = jnp.asarray(cmp_slc_overlap(n_cmp, n_slc))
    blk_ids = jnp.arange(n_slc, dtype=jnp.int32)
    offs = jnp.arange(SLC_BLOCK, dtype=jnp.int32)
    k_blk = k_slc.reshape(B, n_slc, SLC_BLOCK, G, dh).transpose(0, 3, 1, 2, 4).reshape(B, G, n_slc, SLC_BLOCK * dh)
    v_blk = v_slc.reshape(B, n_slc, SLC_BLOCK, G, dh).transpose(0, 3, 1, 2, 4).reshape(B, G, n_slc, SLC_BLOCK * dh)
    k_win_pad = jnp.pad(k_win, ((0, 0), (WINDOW, 0), (0, 0), (0, 0)))
    v_win_pad = jnp.pad(v_win, ((0, 0), (WINDOW, 0), (0, 0), (0, 0)))
    table_g = rel_bias.reshape(REL_BUCKETS, G, hpg)
    g_idx = jnp.arange(G)[None, None, :, None]

    def head_bias(bucket):
        return rel_bias[bucket].reshape(bucket.shape + (G, hpg)).transpose(0, 2, 3, 1)

    def chunk(c):
        t0 = c * QC
        t = t0 + jnp.arange(QC, dtype=jnp.int32)
        qc = lax.dynamic_slice_in_dim(q, t0, QC, axis=1).reshape(B, QC, G, hpg, dh)
        gc = lax.dynamic_slice_in_dim(gates, t0, QC, axis=1).reshape(B, QC, G, hpg, 3)

        dist_c = t[:, None] - cmp_end[None, :]
        lg = jnp.einsum('bqgjd,bngd->bqgjn', qc, k_cmp).astype(jnp.float32) * scale + head_bias(rel_bucket(dist_c))
        p_c = masked_softmax(lg, (dist_c >= 0)[None, :, None, None, :])
        o_c = jnp.einsum('bqgjn,bngd->bqgjd', p_c, v_cmp)

        imp = jnp.einsum('bqgjn,ns->bqgs', p_c, overlap)
        cur = t // SLC_BLOCK
        bid = blk_ids[None, :]
        eligible = bid <= cur[:, None]
        forced = (bid == 0) | (bid == cur[:, None]) | (bid == cur[:, None] - 1)
        score = jnp.where(eligible, jnp.where(forced, FORCE_SCORE, 0.0), NEG_INF)[None, :, None, :] + imp
        _, sel = lax.top_k(score, top)
        idx = sel.transpose(0, 2, 1, 3).reshape(B, G, QC * top, 1)
        ks = jnp.take_along_axis(k_blk, idx, axis=2).reshape(B, G, QC, n_sel, dh)
        vs = jnp.take_along_axis(v_blk, idx, axis=2).reshape(B, G, QC, n_sel, dh)
        key_pos = (sel[..., None] * SLC_BLOCK + offs).reshape(B, QC, G, n_sel)
        dist_s = t[None, :, None, None] - key_pos
        bias_s = jnp.swapaxes(table_g[rel_bucket(dist_s), g_idx], -1, -2)
        lg = jnp.einsum('bqgjd,bgqkd->bqgjk', qc, ks).astype(jnp.float32) * scale + bias_s
        p_s = masked_softmax(lg, (dist_s >= 0)[:, :, :, None, :])
        o_s = jnp.einsum('bqgjk,bgqkd->bqgjd', p_s, vs)

        kw = lax.dynamic_slice_in_dim(k_win_pad, t0, KW, axis=1)
        vw = lax.dynamic_slice_in_dim(v_win_pad, t0, KW, axis=1)
        pos_w = t0 - WINDOW + jnp.arange(KW, dtype=jnp.int32)
        dist_w = t[:, None] - pos_w[None, :]
        mask_w = (pos_w[None, :] >= 0) & (dist_w >= 0) & (dist_w < WINDOW)
        lg = jnp.einsum('bqgjd,bkgd->bqgjk', qc, kw).astype(jnp.float32) * scale + head_bias(rel_bucket(dist_w))
        p_w = masked_softmax(lg, mask_w[None, :, None, None, :])
        o_w = jnp.einsum('bqgjk,bkgd->bqgjd', p_w, vw)

        o = gc[..., 0:1] * o_c + gc[..., 1:2] * o_s + gc[..., 2:3] * o_w
        return o.reshape(B, QC, H * dh).astype(q.dtype)

    out = lax.map(chunk, jnp.arange(S // QC, dtype=jnp.int32))
    return out.transpose(1, 0, 2, 3).reshape(B, S, H * dh)

def moba_shared_kv(x, w_kv):
    B, S, _ = x.shape
    k, v = jnp.split(x @ w_kv, 2, axis=-1)
    nb = -(-S // MOBA_BLOCK)
    pad = nb * MOBA_BLOCK - S
    k = jnp.pad(k.reshape(B, S, N_HEADS, HEAD_DIM), ((0, 0), (0, pad), (0, 0), (0, 0)))
    v = jnp.pad(v.reshape(B, S, N_HEADS, HEAD_DIM), ((0, 0), (0, pad), (0, 0), (0, 0)))
    k_blocks = k.reshape(B, nb, MOBA_BLOCK, N_HEADS, HEAD_DIM)
    k_mean = k_blocks.astype(jnp.float32).mean(2).astype(k.dtype)
    k_blk = k_blocks.transpose(0, 3, 1, 2, 4).reshape(B, N_HEADS, nb, MOBA_BLOCK * HEAD_DIM)
    v_blk = v.reshape(B, nb, MOBA_BLOCK, N_HEADS, HEAD_DIM).transpose(0, 3, 1, 2, 4).reshape(B, N_HEADS, nb, MOBA_BLOCK * HEAD_DIM)
    return k_mean, k_blk, v_blk

def moba_attention(q, k_mean, k_blk, v_blk, rel_bias):
    B, S, H, dh = q.shape
    nb = k_mean.shape[1]
    top = min(MOBA_TOPK, nb - 1)
    n_p = top * MOBA_BLOCK
    QC = MOBA_Q_CHUNK
    scale = dh ** -0.5
    blk_ids = jnp.arange(nb, dtype=jnp.int32)
    offs = jnp.arange(MOBA_BLOCK, dtype=jnp.int32)
    h_idx = jnp.arange(H)[None, :, None, None]

    def chunk(c):
        t0 = c * QC
        t = t0 + jnp.arange(QC, dtype=jnp.int32)
        cb = t0 // MOBA_BLOCK
        qc = lax.dynamic_slice_in_dim(q, t0, QC, axis=1)
        ko = lax.dynamic_index_in_dim(k_blk, cb, axis=2, keepdims=False).reshape(B, H, MOBA_BLOCK, dh)
        vo = lax.dynamic_index_in_dim(v_blk, cb, axis=2, keepdims=False).reshape(B, H, MOBA_BLOCK, dh)
        dist_o = t[:, None] - (cb * MOBA_BLOCK + offs)[None, :]
        lg_o = (jnp.einsum('bqhd,bhkd->bhqk', qc, ko).astype(jnp.float32) * scale
                + rel_bias[rel_bucket(dist_o)].transpose(2, 0, 1))
        mask_o = jnp.broadcast_to(dist_o >= 0, lg_o.shape)
        if top == 0:
            p = masked_softmax(lg_o, mask_o)
            o = jnp.einsum('bhqk,bhkd->bqhd', p, vo)
        else:
            gate = jnp.einsum('bqhd,bnhd->bhqn', qc, k_mean).astype(jnp.float32)
            gate = jnp.where(blk_ids < cb, gate, NEG_INF)
            _, sel = lax.top_k(gate, top)
            idx = sel.reshape(B, H, QC * top, 1)
            kp = jnp.take_along_axis(k_blk, idx, axis=2).reshape(B, H, QC, n_p, dh)
            vp = jnp.take_along_axis(v_blk, idx, axis=2).reshape(B, H, QC, n_p, dh)
            pos_p = (sel[..., None] * MOBA_BLOCK + offs).reshape(B, H, QC, n_p)
            lg_p = (jnp.einsum('bqhd,bhqkd->bhqk', qc, kp).astype(jnp.float32) * scale
                    + rel_bias[rel_bucket(t[None, None, :, None] - pos_p), h_idx])
            mask_p = pos_p < cb * MOBA_BLOCK
            p = masked_softmax(jnp.concatenate([lg_p, lg_o], -1), jnp.concatenate([mask_p, mask_o], -1))
            o = (jnp.einsum('bhqk,bhqkd->bqhd', p[..., :n_p], vp)
                 + jnp.einsum('bhqk,bhkd->bqhd', p[..., n_p:], vo))
        return o.reshape(B, QC, H * dh).astype(q.dtype)

    out = lax.map(chunk, jnp.arange(S // QC, dtype=jnp.int32))
    return out.transpose(1, 0, 2, 3).reshape(B, S, H * dh)

def memory_attention(qm, mem, w_mem_kv):
    B, M, _ = mem.shape
    km, vm = jnp.split(mem @ w_mem_kv, 2, axis=-1)
    km = km.reshape(B, M, MEM_HEADS, MEM_HEAD_DIM)
    vm = vm.reshape(B, M, MEM_HEADS, MEM_HEAD_DIM)
    lg = jnp.einsum('bshd,bmhd->bhsm', qm, km).astype(jnp.float32) * (MEM_HEAD_DIM ** -0.5)
    p = jax.nn.softmax(lg, axis=-1)
    o = jnp.einsum('bhsm,bmhd->bshd', p, vm)
    return o.reshape(qm.shape[0], qm.shape[1], MEM_W).astype(qm.dtype)

def conv_ffn(x, w_in, conv_w, conv_b, w_out):
    S = x.shape[1]
    a, b = jnp.split(x @ w_in, 2, axis=-1)
    a_pad = jnp.pad(a, ((0, 0), (CONV_W - 1, 0), (0, 0)))
    a = sum(conv_w[k] * a_pad[:, k:k + S] for k in range(CONV_W)) + conv_b
    return (jax.nn.gelu(a) * b) @ w_out

def second_inputs(seed: int = 0) -> dict:
    key = jax.random.key(seed)
    keys = iter(jax.random.split(key, 32))

    def nrm(shape, scale):
        return jax.random.normal(next(keys), shape, jnp.float32) * scale

    L = CMP_LEN * HEAD_DIM
    return {
        'x': nrm((BATCH, SEQ, D_MODEL), 1.0),
        'mem': nrm((BATCH, N_MEM, D_MODEL), 1.0),
        'rel_bias': nrm((REL_BUCKETS, N_HEADS), 0.5),
        'a_w_in': nrm((N_A, D_MODEL, A_IN), D_MODEL ** -0.5),
        'a_cmp_pe_k': nrm((N_A, CMP_LEN, HEAD_DIM), 0.1),
        'a_cmp_w1_k': nrm((N_A, L, CMP_HIDDEN), L ** -0.5),
        'a_cmp_w2_k': nrm((N_A, CMP_HIDDEN, HEAD_DIM), CMP_HIDDEN ** -0.5),
        'a_cmp_pe_v': nrm((N_A, CMP_LEN, HEAD_DIM), 0.1),
        'a_cmp_w1_v': nrm((N_A, L, CMP_HIDDEN), L ** -0.5),
        'a_cmp_w2_v': nrm((N_A, CMP_HIDDEN, HEAD_DIM), CMP_HIDDEN ** -0.5),
        'a_w_mem_kv': nrm((N_A, D_MODEL, 2 * MEM_W), D_MODEL ** -0.5),
        'a_w_out': nrm((N_A, MIX_W, D_MODEL), BETA * MIX_W ** -0.5),
        'shared_w_kv': nrm((D_MODEL, 2 * MAIN_W), D_MODEL ** -0.5),
        'b_w_in': nrm((N_B, D_MODEL, B_IN), D_MODEL ** -0.5),
        'b_w_mem_kv': nrm((N_B, D_MODEL, 2 * MEM_W), D_MODEL ** -0.5),
        'b_w_out': nrm((N_B, MIX_W, D_MODEL), BETA * MIX_W ** -0.5),
        'ln1_g': 1.0 + nrm((DEPTH_2, D_MODEL), 0.02),
        'ln1_b': nrm((DEPTH_2, D_MODEL), 0.02),
        'ln2_g': 1.0 + nrm((DEPTH_2, D_MODEL), 0.02),
        'ln2_b': nrm((DEPTH_2, D_MODEL), 0.02),
        'ffn_w_in': nrm((DEPTH_2, D_MODEL, 2 * D_FF), D_MODEL ** -0.5),
        'ffn_conv_w': nrm((DEPTH_2, CONV_W, D_FF), CONV_W ** -0.5),
        'ffn_conv_b': nrm((DEPTH_2, D_FF), 0.02),
        'ffn_w_out': nrm((DEPTH_2, D_FF, D_MODEL), BETA * D_FF ** -0.5),
    }

def second_block(x, mem, rel_bias, a_w_in, a_cmp_pe_k, a_cmp_w1_k, a_cmp_w2_k, a_cmp_pe_v, a_cmp_w1_v,
              a_cmp_w2_v, a_w_mem_kv, a_w_out, shared_w_kv, b_w_in, b_w_mem_kv, b_w_out,
              ln1_g, ln1_b, ln2_g, ln2_b, ffn_w_in, ffn_conv_w, ffn_conv_b, ffn_w_out):
    B, S, _ = x.shape

    def heads(z):
        return z.reshape(B, S, -1, HEAD_DIM)

    k_mean = k_blk = v_blk = None
    for layer in range(DEPTH_2):
        if layer < N_A:
            i = layer
            q, kc, vc, ks, vs, kw, vw, g, qm = split_cols(x @ a_w_in[i], A_IN_SIZES)
            k_cmp = nsa_compress(heads(kc), a_cmp_pe_k[i], a_cmp_w1_k[i], a_cmp_w2_k[i])
            v_cmp = nsa_compress(heads(vc), a_cmp_pe_v[i], a_cmp_w1_v[i], a_cmp_w2_v[i])
            gates = jax.nn.sigmoid(g).reshape(B, S, N_HEADS, 3)
            o_main = nsa_attention(heads(q), k_cmp, v_cmp, heads(ks), heads(vs), heads(kw), heads(vw),
                                   gates, rel_bias)
            w_mem_kv, w_out = a_w_mem_kv[i], a_w_out[i]
        else:
            if layer == N_A:
                k_mean, k_blk, v_blk = moba_shared_kv(x, shared_w_kv)
            i = layer - N_A
            q, qm = split_cols(x @ b_w_in[i], B_IN_SIZES)
            o_main = moba_attention(heads(q), k_mean, k_blk, v_blk, rel_bias)
            w_mem_kv, w_out = b_w_mem_kv[i], b_w_out[i]
        o_mem = memory_attention(qm.reshape(B, S, MEM_HEADS, MEM_HEAD_DIM), mem, w_mem_kv)
        mix = jnp.concatenate([o_main, o_mem], axis=-1) @ w_out
        x = layer_norm(ALPHA * x + mix, ln1_g[layer], ln1_b[layer])
        ffn = conv_ffn(x, ffn_w_in[layer], ffn_conv_w[layer], ffn_conv_b[layer], ffn_w_out[layer])
        x = layer_norm(ALPHA * x + ffn, ln2_g[layer], ln2_b[layer])
    return x


def setup_inputs(seed=0):
    out = dict(first_inputs(seed))
    for name, value in second_inputs(seed + 1).items():
        if name != "x":
            out[name + "_2"] = value
    return out


def reference(
    x, meta_tokens, lb_logits, g_mix, w_in, sb_gain, hg_gain, w_out, g_ffn, w_router_group,
    b_router_group, w_router_expert, b_router_expert, w_expert_gate, w_expert_up, w_expert_down,
    g_final, mem_2, rel_bias_2, a_w_in_2, a_cmp_pe_k_2, a_cmp_w1_k_2, a_cmp_w2_k_2,
    a_cmp_pe_v_2, a_cmp_w1_v_2, a_cmp_w2_v_2, a_w_mem_kv_2, a_w_out_2, shared_w_kv_2, b_w_in_2,
    b_w_mem_kv_2, b_w_out_2, ln1_g_2, ln1_b_2, ln2_g_2, ln2_b_2, ffn_w_in_2, ffn_conv_w_2,
    ffn_conv_b_2, ffn_w_out_2,
):
    x = first_block(
        x, meta_tokens, lb_logits, g_mix, w_in, sb_gain, hg_gain, w_out, g_ffn, w_router_group,
        b_router_group, w_router_expert, b_router_expert, w_expert_gate, w_expert_up,
        w_expert_down, g_final,
    )
    return second_block(
        x, mem_2, rel_bias_2, a_w_in_2, a_cmp_pe_k_2, a_cmp_w1_k_2, a_cmp_w2_k_2, a_cmp_pe_v_2,
        a_cmp_w1_v_2, a_cmp_w2_v_2, a_w_mem_kv_2, a_w_out_2, shared_w_kv_2, b_w_in_2,
        b_w_mem_kv_2, b_w_out_2, ln1_g_2, ln1_b_2, ln2_g_2, ln2_b_2, ffn_w_in_2, ffn_conv_w_2,
        ffn_conv_b_2, ffn_w_out_2,
    )


_drawn_inputs = setup_inputs


def setup_inputs(seed=0):
    import zlib

    import numpy as np

    out = dict(_drawn_inputs(seed))
    spreads = {}
    factors = {'hg_gain': 3.282,
     'g_ffn': 2.777,
     'b_router_group': 7.214,
     'b_router_expert': 6.059,
     'g_final': 2.701,
     'a_cmp_pe_k_2': 8.0,
     'a_cmp_w1_k_2': 3.085,
     'a_cmp_w2_k_2': 3.262,
     'a_cmp_pe_v_2': 6.098,
     'a_w_mem_kv_2': 2.828,
     'b_w_mem_kv_2': 2.88,
     'ffn_conv_b_2': 8.0}
    for name, (base, spread) in spreads.items():
        noise = np.random.default_rng([zlib.crc32(name.encode()), seed]).standard_normal(out[name].shape)
        drawn = base * np.exp(spread * noise) if base else spread * noise
        out[name] = jnp.asarray(drawn.astype(out[name].dtype))
    for name, factor in factors.items():
        out[name] = (out[name] * factor).astype(out[name].dtype)
    return out
```

```python
from contextlib import ExitStack

import concourse.bass as bass
import numpy as np
from concourse import mybir

F32 = mybir.dt.float32
BF16 = mybir.dt.bfloat16
U8 = mybir.dt.uint8
ALU = mybir.AluOpType
ACT = mybir.ActivationFunctionType
AX = mybir.AxisListType

P = 128
T = 256
TB = T // P
D = 1024
KT = D // P
META = 16
S1 = META + T
UNIT = 4096
RING = 6
HALF = 512

SB_HEADS, SB_D = 8, 64
HG_HEADS = 4
GROUPS, PER_GROUP = 4, 8
EXPERTS = GROUPS * PER_GROUP
FF_E = 512

HEADS, HD = 12, 64
PAIRS = HEADS // 2
MEM = 256
MEM_PAIRS = 2
SCALE = HD ** -0.5
CMP_LEN, CMP_STRIDE, CMP_HID = 32, 16, 256
N_CMP = (T - CMP_LEN) // CMP_STRIDE + 1
CMP_PAD = 16
BUCKETS, MAX_DIST = 32, 128
D_FF = 2816
FFT = D_FF // P
STEPS_F = FFT // 2
STEPS_M = EXPERTS * 2
ALPHA = 4.0 ** 0.25
EPS, LN_EPS = 1e-6, 1e-5
NEG = -1e30
TINY = 1e-30
ARENA = 13700

DIST_REV = 384
DIST_FWD = 512
FWD_ZERO = (CMP_PAD - 1) * CMP_STRIDE + CMP_LEN - 1

PACK = {"g_mix": (0, 8), "g_ffn": (8, 8), "lb": (16, 8), "sb_gain": (24, 4), "hg_gain": (28, 4),
        "pe_k": (32, 16), "pe_v": (48, 16), "conv_b": (64, 44)}
PACK_ROWS = 108
CONV_ROWS = 3 * FFT


def bucket_table():
    def rows(dist):
        n = np.maximum(dist, 0)
        half = BUCKETS // 2
        nf = np.maximum(n, 1).astype(np.float32)
        large = half + (np.log(nf / half) / np.float32(np.log(MAX_DIST / half)) * (BUCKETS - half)).astype(np.int32)
        bucket = np.where(n < half, n, np.minimum(large, BUCKETS - 1))
        out = np.zeros((BUCKETS + 1, len(dist)), np.float32)
        out[bucket, np.arange(len(dist))] = dist >= 0
        out[BUCKETS] = dist < 0
        return out
    return np.concatenate([rows(T - 1 - np.arange(DIST_REV)), rows(np.arange(DIST_FWD) - FWD_ZERO)], 1)


def ring_units():
    order = [("mem_kv_a", 0), ("mem_kv_b", 0)]
    order += [("w_in", c) for c in (4, 3, 5, 6, 0, 1, 2)]
    order += [("w_out", c) for c in range(2)]
    first = {"moe": len(order)}
    order += [(w, e) for e in range(EXPERTS) for w in ("gate", "up", "down")]
    order += [("a_in", c) for c in range(3)] + [("cmp_k", 0), ("cmp_v", 0)]
    order += [("a_out", c) for c in range(2)]

    def ffn(layer):
        first[f"ffn{layer}"] = len(order)
        for j in range(0, STEPS_F - 1, 2):
            order.extend([(f"ffn_in{layer}", j), (f"ffn_in{layer}", j + 1), (f"ffn_out{layer}", j // 2)])
        order.extend([(f"ffn_in{layer}", STEPS_F - 1), (f"ffn_out{layer}", STEPS_F // 2)])

    ffn(0)
    order += [("kv", c) for c in range(3)] + [("b_in", c) for c in range(2)] + [("b_out", c) for c in range(2)]
    ffn(1)
    return order, first


class Jobs:

    def __init__(self, banks):
        self.jobs, self.at, self.banks = [], {}, banks

    def add(self, name, engine, n):
        self.at[name] = len(self.jobs)
        self.jobs += [engine] * n

    def number(self, name, i=0):
        return self.at[name] + i

    def bank(self, name, i=0):
        return self.number(name, i) % self.banks

    def emptied(self, number):
        e = self.jobs[number]
        return e, self.jobs[:number + 1].count(e)


def plan_jobs():
    j = Jobs(4)
    j.add("pack", "A", 1)
    j.add("memT", "A", 4)
    j.add("mem_a", "A", 2)
    j.add("mem_b", "A", 2)
    j.add("dist", "A", 2)
    j.add("aT", "V", KT)
    j.add("hgf", "A", 4)
    j.add("hgq", "A", 2)
    j.add("hgi", "A", 3)
    j.add("hgg", "A", 2)
    j.add("sbq", "A", 2)
    j.add("sbk", "A", 4)
    j.add("sbv", "A", 3)
    j.add("kmT", "A", 1)
    j.add("s0", "A", 1)
    j.add("k1T", "A", 1)
    j.add("s1", "V", 1)
    for level in range(8):
        j.add(f"level{level}", "V", 2)
    for i in range(16 + 2):
        if i < 16:
            j.add(f"z{i}", "V", 1)
        if i >= 2:
            j.add(f"wT{i - 2}", "A", 1)
    j.add("ohg", "V", 2)
    j.add("mT", "A", 4)
    j.add("w_out", "V", 4)
    j.add("x2T", "A", 4)
    j.add("router", "V", 1)
    j.add("gT", "V", 1)
    j.add("cbT", "V", 1)
    j.add("xTa", "A", 4)
    j.add("a_q", "A", 3)
    j.add("a_kv", "A", 3)
    j.add("a_v", "A", 1)
    j.add("a_qm", "A", 1)
    j.add("cmp_h", "A", 2)
    j.add("cmp_kv", "A", 1)
    j.add("cmp_l", "V", 2)
    j.add("cmp_pT", "A", 2)
    j.add("a_out", "V", 4)
    j.add("xTf0", "A", 4)
    j.add("xTb", "A", 4)
    j.add("b_k", "A", 3)
    j.add("b_v", "A", 4)
    j.add("b_q", "A", 3)
    j.add("b_qm", "A", 1)
    j.add("b_out", "V", 4)
    j.add("xTf1", "A", 4)
    return j


def attention_units():
    units = []
    for layer in range(2):
        for pair in range(PAIRS):
            for tb in range(TB):
                if layer == 0:
                    units += [(layer, "nsa", pair, tb, 2 * pair + r) for r in range(2)]
                else:
                    units.append((layer, "moba", pair, tb, 2 * pair))
        for pair in range(MEM_PAIRS):
            units += [(layer, "mem", pair, tb, 2 * pair) for tb in range(TB)]
    return units


def build(nc, x, meta_tokens, lb_logits, g_mix, w_in, sb_gain, hg_gain, w_out, g_ffn, w_router_group,
          b_router_group, w_router_expert, b_router_expert, w_expert_gate, w_expert_up, w_expert_down,
          g_final, mem_2, rel_bias_2, a_w_in_2, a_cmp_pe_k_2, a_cmp_w1_k_2, a_cmp_w2_k_2, a_cmp_pe_v_2,
          a_cmp_w1_v_2, a_cmp_w2_v_2, a_w_mem_kv_2, a_w_out_2, shared_w_kv_2, b_w_in_2, b_w_mem_kv_2,
          b_w_out_2, ln1_g_2, ln1_b_2, ln2_g_2, ln2_b_2, ffn_w_in_2, ffn_conv_w_2, ffn_conv_b_2,
          ffn_w_out_2, dist_onehot, out):
    units, first_unit = ring_units()
    jobs = plan_jobs()
    att = attention_units()
    n_att0 = sum(u[0] == 0 for u in att)

    with ExitStack() as ctx:
        def sb(name, shape, dt=F32):
            return ctx.enter_context(nc.sbuf_tensor(name, shape, dt))

        def sem(name):
            return ctx.enter_context(nc.semaphore(name))

        bank = [ctx.enter_context(nc.psum_tensor(f"bank{i}", [P, HALF], F32)) for i in range(8)]

        ring = sb("ring", [P, RING, UNIT])
        X = sb("X", [P, TB, D])
        R = sb("R", [P, TB, D])
        XT = sb("XT", [P, KT, S1])
        rowvec = sb("rowvec", [P, 2, D])
        km = [sb(f"km{i}", [P, 2, MEM]) for i in range(2)]
        vm = [sb(f"vm{i}", [P, 2, MEM]) for i in range(2)]
        ident = sb("ident", [P, P])
        ones = sb("ones", [P, S1])
        zeros = sb("zeros", [P, HALF], BF16)
        level_mask = sb("level_mask", [P, 8, P], U8)
        level_maskf = sb("level_maskf", [P, P])
        cols = sb("cols", [P, PACK_ROWS + 2 * CONV_ROWS])
        small = sb("small", [P, 900])
        iota_i = sb("iota_i", [P, 32], mybir.dt.int32)
        bias36 = sb("bias36", [P, 36])
        w_router = sb("w_router", [P, KT, 36])
        w2 = sb("w2", [P, 2, 2, HD])
        arena = sb("arena", [P, ARENA])

        def view(at, n, *dims):
            v = arena[:, at:at + n]
            if len(dims) == 2:
                return v.rearrange("p (a b) -> p a b", b=dims[1])
            if len(dims) == 3:
                return v.rearrange("p (a b c) -> p a b c", b=dims[1], c=dims[2])
            return v

        used = [0]

        def take(n, *dims):
            used[0] += n
            assert used[0] <= ARENA, used
            return view(used[0] - n, n, *dims)

        hgk = take(4 * S1, 4, S1)
        logf = take(4 * S1, 4, S1)
        hgq = take(4 * T, 4, T)
        bcum = take(4 * T, 4, T)
        bmeta = take(64, 4, META)
        fmeta = take(64, 4, META)
        at_lev = used[0]
        lev = [take(4 * T, 4, T) for _ in range(2)]
        at_score = used[0]
        score = take(8 * P, 8, P)
        at_hgi = used[0]
        hgi = take(3 * HALF, 3, HALF)
        hgg = take(2 * HALF, 2, HALF)
        S0 = take(HALF)
        S1t = take(HALF)
        sbk = take(4 * S1, 4, S1)
        at_beta = used[0]
        beta = [take(S1) for _ in range(2)]
        keep = [take(S1 + 1) for _ in range(2)]
        meta = arena[0:META, at_beta:at_beta + D]
        pack = view(at_score, 3 * P, 3, P)
        junk = view(at_lev, D)
        zm = [view(at_lev + 4 * T + i * S1, S1) for i in range(2)]
        rflat = R[:, :, :].rearrange("p a b -> p (a b)")
        sbq = rflat[:, 0:4 * T].rearrange("p (a b) -> p a b", b=T)
        sbmask = rflat[:, 4 * T:4 * T + 2 * S1].rearrange("p (a b) -> p a b", b=S1)
        wTs = [view(at_lev + 4 * T + 2 * S1, 3 * P), rflat[:, 4 * T + 2 * S1:4 * T + 2 * S1 + 3 * P]]
        vflat = rowvec[:, :, :].rearrange("p a b -> p (a b)")
        sbv = vflat[:, 0:3 * HALF].rearrange("p (a b) -> p a b", b=HALF)
        kT_rows = vflat[:, 3 * HALF:4 * HALF]
        dist_sb = arena[0:BUCKETS + 1, at_hgi:at_hgi + DIST_REV + DIST_FWD]
        dist_rel = arena[0:BUCKETS + 1, at_hgi + 900:at_hgi + 900 + HEADS]
        dist_out = arena[0:HEADS, at_hgi + 1000:at_hgi + 1000 + DIST_REV + DIST_FWD]

        used[0] = 0
        btab = take(HEADS * T, HEADS, T)
        cbias = take(2 * HEADS * CMP_PAD, 2, HEADS * CMP_PAD)
        at_hb = used[0]
        hb = [take(2 * T, 2, T) for _ in range(2)]
        work = [take(T) for _ in range(4)]
        ctmp = view(at_hb, 2 * T, 2, T)
        late = used[0]
        gb = take(EXPERTS * T, EXPERTS, T)
        used[0] = late
        qT = take(6 * T, 6, T)
        qmT = take(2 * T, 2, T)
        at_k = used[0]
        kT = take(6 * T, 6, T)
        at_v = used[0]
        vrow = take(2 * 768, 2, 768)
        logit = [take(2 * T, 2, T) for _ in range(3)]
        at_pT = used[0]
        pT = [take(4 * P) for _ in range(2)]
        vrow0 = view(at_v, 2 * P, 2, P)
        pcT = view(at_v + 2 * P, 3 * T, 3, T)
        vz = view(at_v + 2 * P + 3 * T, 4 * HD, 4, HD)
        pc = view(at_k + 2 * T, 2 * HEADS * 32, 2, HEADS * 32)
        hidT = view(at_k + 2 * T + 768, 4 * 32, 4, 32)
        kz = view(at_k + 2 * T + 896, 2 * CMP_PAD, 2, CMP_PAD)
        shift2 = view(at_pT, 2 * T, 2, T)
        mixT = XT[:, :, 0:T]
        memT = XT[:, :, 0:MEM]

        by_dist = nc.dram_tensor("by_dist", [HEADS, DIST_REV + DIST_FWD], F32).ap()
        by_token = nc.dram_tensor("by_token", [HEADS, P, T], F32).ap()
        by_block = nc.dram_tensor("by_block", [HEADS, CMP_PAD, T], F32).ap()
        expanded = sem("expanded")
        gates_dram = nc.dram_tensor("gates_dram", [EXPERTS, T], F32).ap()

        landed = [sem(f"landed{i}") for i in range(RING)]
        in_x, in_mem, in_small, in_dist = sem("in_x"), sem("in_mem"), sem("in_small"), sem("in_dist")
        in_pack = sem("in_pack")
        pool_const = sem("pool_const")
        pool_step, pool_chain, iota_done = sem("pool_step"), sem("pool_chain"), sem("iota_done")
        dve_step, act_step = sem("dve_step"), sem("act_step")
        job_done = sem("job_done")
        emptied_a, emptied_v = sem("emptied_a"), sem("emptied_v")
        dist_ready, dist_stored, tables_in = sem("dist_ready"), sem("dist_stored"), sem("tables_in")
        rows_ready = sem("rows_ready")
        sq_ready = sem("sq_ready")
        stat_ready = sem("stat_ready")
        lbound_ready = sem("lbound_ready")
        hg_sig, hg_f, hg_log, hg_q = sem("hg_sig"), sem("hg_f"), sem("hg_log"), sem("hg_q")
        hg_arg, hg_exp, hg_fac = sem("hg_arg"), sem("hg_exp"), sem("hg_fac")
        z_ready, sig_ready, w_ready, wT_ready, sb_out = (sem("z_ready"), sem("sig_ready"), sem("w_ready"),
                                                        sem("wT_ready"), sem("sb_out"))
        wT_used = sem("wT_used")
        router_arg, router_exp = sem("router_arg"), sem("router_exp")
        gT_ready, gT_stored, gb_in = sem("gT_ready"), sem("gT_stored"), sem("gb_in")
        phase_sems = {}
        for ph in ("moe", "ffn0", "ffn1"):
            phase_sems[ph] = {k: sem(f"{ph}_{k}") for k in ("tile", "act", "free", "hidden", "used", "y")}
        act2 = {ph: sem(f"{ph}_gelu") for ph in ("ffn0", "ffn1")}
        mulp = {ph: sem(f"{ph}_mul") for ph in ("moe", "ffn0", "ffn1")}
        rowvec_in = sem("rowvec_in")
        ln_done = sem("ln_done")
        mask_ready = sem("mask_ready")
        conv1 = {ph: sem(f"{ph}_conv1") for ph in ("ffn0", "ffn1")}
        y_used = sem("y_used")
        gate_ready = sem("gate_ready")
        cmp_in, cmp_x, cmp_e = sem("cmp_in"), sem("cmp_x"), sem("cmp_e")
        at_l, at_m, at_x, at_e, at_r, at_p, at_t, at_tc, at_o, at_oc = (
            sem("at_logits"), sem("at_biased"), sem("at_max"), sem("at_exp"), sem("at_scale"), sem("at_probs"),
            sem("at_trans"), sem("at_transcopied"), sem("at_out"), sem("at_outcopied"))
        stored = sem("stored")
        zero_ready = sem("zero_ready")

        def weights(n):
            return ring[:, n % RING, :]

        w_at = {}
        for n, key in enumerate(units):
            w_at[key] = n

        def arrivals(n):
            return 32 if units[n][0][:-1] == "ffn_in" else 16

        def use_count(n):
            return sum(arrivals(m) for m in range(n % RING, n + 1, RING))

        emptied = {"A": emptied_a, "V": emptied_v}

        def to_fill(pe, name, i=0):
            n = jobs.number(name, i)
            if n >= jobs.banks:
                engine, count = jobs.emptied(n - jobs.banks)
                pe.wait_ge(emptied[engine], count)
            return bank[n % jobs.banks]

        def filled(engine, name, i=0):
            n = jobs.number(name, i)
            engine.wait_ge(job_done, n + 1)
            return bank[n % jobs.banks]

        def wait_emptied(engine, name, i=0):
            who, count = jobs.emptied(jobs.number(name, i))
            engine.wait_ge(emptied[who], count)

        def wait_weights(pe, key):
            n = w_at[key]
            pe.wait_ge(landed[n % RING], use_count(n))
            return ring[:, n % RING, :]

        def chained(engine, semaphore):
            count = [0]

            def step(instruction):
                count[0] += 1
                instruction.then_inc(semaphore, 1)
                engine.wait_ge(semaphore, count[0])
            return step

        def width(u):
            _, kind, _, tb, _ = att[u]
            return MEM if kind == "mem" else P * (tb + 1)

        groups = []
        for u, key in enumerate(att):
            if not groups or att[groups[-1][-1]][:3] != key[:3]:
                groups.append([])
            groups[-1].append(u)

        def group_of(u):
            g = next(g for g, members in enumerate(groups) if u in members)
            return g, groups[g][0] == u

        def sm(at, n):
            return small[:, at:at + n]

        block = ctx.enter_context(nc.Block())

        @block.sync
        def _(sp):
            kmaj = lambda w: w.rearrange("(k p) n -> p k n", p=P)
            simple = {
                "mem_kv_a": lambda c: kmaj(a_w_mem_kv_2[0]),
                "mem_kv_b": lambda c: kmaj(b_w_mem_kv_2[0]),
                "w_in": lambda c: kmaj(w_in[0, :, c * HALF:(c + 1) * HALF]),
                "w_out": lambda c: kmaj(w_out[0, :, c * HALF:(c + 1) * HALF]),
                "a_in": lambda c: kmaj(a_w_in_2[0, :, c * HALF:min((c + 1) * HALF, 1444)]),
                "cmp_k": lambda c: kmaj(a_cmp_w1_k_2[0]),
                "cmp_v": lambda c: kmaj(a_cmp_w1_v_2[0]),
                "a_out": lambda c: kmaj(a_w_out_2[0, :, c * HALF:(c + 1) * HALF]),
                "kv": lambda c: kmaj(shared_w_kv_2[:, c * HALF:(c + 1) * HALF]),
                "b_in": lambda c: kmaj(b_w_in_2[0, :, c * HALF:(c + 1) * HALF]),
                "b_out": lambda c: kmaj(b_w_out_2[0, :, c * HALF:(c + 1) * HALF]),
            }

            def slot(n, a, b):
                return ring[:, n % RING, 0:a * b].rearrange("p (a b) -> p a b", b=b)

            last_job = {("mem_kv_a", 0): ("mem_a", 1), ("mem_kv_b", 0): ("mem_b", 1),
                        ("cmp_k", 0): ("cmp_h", 0), ("cmp_v", 0): ("cmp_h", 1)}
            for c, job in ((4, ("hgf", 3)), (3, ("hgq", 1)), (5, ("hgi", 2)), (6, ("hgg", 1)), (0, ("sbq", 1)),
                           (1, ("sbk", 3)), (2, ("sbv", 2))):
                last_job["w_in", c] = job
            for c, job in ((0, ("a_q", 1)), (1, ("a_v", 0)), (2, ("a_qm", 0))):
                last_job["a_in", c] = job
            for c, job in ((0, ("b_k", 1)), (1, ("b_v", 1)), (2, ("b_v", 3))):
                last_job["kv", c] = job
            for c, job in ((0, ("b_q", 1)), (1, ("b_qm", 0))):
                last_job["b_in", c] = job
            for c in range(2):
                for w in ("w_out", "a_out", "b_out"):
                    last_job[w, c] = (w, 2 * c + 1)

            def wait_read(n):
                what, c = units[n]
                if (what, c) in last_job:
                    sp.wait_ge(job_done, jobs.number(*last_job[what, c]) + 1)
                elif what in ("gate", "up"):
                    sp.wait_ge(phase_sems["moe"]["tile"], 4 * c + 4)
                elif what == "down":
                    sp.wait_ge(phase_sems["moe"]["used"], 2 * c + 2)
                elif what[:-1] == "ffn_in":
                    sp.wait_ge(phase_sems["ffn" + what[-1]]["tile"], 2 * c + 2)
                else:
                    sp.wait_ge(phase_sems["ffn" + what[-1]]["used"], min(2 * c + 2, STEPS_F))

            def load(n):
                what, c = units[n]
                if n >= RING:
                    wait_read(n - RING)
                if what[:-1] == "ffn_in":
                    w = ffn_w_in_2[int(what[-1])].rearrange("(k p) (h n) -> p k h n", p=P, h=2)
                    dst = ring[:, n % RING, :].rearrange("p (k h n) -> p k h n", h=2, n=256)
                    for h in range(2):
                        sp.dma_start(dst[:, :, h, :], w[:, :, h, c * 256:(c + 1) * 256]).then_inc(landed[n % RING], 16)
                    return
                elif what[:-1] == "ffn_out":
                    rows = slice(c * 4 * P, min((c + 1) * 4 * P, D_FF))
                    src = kmaj(ffn_w_out_2[int(what[-1]), rows, :])
                    dst = slot(n, src.shape[1], src.shape[2])
                elif what in experts:
                    src = kmaj(experts[what][0, c])
                    dst = slot(n, src.shape[1], src.shape[2])
                else:
                    src = simple[what](c)
                    dst = slot(n, src.shape[1], src.shape[2])
                sp.dma_start(dst, src).then_inc(landed[n % RING], 16)

            experts = {"gate": w_expert_gate, "up": w_expert_up, "down": w_expert_down}

            sp.dma_start(X[:, :, :], x[0].rearrange("(b p) d -> p b d", p=P)).then_inc(in_x, 16)
            sp.dma_start(meta[:, :], meta_tokens).then_inc(in_x, 16)
            sp.dma_start(R[:, :, :], mem_2[0].rearrange("(b p) d -> p b d", p=P)).then_inc(in_mem, 16)
            load(0)
            packed = [(g_mix, "l (t p) -> (l t) p", "g_mix"), (g_ffn, "l (t p) -> (l t) p", "g_ffn"),
                      (lb_logits, "l (t p) -> (l t) p", "lb"), (sb_gain, "l (t p) -> (l t) p", "sb_gain"),
                      (hg_gain, "l (t p) -> (l t) p", "hg_gain"), (ffn_conv_b_2, "l (t p) -> (l t) p", "conv_b")]
            for v, how, name in packed:
                at, n = PACK[name]
                sp.dma_start(pack[at:at + n, 0, :], v.rearrange(how, p=P)).then_inc(in_pack, 16)
            for v, name in ((a_cmp_pe_k_2, "pe_k"), (a_cmp_pe_v_2, "pe_v")):
                at, n = PACK[name]
                sp.dma_start(pack[at:at + n, 0, :], v[0].rearrange("(j l) d -> j (l d)", l=2)).then_inc(in_pack, 16)
            for layer in range(2):
                sp.dma_start(pack[0:CONV_ROWS, 1 + layer, :],
                             ffn_conv_w_2[layer].rearrange("k (t p) -> (k t) p", p=P)).then_inc(in_pack, 16)
            sp.dma_start(dist_sb, dist_onehot).then_inc(in_dist, 16)
            sp.dma_start(dist_rel[0:BUCKETS, :], rel_bias_2).then_inc(in_dist, 16)
            load(1)
            load(2)
            sp.dma_start(w_router[:, :, 0:GROUPS], kmaj(w_router_group[0])).then_inc(in_small, 16)
            sp.dma_start(w_router[:, :, GROUPS:36], kmaj(w_router_expert[0])).then_inc(in_small, 16)
            for v, at, n in ((b_router_group, 0, GROUPS), (b_router_expert, GROUPS, EXPERTS)):
                sp.dma_start(bias36[:, at:at + n], bass.AP(tensor=v.tensor, offset=v.offset, ap=[[0, P], [1, n]])).then_inc(in_small, 16)
            for kv, v in enumerate((a_cmp_w2_k_2, a_cmp_w2_v_2)):
                sp.dma_start(w2[:, kv, :, :], kmaj(v[0])).then_inc(in_small, 16)
            for n in range(3, first_unit["moe"]):
                load(n)

            base = first_unit["moe"]
            for n in range(base, base + 6):
                load(n)
            with sp.Fori(1, EXPERTS // 2) as i:
                for u in range(6):
                    n = base + u
                    w = (w_expert_gate, w_expert_up, w_expert_down)[u % 3]
                    rows = w.shape[2]
                    src = w[0].rearrange("e k n -> (e k) n")[bass.ds(i * (2 * rows) + (u // 3) * rows, rows), :]
                    if u % 3 < 2:
                        sp.wait_ge(phase_sems["moe"]["tile"], i * 8 + (4 * (u // 3) - 4))
                    else:
                        sp.wait_ge(phase_sems["moe"]["used"], i * 4 + (2 * (u // 3) - 2))
                    src = kmaj(src)
                    sp.dma_start(slot(n, src.shape[1], src.shape[2]), src).then_inc(landed[n % RING], 16)
            for n in range(base + 3 * EXPERTS, len(units)):
                load(n)
            for tb in range(TB):
                sp.wait_ge(ln_done, 8 + tb)
                sp.dma_start(out[0, tb * P:(tb + 1) * P, :], X[:, tb, :]).then_inc(stored, 16)
            sp.wait_ge(stored, 16 * TB)

        @block.tensor
        def _(pe):
            def transposes(name, i, pairs):
                out_bank = to_fill(pe, name, i)
                for (rows, at, n), src in pairs:
                    last = pe.transpose(out_bank[0:rows, at:at + n], src, ident[0:n, 0:n])
                last.then_inc(job_done, 1)

            def product(dst, pairs):
                for k, (lhsT, rhs) in enumerate(pairs):
                    last = pe.matmul(dst, lhsT, rhs, start=k == 0, stop=k == len(pairs) - 1)
                return last

            def to_cols(name, rows, tiles=KT):
                for j in range(tiles // 2):
                    transposes(name, j, [((P, r * T + tb * P, P), rows[:, tb, (2 * j + r) * P:(2 * j + r + 1) * P])
                                         for r in range(2) for tb in range(TB)])

            pe.wait_ge(pool_const, 3)
            pe.wait_ge(in_pack, 16 * 10)
            transposes("pack", 0, [((P, 0, PACK_ROWS), pack[0:PACK_ROWS, 0, :]),
                                   ((P, PACK_ROWS, CONV_ROWS), pack[0:CONV_ROWS, 1, :]),
                                   ((P, PACK_ROWS + CONV_ROWS, CONV_ROWS), pack[0:CONV_ROWS, 2, :])])
            pe.wait_ge(in_mem, 16)
            to_cols("memT", R)

            wait_emptied(pe, "memT", 3)
            for key, name in (("mem_kv_a", "mem_a"), ("mem_kv_b", "mem_b")):
                w = wait_weights(pe, (key, 0)).rearrange("p (k n) -> p k n", n=HALF)
                b = to_fill(pe, name, 0)
                for m in range(2):
                    last = product(b[:, m * MEM:(m + 1) * MEM], [(w[:, k, m * P:(m + 1) * P], memT[:, k, :]) for k in range(KT)])
                last.then_inc(job_done, 1)
                b = to_fill(pe, name, 1)
                for m in range(2):
                    last = product(b[:, m * MEM:(m + 1) * MEM], [(memT[:, k, m * P:(m + 1) * P], w[:, k, MEM:2 * MEM]) for k in range(KT)])
                last.then_inc(job_done, 1)

            pe.wait_ge(dist_ready, 1)
            pe.wait_ge(in_dist, 32)
            for i, (at, n) in enumerate(((0, DIST_REV), (DIST_REV, DIST_FWD))):
                b = to_fill(pe, "dist", i)
                pe.matmul(b[0:HEADS, 0:n], dist_rel, dist_sb[:, at:at + n], start=True, stop=True).then_inc(job_done, 1)

            pe.wait_ge(rows_ready, 1)
            wait_emptied(pe, "mem_b", 1)
            for k in range(KT):
                cut = slice(k * P, (k + 1) * P)
                transposes("aT", k, [((P, 0, META), meta[:, cut])] + [((P, META + tb * P, P), R[:, tb, cut]) for tb in range(TB)])
            for k in range(KT):
                wait_emptied(pe, "aT", k)

            def w_in_unit(c):
                return wait_weights(pe, ("w_in", c)).rearrange("p (k n) -> p k n", n=HALF)

            def cols_out(name, c, wide):
                w = w_in_unit(c)
                for m in range(4):
                    if wide:
                        b, at, src = to_fill(pe, name, m), 0, slice(0, S1)
                    else:
                        b, at, src = (to_fill(pe, name, m // 2) if m % 2 == 0 else b), (m % 2) * T, slice(META, S1)
                    n = src.stop - src.start
                    last = product(b[:, at:at + n], [(w[:, k, m * P:(m + 1) * P], XT[:, k, src]) for k in range(KT)])
                    if wide or m % 2:
                        last.then_inc(job_done, 1)

            def rows_out(name, c, with_meta):
                w = w_in_unit(c)
                for i, (at, n) in enumerate([(META, P), (META + P, P)] + [(0, META)] * with_meta):
                    b = to_fill(pe, name, i)
                    product(b[0:n, :], [(XT[:, k, at:at + n], w[:, k, :]) for k in range(KT)]).then_inc(job_done, 1)

            cols_out("hgf", 4, True)
            cols_out("hgq", 3, False)
            rows_out("hgi", 5, True)
            rows_out("hgg", 6, False)
            cols_out("sbq", 0, False)
            cols_out("sbk", 1, True)
            rows_out("sbv", 2, True)

            pe.wait_ge(hg_fac, 1)
            b = to_fill(pe, "kmT")
            for h in range(HG_HEADS):
                last = pe.transpose(b[0:META, h * P:(h + 1) * P], fmeta[:, h, :], ident[:, :])
            last.then_inc(job_done, 1)
            b = to_fill(pe, "s0")
            wait_emptied(pe, "kmT")
            for h in range(HG_HEADS):
                cut = slice(h * P, (h + 1) * P)
                last = pe.matmul(b[:, cut], kT_rows[0:META, cut], hgi[0:META, 2, cut], start=True, stop=True)
            last.then_inc(job_done, 1)
            pe.wait_ge(hg_fac, 2)
            b = to_fill(pe, "k1T")
            for h in range(HG_HEADS):
                last = pe.transpose(b[:, h * P:(h + 1) * P], lev[1][:, h, 0:P], ident[:, :])
            last.then_inc(job_done, 1)
            b = to_fill(pe, "s1")
            wait_emptied(pe, "k1T")
            for h in range(HG_HEADS):
                cut = slice(h * P, (h + 1) * P)
                last = pe.matmul(b[:, cut], kT_rows[:, cut], hgi[:, 0, cut], start=True, stop=True)
            last.then_inc(job_done, 1)

            for level in range(8):
                if level < 7:
                    pe.wait_ge(hg_fac, level + 3)
                for i in range(2):
                    b = to_fill(pe, f"level{level}", i)
                    for c in range(4):
                        h, tb = (4 * i + c) // 2, c % 2
                        cut = slice(tb * P, (tb + 1) * P)
                        if level < 7:
                            left = right = lev[level % 2][:, h, cut]
                        else:
                            left, right = hgk[:, h, META + tb * P:META + (tb + 1) * P], hgq[:, h, cut]
                        last = pe.matmul(b[:, c * P:(c + 1) * P], left, right, start=True, stop=True)
                    last.then_inc(job_done, 1)

            def sb_unit(i):
                tb, h = divmod(i, SB_HEADS)
                return tb, h, META + (tb + 1) * P, slice(SB_D * (h % 2), SB_D * (h % 2) + SB_D)

            def sb_scores(i):
                tb, h, w, half = sb_unit(i)
                b = to_fill(pe, f"z{i}")
                pe.matmul(b[:, 0:w], sbq[half, h // 2, tb * P:(tb + 1) * P], sbk[half, h // 2, 0:w],
                          start=True, stop=True).then_inc(job_done, 1)

            def sb_transpose(i):
                tb, h, w, half = sb_unit(i)
                pe.wait_ge(w_ready, i + 1)
                src = beta[i % 2]
                b = to_fill(pe, f"wT{i}")
                last = pe.transpose(b[0:META, 0:P], src[:, 0:META], ident[:, :])
                for k in range(tb + 1):
                    last = pe.transpose(b[:, (k + 1) * P:(k + 2) * P], src[:, META + k * P:META + (k + 1) * P], ident[:, :])
                last.then_inc(job_done, 1)

            def sb_values(i):
                tb, h, w, half = sb_unit(i)
                wait_emptied(pe, f"wT{i}")
                dst = bank[4 + tb][:, h * SB_D:(h + 1) * SB_D]
                cut = slice(h * SB_D, (h + 1) * SB_D)
                wT = wTs[i % 2]
                product(dst, [(wT[0:META, 0:P], sbv[0:META, 2, cut])] +
                        [(wT[:, (k + 1) * P:(k + 2) * P], sbv[:, k, cut]) for k in range(tb + 1)]).then_inc(wT_used, 1)

            for i in range(16 + 3):
                if i < 16:
                    sb_scores(i)
                if 2 <= i < 18:
                    sb_transpose(i - 2)
                if i >= 3:
                    sb_values(i - 3)

            pe.wait_ge(hg_fac, 10)
            for tb in range(TB):
                b = to_fill(pe, "ohg", tb)
                state = (S0, S1t)[tb]
                for h in range(HG_HEADS):
                    cut = slice(h * P, (h + 1) * P)
                    last = product(b[:, cut], [(score[:, 2 * h + tb, :], hgi[:, tb, cut]),
                                               (lev[0][:, h, tb * P:(tb + 1) * P], state[:, cut])])
                last.then_inc(job_done, 1)

            pe.wait_ge(rows_ready, 2)
            to_cols("mT", R)

            def rows_from(name, keys, lhs):
                for n, key in enumerate(keys):
                    w = wait_weights(pe, key).rearrange("p (k n) -> p k n", n=HALF)
                    for tb in range(TB):
                        b = to_fill(pe, name, 2 * n + tb)
                        product(b[:, :], [(lhs[:, k, tb * P:(tb + 1) * P], w[:, k, :]) for k in range(KT)]).then_inc(job_done, 1)

            wait_emptied(pe, "mT", 3)
            rows_from("w_out", [("w_out", 0), ("w_out", 1)], mixT)

            pe.wait_ge(rows_ready, 3)
            to_cols("x2T", R)
            wait_emptied(pe, "x2T", 3)
            pe.wait_ge(in_small, 16 * 6)
            b = to_fill(pe, "router")
            for tb in range(TB):
                last = product(b[:, tb * 64:tb * 64 + 36], [(XT[:, k, tb * P:(tb + 1) * P], w_router[:, k, :]) for k in range(KT)])
            last.then_inc(job_done, 1)
            pe.wait_ge(gate_ready, 1)
            b = to_fill(pe, "gT")
            for tb in range(TB):
                last = pe.transpose(b[0:EXPERTS, tb * P:(tb + 1) * P], sm(64 + 32 * tb, 32), ident[:, :])
            last.then_inc(job_done, 1)
            pe.wait_ge(tables_in, 16 * 3)
            b = to_fill(pe, "cbT")
            for tb in range(TB):
                at = tb * HEADS * CMP_PAD
                pe.transpose(b[:, at:at + P], ctmp[:, 0, tb * P:(tb + 1) * P], ident[:, :])
                last = pe.transpose(b[:, at + P:at + P + 64], ctmp[0:64, 1, tb * P:(tb + 1) * P], ident[0:64, 0:64])
            last.then_inc(job_done, 1)
            for name in ("router", "gT", "cbT"):
                wait_emptied(pe, name)

            def clear_y():
                for y in range(4):
                    pe.matmul(bank[4 + y][:, :], zeros[:, 0:P], zeros[:, :], start=True, stop=False)

            def down(hidden, w, dst_last):
                for tb in range(TB):
                    for n in range(2):
                        for q in range(2):
                            last = pe.matmul(bank[4 + 2 * tb + n][:, :], hidden[:, q, tb * P:(tb + 1) * P],
                                             w[:, q, n * HALF:(n + 1) * HALF], start=False, stop=dst_last and q == 1)
                return last

            def up(bank_at, tiles):
                for ab, weights_of in enumerate(tiles):
                    last = product(bank[bank_at][:, ab * T:(ab + 1) * T],
                                   [(weights_of(k), XT[:, k, 0:T]) for k in range(KT)])
                return last

            ph = phase_sems["moe"]
            base = first_unit["moe"]

            def moe_up(s, k, offset=0):
                e, half = s // 2, s % 2
                g = base + 3 * e
                if half == 0:
                    for n in (g, g + 1):
                        pe.wait_ge(landed[n % RING], k * 16 + use_count(n))
                wg = ring[:, g % RING, :].rearrange("p (k n) -> p k n", n=HALF)
                wu = ring[:, (g + 1) % RING, :].rearrange("p (k n) -> p k n", n=HALF)
                if s >= 1:
                    pe.wait_ge(ph["free"], k * 8 + max(2 * s - 2, 1))
                for q in range(2):
                    cut = slice((2 * half + q) * P, (2 * half + q + 1) * P)
                    last = up(2 * (s % 2) + q, [lambda kk, cut=cut: wg[:, kk, cut], lambda kk, cut=cut: wu[:, kk, cut]])
                    last.then_inc(ph["tile"], 1)

            def moe_down(s, k, final=False):
                e, half = s // 2, s % 2
                n = base + 3 * e + 2
                if half == 0:
                    pe.wait_ge(landed[n % RING], k * 16 + use_count(n))
                w = ring[:, n % RING, :].rearrange("p (k n) -> p k n", n=D)[:, 2 * half:2 * half + 2, :]
                pe.wait_ge(ph["hidden"], k * 8 + (2 * s + 2))
                down(hb[s % 2], w, final).then_inc(ph["used"], 1)

            pe.wait_ge(zero_ready, 1)
            pe.wait_ge(sb_out, 1)
            clear_y()
            moe_up(0, 0)
            with pe.Fori(0, EXPERTS // 2 - 1) as i:
                for u in range(4):
                    moe_up(u + 1, i)
                    moe_down(u, i)
            tail = STEPS_M - 4
            for u in range(3):
                moe_up(tail + u + 1, 0)
                moe_down(tail + u, 0)
            moe_down(STEPS_M - 1, 0, final=True)

            attention = [0]

            def attend(layer):
                mine = [u for u, key in enumerate(att) if key[0] == layer]

                def scores(u):
                    _, kind, pair, tb, h = att[u]
                    if u - mine[0] >= 2:
                        pe.wait_ge(at_m, 2 * (u - 1))
                    for seg in range(2):
                        r = h % 2 if kind == "nsa" else seg
                        half = slice(64 * r, 64 * r + 64)
                        if kind == "mem":
                            q, k, w = qmT[half, pair, :], km[layer][half, pair, :], MEM
                        else:
                            q, k, w = qT[half, pair, :], kT[half, seg if kind == "nsa" else pair, :], P * (tb + 1)
                        last = pe.matmul(bank[2 * (u % 2) + seg][:, 0:w], q[:, tb * P:(tb + 1) * P], k[:, 0:w], start=True, stop=True)
                        last.then_inc(at_l, 1)

                def blocks_of(u):
                    _, kind, pair, tb, h = att[u]
                    return 2 if kind == "mem" else tb + 1

                def trans(u):
                    pe.wait_ge(at_p, u + 1)
                    if u >= 2:
                        pe.wait_ge(at_tc, u - 1)
                    nb = blocks_of(u)
                    for seg in range(2):
                        for b in range(nb):
                            at = (seg * nb + b) * P
                            last = pe.transpose(bank[4 + u % 2][:, at:at + P], logit[u % 3][:, seg, b * P:(b + 1) * P], ident[:, :])
                    last.then_inc(at_t, 1)

                def values(u):
                    _, kind, pair, tb, h = att[u]
                    g, first = group_of(u)
                    pe.wait_ge(at_tc, u + 1)
                    if first and g >= 2:
                        pe.wait_ge(at_oc, g - 1)
                    nb = blocks_of(u)
                    o = bank[6 + g % 2]
                    for seg in range(2):
                        r = h % 2 if kind == "nsa" else seg
                        dst = o[64 * r:64 * r + 64, tb * P:(tb + 1) * P]
                        pairs = []
                        if kind == "nsa" and seg == 0:
                            pairs.append((vz[:, h % 4, :], pcT[:, h // 4, tb * P:(tb + 1) * P]))
                        for b in range(nb):
                            at = (seg * nb + b) * P
                            if kind == "nsa":
                                v = vrow0[:, b, 64 * seg:64 * seg + 64]
                            elif kind == "moba":
                                v = vrow[:, b, 64 * (h + seg):64 * (h + seg) + 64]
                            else:
                                v = vm[layer][:, b, 64 * (h + seg):64 * (h + seg) + 64]
                            pairs.append((v, pT[u % 2][:, at:at + P]))
                        for k, (lhsT, rhs) in enumerate(pairs):
                            last = pe.matmul(dst, lhsT, rhs, start=k == 0 and not (kind == "nsa" and seg == 1),
                                             stop=k == len(pairs) - 1 and not (kind == "nsa" and seg == 0))
                    last.then_inc(at_o, 1)

                n = len(mine)
                for i in range(n + 3):
                    if i < n:
                        scores(mine[i])
                    if 2 <= i < n + 2:
                        trans(mine[i - 2])
                    if i >= 3:
                        values(mine[i - 3])

            pe.wait_ge(ln_done, 1)
            to_cols("xTa", X)
            wait_emptied(pe, "xTa", 3)
            wa = [wait_weights(pe, ("a_in", c))[:, 0:KT * n].rearrange("p (k n) -> p k n", n=n)
                  for c, n in ((0, HALF), (1, HALF), (2, 1444 - 2 * HALF))]

            def a_cols(at, n):
                c = at // HALF
                return lambda k: wa[c][:, k, at - c * HALF:at - c * HALF + n]

            def twice(b, at, w_of):
                for r in range(2):
                    last = product(b[64 * r:64 * r + 64, at:at + T], [(w_of(k), XT[:, k, 0:T]) for k in range(KT)])
                return last

            def tiles(name, job, w_of_tiles):
                b = to_fill(pe, name, job)
                for i, w_of in enumerate(w_of_tiles):
                    last = product(b[:, i * T:(i + 1) * T], [(w_of(k), XT[:, k, 0:T]) for k in range(KT)])
                last.then_inc(job_done, 1)

            for j in range(3):
                tiles("a_q", j, [a_cols((2 * j + r) * P, P) for r in range(2)])
            b = to_fill(pe, "a_kv", 0)
            twice(b, 0, a_cols(768, 64))
            twice(b, T, a_cols(832, 64)).then_inc(job_done, 1)
            b = to_fill(pe, "a_kv", 1)
            twice(b, 0, a_cols(896, 64))
            twice(b, T, a_cols(1024, 64)).then_inc(job_done, 1)
            b = to_fill(pe, "a_kv", 2)
            for tb in range(TB):
                last = product(b[:, tb * 64:tb * 64 + 36], [(XT[:, k, tb * P:(tb + 1) * P], a_cols(1152, 36)(k)) for k in range(KT)])
            last.then_inc(job_done, 1)
            b = to_fill(pe, "a_v")
            for tb in range(TB):
                for i, at in enumerate((960, 1088)):
                    last = product(b[:, tb * P + 64 * i:tb * P + 64 * i + 64],
                                   [(XT[:, k, tb * P:(tb + 1) * P], a_cols(at, 64)(k)) for k in range(KT)])
            last.then_inc(job_done, 1)
            tiles("a_qm", 0, [a_cols(1188 + r * P, P) for r in range(2)])

            pe.wait_ge(cmp_in, 1)
            for kv in range(2):
                w = wait_weights(pe, (("cmp_k", "cmp_v")[kv], 0)).rearrange("p (j n) -> p j n", n=CMP_HID)
                b = to_fill(pe, "cmp_h", kv)
                for m in range(2):
                    last = product(b[:, m * CMP_PAD:m * CMP_PAD + N_CMP],
                                   [(w[:, j, m * P:(m + 1) * P], logit[2][:, kv, j * N_CMP:(j + 1) * N_CMP]) for j in range(16)])
                last.then_inc(job_done, 1)
            wait_emptied(pe, "cmp_h", 1)
            pe.wait_ge(in_small, 16 * 6)
            b = to_fill(pe, "cmp_kv")
            for r in range(2):
                product(b[64 * r:64 * r + 64, 0:CMP_PAD], [(w2[:, 0, m, :], hidT[:, m, 0:CMP_PAD]) for m in range(2)])
            for r in range(4):
                last = product(b[32 * r:32 * r + 32, 64:128], [(hidT[:, 2 + m, :], w2[:, 1, m, :]) for m in range(2)])
            last.then_inc(job_done, 1)
            wait_emptied(pe, "cmp_kv")
            for tb in range(TB):
                b = to_fill(pe, "cmp_l", tb)
                for pair in range(PAIRS):
                    last = pe.matmul(b[:, pair * 32:pair * 32 + 32], qT[:, pair, tb * P:(tb + 1) * P],
                                     kz[:, :, :].rearrange("p a b -> p (a b)"), start=True, stop=True)
                last.then_inc(job_done, 1)
            pe.wait_ge(cmp_x, 2)
            for j, n in enumerate((2, 1)):
                b = to_fill(pe, "cmp_pT", j)
                for i in range(n):
                    for tb in range(TB):
                        last = pe.transpose(b[:, i * T + tb * P:i * T + (tb + 1) * P],
                                            pc[:, tb, (2 * j + i) * P:(2 * j + i + 1) * P], ident[:, :])
                last.then_inc(job_done, 1)
            for name, i in (("cmp_l", 0), ("cmp_l", 1), ("cmp_pT", 0), ("cmp_pT", 1)):
                wait_emptied(pe, name, i)
            pe.wait_ge(y_used, 1)
            attend(0)
            pe.wait_ge(at_oc, 8)
            rows_from("a_out", [("a_out", 0), ("a_out", 1)], mixT)

            def ffn(layer):
                ph = phase_sems[f"ffn{layer}"]
                base = first_unit[f"ffn{layer}"]

                def ffn_up(j, k):
                    n = base + 3 * (j // 2) + j % 2
                    pe.wait_ge(landed[n % RING], k * 32 + use_count(n))
                    w = ring[:, n % RING, :].rearrange("p (k h n) -> p k h n", h=2, n=256)
                    if j >= 1:
                        pe.wait_ge(ph["hidden"], k * 8 + max(2 * j - 2, 1))
                    for q in range(2):
                        last = up(2 * (j % 2) + q, [lambda kk, h=h, q=q: w[:, kk, h, q * P:(q + 1) * P] for h in range(2)])
                        last.then_inc(ph["tile"], 1)

                def ffn_down(j, k, final=False):
                    n = base + 3 * (j // 2) + (2 if j < STEPS_F - 1 else 1)
                    if j % 2 == 0:
                        pe.wait_ge(landed[n % RING], k * 16 + use_count(n))
                    w = ring[:, n % RING, :].rearrange("p (k n) -> p k n", n=D)[:, 2 * (j % 2):2 * (j % 2) + 2, :]
                    pe.wait_ge(ph["hidden"], k * 8 + (2 * j + 2))
                    down(hb[j % 2], w, final).then_inc(ph["used"], 1)

                clear_y()
                ffn_up(0, 0)
                with pe.Fori(0, 2) as i:
                    for u in range(4):
                        ffn_up(u + 1, i)
                        ffn_down(u, i)
                for j in (8, 9):
                    ffn_up(j + 1, 0)
                    ffn_down(j, 0)
                ffn_down(10, 0, final=True)

            pe.wait_ge(ln_done, 3)
            to_cols("xTf0", X)
            for j in range(4):
                wait_emptied(pe, "xTf0", j)
            ffn(0)

            pe.wait_ge(ln_done, 5)
            to_cols("xTb", X)
            wait_emptied(pe, "xTb", 3)
            wk = [wait_weights(pe, ("kv", c)).rearrange("p (k n) -> p k n", n=HALF) for c in range(3)]

            def kv_cols(at, n):
                return lambda k: wk[at // HALF][:, k, at % HALF:at % HALF + n]

            for j in range(3):
                tiles("b_k", j, [kv_cols((2 * j + r) * P, P) for r in range(2)])
            for i, (tb, at, n) in enumerate([(tb, at, n) for at, n in ((768, 256), (1024, 512)) for tb in range(TB)]):
                b = to_fill(pe, "b_v", i)
                product(b[:, 0:n], [(XT[:, k, tb * P:(tb + 1) * P], kv_cols(at, n)(k)) for k in range(KT)]).then_inc(job_done, 1)
            wq = [wait_weights(pe, ("b_in", c)).rearrange("p (k n) -> p k n", n=HALF) for c in range(2)]

            def b_cols(at):
                return lambda k: wq[at // HALF][:, k, at % HALF:at % HALF + P]

            for j in range(3):
                tiles("b_q", j, [b_cols((2 * j + r) * P) for r in range(2)])
            tiles("b_qm", 0, [b_cols(768 + r * P) for r in range(2)])
            for j in range(3):
                wait_emptied(pe, "b_q", j)
            wait_emptied(pe, "b_qm")
            attend(1)
            pe.wait_ge(at_oc, 16)
            rows_from("b_out", [("b_out", 0), ("b_out", 1)], mixT)
            pe.wait_ge(ln_done, 7)
            to_cols("xTf1", X)
            for j in range(4):
                wait_emptied(pe, "xTf1", j)
            ffn(1)

        @block.scalar
        def _(act):
            step = chained(act, act_step)

            def empty(name, i, *moves):
                b = filled(act, name, i)
                for dst, src, func in moves:
                    last = act.activation(dst, src(b), func)
                last.then_inc(emptied_a, 1)

            act.wait_ge(pool_const, 1)
            act.wait_ge(in_x, 32)
            step(act.activation(junk, X[:, 0, :], ACT.Square, accum_out=sm(0, 1)))
            step(act.activation(junk, X[:, 1, :], ACT.Square, accum_out=sm(1, 1)))
            act.activation(junk[0:META, :], meta, ACT.Square, accum_out=small[0:META, 2:3]).then_inc(sq_ready, 1)

            empty("pack", 0, (cols[:, :], lambda b: b[:, 0:PACK_ROWS + 2 * CONV_ROWS], ACT.Copy))
            for j in range(4):
                empty("memT", j, (memT[:, 2 * j:2 * j + 2, :], lambda b: b[:, :].rearrange("p (a t) -> p a t", t=T), ACT.Copy))
            act.wait_ge(stat_ready, 1)
            act.activation(sm(3, 3), sm(3, 3), ACT.Sqrt).then_inc(sq_ready, 1)
            for l, name in enumerate(("mem_a", "mem_b")):
                for i, dst in enumerate((km[l], vm[l])):
                    empty(name, i, (dst[:, :, :].rearrange("p a b -> p (a b)"), lambda b: b[:, :], ACT.Copy))
            for i, (at, n) in enumerate(((0, DIST_REV), (DIST_REV, DIST_FWD))):
                empty("dist", i, (dist_out[:, at:at + n], lambda b, n=n: b[0:HEADS, 0:n], ACT.Copy))

            act.wait_ge(lbound_ready, 1)
            act.activation(sm(16, 8), sm(16, 8), ACT.Exp).then_inc(lbound_ready, 1)

            for h in range(HG_HEADS):
                b = filled(act, "hgf", h)
                act.activation(logf[:, h, :], b[:, 0:S1], ACT.Sigmoid)
                act.activation(hgk[:, h, :], b[:, 0:S1], ACT.Sigmoid, scale=-1.0).then_inc(emptied_a, 1)
            pair = lambda b: b[:, :].rearrange("p (a t) -> p a t", t=T)
            for i in range(2):
                empty("hgq", i, (hgq[:, 2 * i:2 * i + 2, :], pair, ACT.Silu))
            act.wait_ge(dist_stored, 16)
            act.wait_ge(hg_f, 1)
            act.activation(logf[:, :, :], logf[:, :, :], ACT.Ln).then_inc(hg_log, 1)
            for i in range(3):
                n = META if i == 2 else P
                empty("hgi", i, (hgi[0:n, i, :], lambda b, n=n: b[0:n, :], ACT.Copy))
            for i in range(2):
                empty("hgg", i, (hgg[:, i, :], lambda b: b[:, :], ACT.Silu))

            def decay(k):
                dst = [fmeta[:, :, :], lev[1][:, :, 0:P]] + [lev[level % 2][:, :, :] for level in range(7)] + [lev[0][:, :, :]]
                act.wait_ge(hg_arg, k + 1)
                act.activation(dst[k], dst[k], ACT.Exp).then_inc(hg_exp, 1)

            decay(0)
            decay(1)
            act.activation(sm(24, 4), bcum[:, :, P - 1], ACT.Exp).then_inc(hg_q, 1)
            for i in range(2):
                empty("sbq", i, (sbq[:, 2 * i:2 * i + 2, :], pair, ACT.Copy))
            for i in range(4):
                empty("sbk", i, (sbk[:, i, :], lambda b: b[:, 0:S1], ACT.Copy))
            for i in range(3):
                n = META if i == 2 else P
                empty("sbv", i, (sbv[0:n, i, :], lambda b, n=n: b[0:n, :], ACT.Copy))
            empty("kmT", 0, (kT_rows[0:META, :], lambda b: b[0:META, :], ACT.Copy))
            empty("s0", 0, (S0, lambda b: b[:, :], ACT.Copy))
            empty("k1T", 0, (kT_rows, lambda b: b[:, :], ACT.Copy))
            for k in range(2, 10):
                decay(k)

            def sb_sigmoids(i):
                w = META + (i // SB_HEADS + 1) * P
                wait_emptied(act, f"z{i}")
                if i >= 2:
                    act.wait_ge(w_ready, i - 1)
                    act.wait_ge(job_done, jobs.number(f"wT{i - 2}") + 1)
                act.activation(beta[i % 2][:, 0:w], zm[i % 2][:, 0:w], ACT.Sigmoid)
                act.activation(keep[i % 2][:, 0:w], zm[i % 2][:, 0:w], ACT.Sigmoid, scale=-1.0).then_inc(sig_ready, 1)

            def sb_transposed(i):
                tb = i // SB_HEADS
                b = filled(act, f"wT{i}")
                if i >= 2:
                    act.wait_ge(wT_used, i - 1)
                act.activation(wTs[i % 2][0:META, 0:P], b[0:META, 0:P], ACT.Copy)
                act.activation(wTs[i % 2][:, P:P * (tb + 2)], b[:, P:P * (tb + 2)], ACT.Copy).then_inc(emptied_a, 1)

            for i in range(16 + 2):
                if i >= 2:
                    sb_transposed(i - 2)
                if i < 16:
                    sb_sigmoids(i)

            act.wait_ge(stat_ready, 2)
            act.activation(sm(30, 24), sm(30, 24), ACT.Sqrt).then_inc(sq_ready, 1)

            def empty_gained(name, gain_at):
                for j in range(4):
                    b = filled(act, name, j)
                    for r in range(2):
                        k = 2 * j + r
                        last = act.activation(XT[:, k, 0:T], b[:, r * T:(r + 1) * T], ACT.Copy, scale=cols[:, gain_at + k:gain_at + k + 1])
                    last.then_inc(emptied_a, 1)

            empty_gained("mT", PACK["sb_gain"][0])
            wait_emptied(act, "w_out", 3)
            for tb in range(TB):
                last = act.activation(R[:, tb, :], X[:, tb, :], ACT.Square, accum_out=sm(6 + tb, 1))
            last.then_inc(sq_ready, 1)
            act.wait_ge(stat_ready, 3)
            act.activation(sm(8, 2), sm(8, 2), ACT.Sqrt).then_inc(sq_ready, 1)
            empty_gained("x2T", PACK["g_ffn"][0])

            act.wait_ge(router_arg, 1)
            act.activation(sm(200, 8), sm(200, 8), ACT.Exp).then_inc(router_exp, 1)
            act.wait_ge(router_arg, 2)
            act.activation(sm(240, 2), sm(240, 2), ACT.Exp).then_inc(router_exp, 1)

            act.wait_ge(gT_stored, 16)
            ph = phase_sems["moe"]

            def moe_silu(s, k):
                for q in range(2):
                    act.wait_ge(ph["tile"], k * 8 + (2 * s + q + 1))
                    if s >= 1:
                        act.wait_ge(ph["hidden"], k * 8 + max(2 * s - 2 + q, 1))
                    act.activation(work[(2 * s + q) % 4], bank[2 * (s % 2) + q][:, 0:T], ACT.Silu).then_inc(ph["act"], 1)

            moe_silu(0, 0)
            with act.Fori(0, EXPERTS // 2 - 1) as i:
                for u in range(4):
                    moe_silu(u + 1, i)
            for s in range(STEPS_M - 3, STEPS_M):
                moe_silu(s, 0)

            act.wait_ge(y_used, 1)
            for tb in range(TB):
                last = act.activation(R[:, tb, :], X[:, tb, :], ACT.Square, accum_out=sm(10 + tb, 1))
            last.then_inc(sq_ready, 1)
            act.wait_ge(stat_ready, 4)
            act.activation(sm(12, 2), sm(12, 2), ACT.Sqrt).then_inc(sq_ready, 1)

            def empty_cols(name):
                for j in range(4):
                    empty(name, j, (XT[:, 2 * j:2 * j + 2, 0:T], pair, ACT.Copy))

            empty_cols("xTa")
            for j in range(3):
                empty("a_q", j, (qT[:, 2 * j:2 * j + 2, :], pair, ACT.Copy))
            b = filled(act, "a_kv", 0)
            for kv in range(2):
                act.activation(shift2[0:64, kv, :], b[0:64, kv * T:(kv + 1) * T], ACT.Copy)
                last = act.activation(shift2[64:128, kv, 0:T - 1], b[64:128, kv * T + 1:(kv + 1) * T], ACT.Copy)
            last.then_inc(emptied_a, 1)
            empty("a_kv", 1, (kT[:, 0:2, :], pair, ACT.Copy))
            empty("a_kv", 2, (sm(260, 72).rearrange("p (b g) -> p b g", b=2),
                              lambda b: b[:, 0:128].rearrange("p (b g) -> p b g", b=2)[:, :, 0:36], ACT.Sigmoid))
            empty("a_v", 0, (vrow0[:, :, :], lambda b: b[:, 0:2 * P].rearrange("p (b n) -> p b n", b=2), ACT.Copy))
            empty("a_qm", 0, (qmT[:, :, :], pair, ACT.Copy))
            act.wait_ge(pool_step, 1)
            for kv in range(2):
                empty("cmp_h", kv, (hidT[:, 2 * kv:2 * kv + 2, 0:N_CMP],
                                    lambda b: b[:, 0:2 * CMP_PAD].rearrange("p (m n) -> p m n", m=2)[:, :, 0:N_CMP], ACT.Gelu_apprx_tanh))
            b = filled(act, "cmp_kv")
            for r in range(2):
                act.activation(kz[64 * r:64 * r + 64, r, :], b[64 * r:64 * r + 64, 0:CMP_PAD], ACT.Copy)
            for r in range(4):
                last = act.activation(vz[32 * r:32 * r + 32, r, :], b[32 * r:32 * r + 32, 64:128], ACT.Copy)
            last.then_inc(emptied_a, 1)
            act.wait_ge(cmp_e, 1)
            act.activation(sm(340, 12 * 16 + 0), sm(340, 192), ACT.Exp).then_inc(cmp_e, 1)
            act.wait_ge(cmp_e, 3)
            act.activation(sm(340, 192), sm(340, 192), ACT.Exp).then_inc(cmp_e, 1)
            for j, n in enumerate((2, 1)):
                empty("cmp_pT", j, (pcT[:, 2 * j:2 * j + n, :], lambda b, n=n: b[:, 0:n * T].rearrange("p (a t) -> p a t", t=T), ACT.Copy))

            def attend(layer):
                mine = [u for u, key in enumerate(att) if key[0] == layer]

                def exps(u):
                    act.wait_ge(at_x, u + 1)
                    w = width(u)
                    for seg in range(2):
                        last = act.activation(logit[u % 3][:, seg, 0:w], logit[u % 3][:, seg, 0:w], ACT.Exp,
                                              bias=sm(540 + 8 * (u % 3) + seg, 1), accum_out=sm(542 + 8 * (u % 3) + seg, 1))
                    last.then_inc(at_e, 1)

                def trans(u):
                    act.wait_ge(at_t, u + 1)
                    if u >= 2:
                        act.wait_ge(at_o, u - 1)
                    n = 2 * width(u)
                    act.activation(pT[u % 2][:, 0:n], bank[4 + u % 2][:, 0:n], ACT.Copy).then_inc(at_tc, 1)

                for i in range(len(mine) + 2):
                    if i < len(mine):
                        exps(mine[i])
                    if i >= 2:
                        trans(mine[i - 2])

            attend(0)

            def norm_root(k):
                act.wait_ge(stat_ready, 5 + k)
                act.activation(sm(600, 2), sm(600, 2), ACT.Sqrt).then_inc(sq_ready, 1)

            def ffn(layer):
                ph = phase_sems[f"ffn{layer}"]
                at_w = PACK_ROWS + layer * CONV_ROWS
                at_b = PACK["conv_b"][0] + layer * FFT

                def gelu_step(j, k):
                    for q in range(2):
                        act.wait_ge(ph["tile"], k * 8 + (2 * j + q + 1))
                        if j >= 1:
                            act.wait_ge(ph["hidden"], k * 8 + max(2 * j - 2 + q, 1))
                        act.activation(work[(2 * j + q) % 4], bank[2 * (j % 2) + q][:, 0:T], ACT.Identity,
                                       scale=cols[:, bass.ds(k * 8 + (at_w + 2 * FFT + 2 * j + q), 1)],
                                       bias=cols[:, bass.ds(k * 8 + (at_b + 2 * j + q), 1)]).then_inc(ph["act"], 1)
                    for q in range(2):
                        act.wait_ge(mulp[f"ffn{layer}"], k * 8 + (2 * j + q + 1))
                        w = work[(2 * j + q) % 4]
                        act.activation(w, w, ACT.Gelu_apprx_tanh).then_inc(act2[f"ffn{layer}"], 1)

                gelu_step(0, 0)
                with act.Fori(0, 2) as i:
                    for u in range(4):
                        gelu_step(u + 1, i)
                for j in (9, 10):
                    gelu_step(j, 0)

            norm_root(0)
            empty_cols("xTf0")
            ffn(0)
            norm_root(1)
            empty_cols("xTb")
            for j in range(3):
                empty("b_k", j, (kT[:, 2 * j:2 * j + 2, :], pair, ACT.Copy))
            for i, (tb, at, n) in enumerate([(tb, at, n) for at, n in ((0, 256), (256, 512)) for tb in range(TB)]):
                empty("b_v", i, (vrow[:, tb, at:at + n], lambda b, n=n: b[:, 0:n], ACT.Copy))
            for j in range(3):
                empty("b_q", j, (qT[:, 2 * j:2 * j + 2, :], pair, ACT.Copy))
            empty("b_qm", 0, (qmT[:, :, :], pair, ACT.Copy))
            attend(1)
            norm_root(2)
            empty_cols("xTf1")
            ffn(1)
            norm_root(3)

        @block.vector
        def _(dve):
            step = chained(dve, dve_step)
            tt, ts, stt = dve.tensor_tensor, dve.tensor_scalar, dve.scalar_tensor_tensor

            def emptied_self():
                dve.wait_ge(emptied_v, emptied_self.count)
            emptied_self.count = 0

            def count_emptied(instruction):
                emptied_self.count += 1
                instruction.then_inc(emptied_v, 1)

            dve.memset(arena[BUCKETS:BUCKETS + 1, at_hgi + 900:at_hgi + 900 + HEADS], NEG).then_inc(dist_ready, 1)

            dve.wait_ge(sq_ready, 1)
            step(ts(sm(3, 2), sm(0, 2), 1.0 / D, EPS, ALU.mult, ALU.add))
            ts(small[0:META, 5:6], small[0:META, 2:3], 1.0 / D, EPS, ALU.mult, ALU.add).then_inc(stat_ready, 1)
            dve.wait_ge(sq_ready, 2)
            step(dve.reciprocal(sm(3, 3), sm(3, 3)))
            dve.wait_ge(job_done, jobs.number("memT", 3) + 1)
            ts(meta, meta, small[0:META, 5:6], None, ALU.mult)
            for tb in range(TB):
                last = ts(R[:, tb, :], X[:, tb, :], sm(3 + tb, 1), None, ALU.mult)
            last.then_inc(rows_ready, 1)

            wait_emptied(dve, "pack")
            l0, l1 = (cols[:, PACK["lb"][0] + 4 * i:PACK["lb"][0] + 4 * i + 4] for i in range(2))
            step(tt(sm(650, 4), l0, l1, ALU.max))
            tt(sm(16, 4), l0, sm(650, 4), ALU.subtract)
            tt(sm(20, 4), l1, sm(650, 4), ALU.subtract).then_inc(lbound_ready, 1)

            for k in range(KT):
                b = filled(dve, "aT", k)
                at = PACK["g_mix"][0] + k
                count_emptied(ts(XT[:, k, :], b[:, 0:S1], cols[:, at:at + 1], None, ALU.mult))

            dve.wait_ge(lbound_ready, 2)
            step(tt(sm(650, 4), sm(16, 4), sm(20, 4), ALU.add))
            step(dve.reciprocal(sm(650, 4), sm(650, 4)))
            step(tt(sm(16, 4), sm(16, 4), sm(650, 4), ALU.mult))
            step(ts(sm(20, 4), sm(16, 4), -1.0, 1.0, ALU.mult, ALU.add))

            for h in range(HG_HEADS):
                wait_emptied(dve, "hgf", h)
                ts(logf[:, h, :], logf[:, h, :], sm(20 + h, 1), sm(16 + h, 1), ALU.mult, ALU.add)
                last = ts(hgk[:, h, :], hgk[:, h, :], sm(20 + h, 1), None, ALU.mult)
            last.then_inc(hg_f, 1)
            dve.wait_ge(hg_log, 1)
            dve.wait_ge(pool_const, 3)
            for h in range(HG_HEADS):
                dve.tensor_tensor_scan(bmeta[:, h, :], ones[:, 0:META], logf[:, h, 0:META], 0.0, ALU.mult, ALU.add)
                for c in range(TB):
                    last = dve.tensor_tensor_scan(bcum[:, h, c * P:(c + 1) * P], ones[:, 0:P],
                                                  logf[:, h, META + c * P:META + (c + 1) * P], 0.0, ALU.mult, ALU.add)
            step(last)
            tt(fmeta[:, :, :], bmeta[:, :, META - 1:META].broadcast_to([P, 4, META]), bmeta[:, :, :], ALU.subtract).then_inc(hg_arg, 1)
            tt(lev[1][:, :, 0:P], bcum[:, :, P - 1:P].broadcast_to([P, 4, P]), bcum[:, :, 0:P], ALU.subtract).then_inc(hg_arg, 1)

            def sides(t, half):
                v = t.rearrange("p h (x two r) -> p h x two r", two=2, r=half)
                return v[:, :, :, 0, :], v[:, :, :, 1, :]

            def flat_sides(t, half):
                v = t.rearrange("p h t -> p (h t)").rearrange("p (x two r) -> p x two r", two=2, r=half)
                return v[:, :, 0, :], v[:, :, 1, :]

            def level_args(level):
                half = P >> (level + 1)
                left, right = flat_sides(bcum[:, :, :], half)
                to_left, to_right = flat_sides(lev[level % 2][:, :, :], half)
                shape = list(left.shape)
                ref = left[:, :, half - 1:half].broadcast_to(shape)
                tt(to_left, ref, left, ALU.subtract)
                tt(to_right, right, ref, ALU.subtract).then_inc(hg_arg, 1)

            def level_factors(level):
                half = P >> (level + 1)
                dve.wait_ge(hg_exp, level + 3)
                to_left, to_right = sides(lev[level % 2][:, :, :], half)
                tt(to_left, to_left, sides(hgk[:, :, META:S1], half)[0], ALU.mult)
                tt(to_right, to_right, sides(hgq[:, :, :], half)[1], ALU.mult).then_inc(hg_fac, 1)

            def level_scores(level):
                for i in range(2):
                    b = filled(dve, f"level{level}", i)
                    count_emptied(dve.copy_predicated(score[:, 4 * i:4 * i + 4, :],
                                                      level_mask[:, level:level + 1, :].broadcast_to([P, 4, P]),
                                                      b[:, :].rearrange("p (a t) -> p a t", t=P)))

            dve.wait_ge(hg_exp, 1)
            tt(fmeta[:, :, :], fmeta[:, :, :], hgk[:, :, 0:META], ALU.mult).then_inc(hg_fac, 1)
            level_args(0)
            dve.wait_ge(hg_exp, 2)
            tt(lev[1][:, :, 0:P], lev[1][:, :, 0:P], hgk[:, :, META:META + P], ALU.mult).then_inc(hg_fac, 1)
            wait_emptied(dve, "hgq", 1)
            b = filled(dve, "s1")
            wait_emptied(dve, "s0")
            dve.wait_ge(hg_q, 1)
            for h in range(HG_HEADS):
                cut = slice(h * P, (h + 1) * P)
                last = stt(S1t[:, cut], S0[:, cut], sm(24 + h, 1), b[:, cut], ALU.mult, ALU.add)
            count_emptied(last)
            dve.wait_ge(mask_ready, 1)
            for level in range(7):
                if level < 6:
                    if level == 0:
                        dve.wait_ge(job_done, jobs.number("k1T") + 1)
                    else:
                        dve.wait_ge(job_done, jobs.number(f"level{level - 1}", 1) + 1)
                    level_args(level + 1)
                level_factors(level)
                if level >= 1:
                    level_scores(level - 1)
                    emptied_self()
            level_scores(6)
            emptied_self()
            level_scores(7)
            dve.wait_ge(job_done, jobs.number("level6", 1) + 1)
            dve.tensor_copy(lev[0][:, :, :], bcum[:, :, :]).then_inc(hg_arg, 1)
            dve.wait_ge(hg_exp, 10)
            tt(lev[0][:, :, :], lev[0][:, :, :], hgq[:, :, :], ALU.mult).then_inc(hg_fac, 1)

            def sb_masked(i):
                tb = i // SB_HEADS
                w = META + (tb + 1) * P
                b = filled(dve, f"z{i}")
                count_emptied(stt(zm[i % 2][:, 0:w], b[:, 0:w], SCALE, sbmask[:, tb, 0:w], ALU.mult, ALU.add))

            def sb_shares(i):
                tb = i // SB_HEADS
                w = META + (tb + 1) * P
                if i % SB_HEADS < 2:
                    step(dve.memset(keep[i % 2][:, w:w + 1], 1.0))
                dve.wait_ge(sig_ready, i + 1)
                step(dve.tensor_tensor_scan(zm[i % 2][:, w - 1::-1], keep[i % 2][:, w:0:-1], ones[:, 0:w], 1.0, ALU.mult, ALU.mult))
                tt(beta[i % 2][:, 0:w], beta[i % 2][:, 0:w], zm[i % 2][:, 0:w], ALU.mult).then_inc(w_ready, 1)

            dve.wait_ge(mask_ready, 3)
            for i in range(17):
                if i < 16:
                    if i >= 2:
                        dve.wait_ge(w_ready, i - 1)
                    sb_masked(i)
                if i >= 1:
                    sb_shares(i - 1)

            dve.wait_ge(wT_used, 16)
            for tb in range(TB):
                last = dve.tensor_copy(R[:, tb, 0:HALF], bank[4 + tb][:, :])
            last.then_inc(sb_out, 1)
            for tb in range(TB):
                b = filled(dve, "ohg", tb)
                count_emptied(dve.tensor_copy(R[:, tb, HALF:D], b[:, :]))
            emptied_self()
            for tb in range(TB):
                last = tt(lev[tb][:, :, :].rearrange("p a b -> p (a b)"), R[:, tb, :], R[:, tb, :], ALU.mult)
            step(last)
            for tb in range(TB):
                sq = lev[tb][:, :, :].rearrange("p a b -> p (a b)")
                dve.reduce_sum(sm(30 + 12 * tb, 8), sq[:, 0:HALF].rearrange("p (h d) -> p h d", d=SB_D), axis=AX.X)
                last = dve.reduce_sum(sm(38 + 12 * tb, 4), sq[:, HALF:D].rearrange("p (h d) -> p h d", d=P), axis=AX.X)
            step(last)
            for tb in range(TB):
                ts(sm(30 + 12 * tb, 8), sm(30 + 12 * tb, 8), 1.0 / SB_D, EPS, ALU.mult, ALU.add)
                last = ts(sm(38 + 12 * tb, 4), sm(38 + 12 * tb, 4), 1.0 / P, EPS, ALU.mult, ALU.add)
            last.then_inc(stat_ready, 1)
            dve.wait_ge(sq_ready, 3)
            step(dve.reciprocal(sm(30, 24), sm(30, 24)))
            wait_emptied(dve, "hgg", 1)
            for tb in range(TB):
                for at, n, d, r in ((0, SB_HEADS, SB_D, 30), (HALF, HG_HEADS, P, 38)):
                    v = R[:, tb, at:at + HALF].rearrange("p (h d) -> p h d", d=d)
                    last = tt(v, v, sm(r + 12 * tb, n).unsqueeze(2).broadcast_to([P, n, d]), ALU.mult)
            step(last)
            for tb in range(TB):
                last = tt(R[:, tb, HALF:D], R[:, tb, HALF:D], hgg[:, tb, :], ALU.mult)
            last.then_inc(rows_ready, 1)

            def add_rows(name, scale):
                for n in range(2):
                    for tb in range(TB):
                        b = filled(dve, name, 2 * n + tb)
                        v = X[:, tb, n * HALF:(n + 1) * HALF]
                        count_emptied(stt(v, v, scale, b[:, :], ALU.mult, ALU.add))
                emptied_self()

            def rms(at, k):
                dve.wait_ge(sq_ready, k + 1)
                ts(sm(at + 2, 2), sm(at, 2), 1.0 / D, EPS, ALU.mult, ALU.add).then_inc(stat_ready, 1)
                dve.wait_ge(sq_ready, k + 2)
                step(dve.reciprocal(sm(at + 2, 2), sm(at + 2, 2)))

            add_rows("w_out", 1.0)
            rms(6, 3)
            for tb in range(TB):
                last = ts(R[:, tb, :], X[:, tb, :], sm(8 + tb, 1), None, ALU.mult)
            last.then_inc(rows_ready, 1)

            per_tb = lambda v: v.rearrange("p (b n) -> p b n", b=TB)
            dve.wait_ge(in_small, 16 * 6)
            b = filled(dve, "router")
            rl = per_tb(sm(650, 72))
            count_emptied(tt(rl, per_tb(b[:, 0:128])[:, :, 0:36], bias36[:, :].unsqueeze(1).broadcast_to([P, TB, 36]), ALU.add))
            emptied_self()
            wide = lambda v, n: v.unsqueeze(2).broadcast_to([P, TB, n])
            iota = lambda n: sm(850, n).unsqueeze(1).broadcast_to([P, TB, n])

            def first_best(dst, src, best, n, scratch, index):
                step(tt(per_tb(scratch), src, wide(best, n), ALU.is_lt))
                step(stt(per_tb(scratch), per_tb(scratch), 100.0, iota(n), ALU.mult, ALU.add))
                step(dve.tensor_reduce(index, per_tb(scratch), axis=AX.X, op=ALU.min))
                step(tt(dst, iota(n), wide(index, n), ALU.is_equal))

            step(dve.reduce_max(sm(722, 2), rl[:, :, 0:GROUPS], axis=AX.X))
            tt(per_tb(sm(200, 8)), rl[:, :, 0:GROUPS], wide(sm(722, 2), GROUPS), ALU.subtract).then_inc(router_arg, 1)
            first_best(per_tb(sm(736, 8)), rl[:, :, 0:GROUPS], sm(722, 2), GROUPS, sm(726, 8), sm(734, 2))
            step(ts(sm(736, 8), sm(736, 8), -1.0, -NEG, ALU.add, ALU.mult))
            el = sm(744, 64).rearrange("p (b g e) -> p b g e", b=TB, g=GROUPS)
            for tb in range(TB):
                last = tt(el[:, tb], rl[:, tb, GROUPS:36].rearrange("p (g e) -> p g e", g=GROUPS),
                          sm(736 + 4 * tb, 4).unsqueeze(2).broadcast_to([P, GROUPS, PER_GROUP]), ALU.add)
            step(last)
            elf = per_tb(sm(744, 64))
            step(dve.reduce_max(sm(808, 2), elf, axis=AX.X))
            oh1, oh2 = per_tb(sm(64, 64)), per_tb(sm(128, 64))
            first_best(oh1, elf, sm(808, 2), EXPERTS, sm(128, 64), sm(810, 2))
            step(stt(elf, oh1, 3 * NEG, elf, ALU.mult, ALU.add))
            step(dve.reduce_max(sm(812, 2), elf, axis=AX.X))
            tt(sm(240, 2), sm(812, 2), sm(808, 2), ALU.subtract).then_inc(router_arg, 1)
            first_best(oh2, elf, sm(812, 2), EXPERTS, sm(128, 64), sm(814, 2))
            dve.wait_ge(router_exp, 1)
            step(dve.reduce_sum(sm(816, 2), per_tb(sm(200, 8)), axis=AX.X))
            step(dve.reciprocal(sm(816, 2), sm(816, 2)))
            dve.wait_ge(router_exp, 2)
            step(ts(sm(818, 2), sm(240, 2), 1.0, None, ALU.add))
            step(dve.reciprocal(sm(818, 2), sm(818, 2)))
            step(tt(sm(818, 2), sm(818, 2), sm(816, 2), ALU.mult))
            step(tt(sm(820, 2), sm(818, 2), sm(240, 2), ALU.mult))
            for tb in range(TB):
                last = ts(sm(64 + 32 * tb, 32), sm(64 + 32 * tb, 32), sm(818 + tb, 1), None, ALU.mult)
            step(last)
            for tb in range(TB):
                v = sm(64 + 32 * tb, 32)
                last = stt(v, sm(128 + 32 * tb, 32), sm(820 + tb, 1), v, ALU.mult, ALU.add)
            last.then_inc(gate_ready, 1)
            b = filled(dve, "gT")
            count_emptied(dve.tensor_copy(work[0][0:EXPERTS, :], b[0:EXPERTS, 0:T]))
            b = filled(dve, "cbT")
            count_emptied(dve.tensor_copy(cbias[:, :, :].rearrange("p a b -> p (a b)"), b[:, 0:2 * HEADS * CMP_PAD]))

            ph = phase_sems["moe"]

            def moe_product(s, k):
                for q in range(2):
                    dve.wait_ge(ph["act"], k * 8 + (2 * s + q + 1))
                    w = work[(2 * s + q) % 4]
                    tt(w, w, bank[2 * (s % 2) + q][:, T:2 * T], ALU.mult).then_inc(ph["free"], 1)
                for q in range(2):
                    dve.wait_ge(ph["free"], k * 8 + (2 * s + q + 1))
                    if s >= 1:
                        dve.wait_ge(ph["used"], k * 4 + max(s - 1, 1))
                    tt(hb[s % 2][:, q, :], work[(2 * s + q) % 4], gflat[:, bass.ds(k * (2 * T) + (s // 2) * T, T)],
                       ALU.mult).then_inc(ph["hidden"], 1)

            gflat = gb[:, :, :].rearrange("p a b -> p (a b)")
            dve.wait_ge(gb_in, 16 * 4)
            moe_product(0, 0)
            with dve.Fori(0, EXPERTS // 2 - 1) as i:
                for u in range(4):
                    moe_product(u + 1, i)
            for s in range(STEPS_M - 3, STEPS_M):
                moe_product(s, 0)

            def add_y(ph, steps, scale):
                dve.wait_ge(phase_sems[ph]["used"], steps)
                for tb in range(TB):
                    for n in range(2):
                        v = X[:, tb, n * HALF:(n + 1) * HALF]
                        last = stt(v, v, scale, bank[4 + 2 * tb + n][:, :], ALU.mult, ALU.add)
                return last

            add_y("moe", STEPS_M, 1.0).then_inc(y_used, 1)
            dve.wait_ge(y_used, 1)
            rms(10, 5)
            dve.wait_ge(rowvec_in, 16)
            for tb in range(TB):
                last = stt(X[:, tb, :], X[:, tb, :], sm(12 + tb, 1), rowvec[:, 0, :], ALU.mult, ALU.mult)
            last.then_inc(ln_done, 1)

            wait_emptied(dve, "a_kv", 0)
            for kv, pe_at in enumerate((PACK["pe_k"][0], PACK["pe_v"][0])):
                v = shift2[:, kv, :]
                v = bass.AP(tensor=v.tensor, offset=v.offset, ap=[list(v.ap[0]), [2, 16], [CMP_STRIDE, N_CMP]])
                last = tt(logit[2][:, kv, 0:16 * N_CMP].rearrange("p (j n) -> p j n", n=N_CMP), v,
                          cols[:, pe_at:pe_at + 16].unsqueeze(2).broadcast_to([P, 16, N_CMP]), ALU.add)
            last.then_inc(cmp_in, 1)
            dve.wait_ge(pool_step, 1)
            wait_emptied(dve, "a_kv", 2)
            for tb in range(TB):
                heads = lambda v: v.rearrange("p (h n) -> p h n", n=CMP_PAD)
                lc = sm(340, HEADS * CMP_PAD)
                b = filled(dve, "cmp_l", tb)
                count_emptied(stt(lc, b[:, 0:HEADS * CMP_PAD], SCALE, cbias[:, tb, :], ALU.mult, ALU.add))
                emptied_self()
                step(dve.reduce_max(sm(564, HEADS), heads(lc), axis=AX.X))
                tt(heads(lc), heads(lc), sm(564, HEADS).unsqueeze(2).broadcast_to([P, HEADS, CMP_PAD]), ALU.subtract).then_inc(cmp_e, 1)
                dve.wait_ge(cmp_e, 2 * tb + 2)
                step(stt(lc, cbias[:, tb, :], NEG / 10, lc, ALU.is_gt, ALU.mult))
                step(dve.reduce_sum(sm(576, HEADS), heads(lc), axis=AX.X))
                step(ts(sm(576, HEADS), sm(576, HEADS), TINY, None, ALU.max))
                step(dve.reciprocal(sm(576, HEADS), sm(576, HEADS)))
                gates = sm(260 + 36 * tb, 36).rearrange("p (h g) -> p h g", g=3)
                step(tt(sm(576, HEADS), sm(576, HEADS), gates[:, :, 0], ALU.mult))
                tt(pc[:, tb, :].rearrange("p (h n) -> p h n", n=32)[:, :, 0:CMP_PAD], heads(lc),
                   sm(576, HEADS).unsqueeze(2).broadcast_to([P, HEADS, CMP_PAD]), ALU.mult).then_inc(cmp_x, 1)
                dve.wait_ge(cmp_x, tb + 1)

            def attend(layer):
                mine = [u for u, key in enumerate(att) if key[0] == layer]

                def biased(u):
                    _, kind, pair, tb, h = att[u]
                    w = width(u)
                    if u >= 3:
                        dve.wait_ge(at_t, u - 2)
                    for seg in range(2):
                        dve.wait_ge(at_l, 2 * u + seg + 1)
                        dst, src = logit[u % 3][:, seg, 0:w], bank[2 * (u % 2) + seg][:, 0:w]
                        if kind == "mem":
                            last = ts(dst, src, SCALE, None, ALU.mult)
                        else:
                            head = h if kind == "nsa" else h + seg
                            last = stt(dst, src, SCALE, btab[:, head, T - w:T], ALU.mult, ALU.add)
                        last.then_inc(at_m, 1)
                    dve.wait_ge(at_m, 2 * u + 2)
                    dve.tensor_reduce(sm(540 + 8 * (u % 3), 2), logit[u % 3][:, :, 0:w], axis=AX.X, op=ALU.max,
                                      negate=True).then_inc(at_x, 1)

                def row_scale(u):
                    _, kind, pair, tb, h = att[u]
                    dve.wait_ge(at_e, u + 1)
                    r = sm(544 + 8 * (u % 3), 2)
                    ins = dve.reciprocal(r, sm(542 + 8 * (u % 3), 2))
                    if kind == "nsa":
                        step(ins)
                        ins = tt(r, r, sm(260 + 36 * tb + 3 * h + 1, 2), ALU.mult)
                    ins.then_inc(at_r, 1)

                def outputs(u):
                    g, _ = group_of(u)
                    if groups[g][-1] != u:
                        return
                    _, kind, pair, _, _ = att[u]
                    dve.wait_ge(at_o, u + 1)
                    k = (PAIRS if kind == "mem" else 0) + pair
                    dve.tensor_copy(mixT[:, k, :], bank[6 + g % 2][:, 0:T]).then_inc(at_oc, 1)

                n = len(mine)
                for i in range(n + 4):
                    if i < n:
                        biased(mine[i])
                    if 1 <= i < n + 1:
                        row_scale(mine[i - 1])
                    if i >= 4:
                        outputs(mine[i - 4])

            def layer_norm(k):
                last = None
                for tb in range(TB):
                    for n in range(2):
                        last = dve.bn_stats(sm(604 + 12 * tb + 6 * n, 6), X[:, tb, n * HALF:(n + 1) * HALF])
                step(last)
                for tb in range(TB):
                    last = dve.bn_aggr(sm(628 + 2 * tb, 2), sm(604 + 12 * tb, 12).rearrange("p (a s) -> p a s", s=6))
                step(last)
                ts(sm(600, 2), sm(628, 4).rearrange("p (b s) -> p b s", s=2)[:, :, 1], LN_EPS, None, ALU.add).then_inc(stat_ready, 1)
                dve.wait_ge(sq_ready, 8 + k)
                step(dve.reciprocal(sm(600, 2), sm(600, 2)))
                dve.wait_ge(rowvec_in, 16 * (3 + 2 * k))
                for tb in range(TB):
                    v = X[:, tb, :]
                    step(ts(v, v, sm(628 + 2 * tb, 1), sm(600 + tb, 1), ALU.subtract, ALU.mult))
                    step(tt(v, v, rowvec[:, 0, :], ALU.mult))
                    tt(v, v, rowvec[:, 1, :], ALU.add).then_inc(ln_done, 1)

            def ffn(layer):
                name = f"ffn{layer}"
                ph = phase_sems[name]
                at_w = PACK_ROWS + layer * CONV_ROWS

                def conv_step(j, k):
                    tap = lambda t, q: cols[:, bass.ds(k * 8 + (at_w + t * FFT + 2 * j + q), 1)]
                    for q in range(2):
                        w, a = work[(2 * j + q) % 4], bank[2 * (j % 2) + q]
                        dve.wait_ge(ph["act"], k * 8 + (2 * j + q + 1))
                        stt(w[:, 1:T], a[:, 0:T - 1], tap(1, q), w[:, 1:T], ALU.mult, ALU.add).then_inc(conv1[name], 1)
                        dve.wait_ge(conv1[name], k * 8 + (2 * j + q + 1))
                        stt(w[:, 2:T], a[:, 0:T - 2], tap(0, q), w[:, 2:T], ALU.mult, ALU.add).then_inc(mulp[name], 1)
                    for q in range(2):
                        dve.wait_ge(act2[name], k * 8 + (2 * j + q + 1))
                        if j >= 1:
                            dve.wait_ge(ph["used"], k * 4 + max(j - 1, 1))
                        tt(hb[j % 2][:, q, :], work[(2 * j + q) % 4], bank[2 * (j % 2) + q][:, T:2 * T], ALU.mult).then_inc(ph["hidden"], 1)

                conv_step(0, 0)
                with dve.Fori(0, 2) as i:
                    for u in range(4):
                        conv_step(u + 1, i)
                for j in (9, 10):
                    conv_step(j, 0)
                step(add_y(name, STEPS_F, ALPHA))

            attend(0)
            add_rows("a_out", ALPHA)
            layer_norm(0)
            ffn(0)
            layer_norm(1)
            attend(1)
            add_rows("b_out", ALPHA)
            layer_norm(2)
            ffn(1)
            layer_norm(3)

        @block.gpsimd
        def _(pool):
            step = chained(pool, pool_chain)

            pool.memset(small[:, :], 1.0).then_inc(pool_const, 1)
            step(pool.memset(ident[:, :], 0.0))
            pool.affine_select(out=ident[:, :], in_=ident[:, :], compare_op=ALU.not_equal, fill=1.0, base=0,
                               pattern=[[-1, P]], channel_multiplier=1).then_inc(pool_const, 1)
            pool.memset(ones[:, :], 1.0).then_inc(pool_const, 1)
            pool.memset(zeros[:, :], 0.0).then_inc(zero_ready, 1)
            pool.wait_ge(pool_const, 3)
            pool.iota(iota_i[:, :], pattern=[[1, 32]], base=0, channel_multiplier=0).then_inc(iota_done, 1)
            pool.wait_ge(iota_done, 1)
            step(pool.tensor_copy(sm(850, 32), iota_i[:, :]))
            for level in range(7):
                half = P >> (level + 1)
                nb = P // (2 * half)
                v = level_maskf[:, :].rearrange("p (b r) -> p b r", b=nb)
                step(pool.memset(level_maskf[:, :], 1.0))
                for base, pattern, mult in ((0, [[-2 * half, nb], [0, 2 * half]], 1),
                                            (half - 1, [[2 * half, nb], [0, 2 * half]], -1),
                                            (-half, [[0, nb], [1, 2 * half]], 0)):
                    step(pool.affine_select(out=v, in_=v, compare_op=ALU.is_ge, fill=0.0, base=base,
                                            pattern=pattern, channel_multiplier=mult))
                step(pool.tensor_copy(level_mask[:, level, :], level_maskf[:, :]))
            step(pool.tensor_copy(level_mask[:, 7, :], ident[:, :]))
            wait_emptied(pool, "pack")
            pool.memset(score[:, :, :], 0.0).then_inc(mask_ready, 1)

            wait_emptied(pool, "dist", 1)
            pool.dma_start(by_dist, dist_out).then_inc(dist_stored, 16)
            pool.wait_ge(dist_stored, 16)
            row = DIST_REV + DIST_FWD
            pool.dma_start(by_token, bass.AP(tensor=by_dist.tensor, offset=P - 1,
                                             ap=[[row, HEADS], [-1, P], [1, T]])).then_inc(expanded, 16)
            pool.dma_start(by_block, bass.AP(tensor=by_dist.tensor, offset=DIST_REV + FWD_ZERO - (CMP_LEN - 1),
                                             ap=[[row, HEADS], [-CMP_STRIDE, CMP_PAD], [1, T]])).then_inc(expanded, 16)
            pool.wait_ge(job_done, jobs.number("aT", KT - 1) + 1)
            step(pool.memset(sbmask[:, :, :], 0.0))
            for tb in range(TB):
                v = sbmask[:, tb, META:S1]
                pool.affine_select(out=v, in_=v, compare_op=ALU.is_ge, fill=NEG, base=tb * P - 1,
                                   pattern=[[-1, T]], channel_multiplier=1).then_inc(mask_ready, 1)

            pool.wait_ge(job_done, jobs.number("mT", 3) + 1)
            pool.wait_ge(rows_ready, 2)
            pool.wait_ge(expanded, 32)
            pool.dma_start(btab[:, :, :], by_token.rearrange("h p j -> p h j")).then_inc(tables_in, 16)
            blocks_flat = by_block.rearrange("h n t -> (h n) t")
            pool.dma_start(ctmp[:, 0, :], blocks_flat[0:P, :]).then_inc(tables_in, 16)
            pool.dma_start(ctmp[0:64, 1, :], blocks_flat[P:P + 64, :]).then_inc(tables_in, 16)

            def load_rowvec(*vectors):
                for i, v in enumerate(vectors):
                    src = bass.AP(tensor=v.tensor, offset=v.offset, ap=[[0, P], [1, D]])
                    pool.dma_start(rowvec[:, i, :], src).then_inc(rowvec_in, 16)

            load_rowvec(g_final)

            wait_emptied(pool, "gT")
            pool.dma_start(gates_dram, work[0][0:EXPERTS, :]).then_inc(gT_stored, 16)
            pool.wait_ge(gT_stored, 16)
            pool.wait_ge(job_done, jobs.number("cbT") + 1)
            for c in range(4):
                src = bass.AP(tensor=gates_dram.tensor, offset=c * 8 * T, ap=[[0, P], [1, 8 * T]])
                pool.dma_start(gb[:, 8 * c:8 * c + 8, :].rearrange("p a b -> p (a b)"), src).then_inc(gb_in, 16)
            pool.wait_ge(phase_sems["moe"]["hidden"], 2 * STEPS_M)
            for t in (pc, vz, hidT):
                pool.memset(t[:, :, :], 0.0)
            pool.memset(kz[:, :, :], 0.0).then_inc(pool_step, 1)
            pool.wait_ge(ln_done, 1)
            load_rowvec(ln1_g_2[0], ln1_b_2[0])

            def attend(layer):
                for u in [u for u, key in enumerate(att) if key[0] == layer]:
                    pool.wait_ge(at_r, u + 1)
                    w = width(u)
                    v = logit[u % 3][:, :, 0:w]
                    pool.tensor_tensor(v, v, sm(544 + 8 * (u % 3), 2).unsqueeze(2).broadcast_to([P, 2, w]), ALU.mult).then_inc(at_p, 1)

            attend(0)
            pool.wait_ge(ln_done, 3)
            load_rowvec(ln2_g_2[0], ln2_b_2[0])
            pool.wait_ge(ln_done, 5)
            load_rowvec(ln1_g_2[1], ln1_b_2[1])
            attend(1)
            pool.wait_ge(ln_done, 7)
            load_rowvec(ln2_g_2[1], ln2_b_2[1])
    return nc


_INS = ("x", "meta_tokens", "lb_logits", "g_mix", "w_in", "sb_gain", "hg_gain", "w_out", "g_ffn", "w_router_group",
        "b_router_group", "w_router_expert", "b_router_expert", "w_expert_gate", "w_expert_up", "w_expert_down",
        "g_final", "mem_2", "rel_bias_2", "a_w_in_2", "a_cmp_pe_k_2", "a_cmp_w1_k_2", "a_cmp_w2_k_2", "a_cmp_pe_v_2",
        "a_cmp_w1_v_2", "a_cmp_w2_v_2", "a_w_mem_kv_2", "a_w_out_2", "shared_w_kv_2", "b_w_in_2", "b_w_mem_kv_2",
        "b_w_out_2", "ln1_g_2", "ln1_b_2", "ln2_g_2", "ln2_b_2", "ffn_w_in_2", "ffn_conv_w_2", "ffn_conv_b_2",
        "ffn_w_out_2")


def kernel(**inputs):
    import numpy as _np
    import concourse.bacc as _bacc
    from concourse import mybir as _mybir
    from concourse.bass_utils import run_bass_kernel_spmd as _run

    nc = _bacc.Bacc("TRN2", target_bir_lowering=False, num_devices=1)
    arrays, args = {}, {}
    for name in _INS + ("dist_onehot",):
        a = bucket_table() if name == "dist_onehot" else _np.ascontiguousarray(inputs[name])
        arrays[f"in_{name}"] = a
        args[name] = nc.dram_tensor(f"in_{name}", a.shape, _mybir.dt.from_np(a.dtype), kind="ExternalInput").ap()
    args["out"] = nc.dram_tensor("out_0", (1, T, D), F32, kind="ExternalOutput").ap()
    build(nc, **args)
    r = _run(nc, [arrays], core_ids=[0])
    return r.results[0]["out_0"]
```

```python
from contextlib import ExitStack

import concourse.bass as bass
import numpy as np
from concourse import mybir

F32 = mybir.dt.float32
BF16 = mybir.dt.bfloat16
U8 = mybir.dt.uint8
U32 = mybir.dt.uint32
I32 = mybir.dt.int32
ALU = mybir.AluOpType
ACT = mybir.ActivationFunctionType
AX = mybir.AxisListType

P = 128
T = 256
TB = T // P
D = 1024
KT = D // P
META = 16
S1 = META + T
UNIT = 4096
RING = 6
HALF = 512

SB_HEADS, SB_D = 8, 64
HG_HEADS = 4
GROUPS, PER_GROUP = 4, 8
EXPERTS = GROUPS * PER_GROUP
FF_E = 512

HEADS, HD = 12, 64
PAIRS = HEADS // 2
MEM = 256
MEM_PAIRS = 2
SCALE = HD ** -0.5
CMP_LEN, CMP_STRIDE, CMP_HID = 32, 16, 256
N_CMP = (T - CMP_LEN) // CMP_STRIDE + 1
CMP_PAD = 16
BUCKETS, MAX_DIST = 32, 128
D_FF = 2816
FFT = D_FF // P
STEPS_F = FFT // 2
SLOTS = 64
PASSES = T // SLOTS
ALPHA = 4.0 ** 0.25
EPS, LN_EPS = 1e-6, 1e-5
NEG = -1e30
TINY = 1e-30
ARENA = 13700

DIST_REV = 384
DIST_FWD = 512
FWD_ZERO = (CMP_PAD - 1) * CMP_STRIDE + CMP_LEN - 1

PACK = {"g_mix": (0, 8), "g_ffn": (8, 8), "lb": (16, 8), "sb_gain": (24, 4), "hg_gain": (28, 4),
        "pe_k": (32, 16), "pe_v": (48, 16), "conv_b": (64, 44)}
PACK_ROWS = 108
CONV_ROWS = 3 * FFT


def bucket_table():
    def rows(dist):
        n = np.maximum(dist, 0)
        half = BUCKETS // 2
        nf = np.maximum(n, 1).astype(np.float32)
        large = half + (np.log(nf / half) / np.float32(np.log(MAX_DIST / half)) * (BUCKETS - half)).astype(np.int32)
        bucket = np.where(n < half, n, np.minimum(large, BUCKETS - 1))
        out = np.zeros((BUCKETS + 1, len(dist)), np.float32)
        out[bucket, np.arange(len(dist))] = dist >= 0
        out[BUCKETS] = dist < 0
        return out
    return np.concatenate([rows(T - 1 - np.arange(DIST_REV)), rows(np.arange(DIST_FWD) - FWD_ZERO)], 1)


def ring_units():
    order = [("mem_kv_a", 0), ("mem_kv_b", 0)]
    order += [("w_in", c) for c in (4, 3, 5, 6, 0, 1, 2)]
    order += [("w_out", c) for c in range(2)]
    first = {"moe": len(order)}
    order += [(w, e) for e in range(EXPERTS) for w in ("gate", "up", "down")]
    order += [("a_in", c) for c in range(3)] + [("cmp_k", 0), ("cmp_v", 0)]
    order += [("a_out", c) for c in range(2)]

    def ffn(layer):
        first[f"ffn{layer}"] = len(order)
        for j in range(0, STEPS_F - 1, 2):
            order.extend([(f"ffn_in{layer}", j), (f"ffn_in{layer}", j + 1), (f"ffn_out{layer}", j // 2)])
        order.extend([(f"ffn_in{layer}", STEPS_F - 1), (f"ffn_out{layer}", STEPS_F // 2)])

    ffn(0)
    order += [("kv", c) for c in range(3)] + [("b_in", c) for c in range(2)] + [("b_out", c) for c in range(2)]
    ffn(1)
    return order, first


class Jobs:

    def __init__(self, banks):
        self.jobs, self.at, self.banks = [], {}, banks

    def add(self, name, engine, n):
        self.at[name] = len(self.jobs)
        self.jobs += [engine] * n

    def number(self, name, i=0):
        return self.at[name] + i

    def bank(self, name, i=0):
        return self.number(name, i) % self.banks

    def emptied(self, number):
        e = self.jobs[number]
        return e, self.jobs[:number + 1].count(e)


def plan_jobs():
    j = Jobs(4)
    j.add("pack", "A", 1)
    j.add("memT", "A", 4)
    j.add("mem_a", "A", 2)
    j.add("mem_b", "A", 2)
    j.add("dist", "A", 2)
    j.add("aT", "V", KT)
    j.add("hgf", "A", 4)
    j.add("hgq", "A", 2)
    j.add("hgi", "A", 3)
    j.add("hgg", "A", 2)
    j.add("sbq", "A", 2)
    j.add("sbk", "A", 4)
    j.add("sbv", "A", 3)
    j.add("kmT", "A", 1)
    j.add("s0", "A", 1)
    j.add("k1T", "A", 1)
    j.add("s1", "V", 1)
    for level in range(8):
        j.add(f"level{level}", "V", 2)
    for i in range(16 + 2):
        if i < 16:
            j.add(f"z{i}", "V", 1)
        if i >= 2:
            j.add(f"wT{i - 2}", "A", 1)
    j.add("ohg", "V", 2)
    j.add("mT", "A", 4)
    j.add("w_out", "V", 4)
    j.add("x2T", "A", 4)
    j.add("router", "V", 1)
    j.add("pos", "V", 1)
    j.add("cbT", "V", 1)
    j.add("xTa", "A", 4)
    j.add("a_q", "A", 3)
    j.add("a_kv", "A", 3)
    j.add("a_v", "A", 1)
    j.add("a_qm", "A", 1)
    j.add("cmp_h", "A", 2)
    j.add("cmp_kv", "A", 1)
    j.add("cmp_l", "V", 2)
    j.add("cmp_pT", "A", 2)
    j.add("a_out", "V", 4)
    j.add("xTf0", "A", 4)
    j.add("xTb", "A", 4)
    j.add("b_k", "A", 3)
    j.add("b_v", "A", 4)
    j.add("b_q", "A", 3)
    j.add("b_qm", "A", 1)
    j.add("b_out", "V", 4)
    j.add("xTf1", "A", 4)
    return j


def attention_units():
    units = []
    for layer in range(2):
        for pair in range(PAIRS):
            for tb in range(TB):
                if layer == 0:
                    units += [(layer, "nsa", pair, tb, 2 * pair + r) for r in range(2)]
                else:
                    units.append((layer, "moba", pair, tb, 2 * pair))
        for pair in range(MEM_PAIRS):
            units += [(layer, "mem", pair, tb, 2 * pair) for tb in range(TB)]
    return units


def build(nc, x, meta_tokens, lb_logits, g_mix, w_in, sb_gain, hg_gain, w_out, g_ffn, w_router_group,
          b_router_group, w_router_expert, b_router_expert, w_expert_gate, w_expert_up, w_expert_down,
          g_final, mem_2, rel_bias_2, a_w_in_2, a_cmp_pe_k_2, a_cmp_w1_k_2, a_cmp_w2_k_2, a_cmp_pe_v_2,
          a_cmp_w1_v_2, a_cmp_w2_v_2, a_w_mem_kv_2, a_w_out_2, shared_w_kv_2, b_w_in_2, b_w_mem_kv_2,
          b_w_out_2, ln1_g_2, ln1_b_2, ln2_g_2, ln2_b_2, ffn_w_in_2, ffn_conv_w_2, ffn_conv_b_2,
          ffn_w_out_2, dist_onehot, out):
    units, first_unit = ring_units()
    jobs = plan_jobs()
    att = attention_units()
    n_att0 = sum(u[0] == 0 for u in att)

    with ExitStack() as ctx:
        def sb(name, shape, dt=F32):
            return ctx.enter_context(nc.sbuf_tensor(name, shape, dt))

        def sem(name):
            return ctx.enter_context(nc.semaphore(name))

        bank = [ctx.enter_context(nc.psum_tensor(f"bank{i}", [P, HALF], F32)) for i in range(8)]

        ring = sb("ring", [P, RING, UNIT])
        X = sb("X", [P, TB, D])
        R = sb("R", [P, TB, D])
        XT = sb("XT", [P, KT, S1])
        rowvec = sb("rowvec", [P, 2, D])
        km = [sb(f"km{i}", [P, 2, MEM]) for i in range(2)]
        vm = [sb(f"vm{i}", [P, 2, MEM]) for i in range(2)]
        ident = sb("ident", [P, P])
        ones = sb("ones", [P, S1])
        zeros = sb("zeros", [P, HALF], BF16)
        level_mask = sb("level_mask", [P, 8, P], U8)
        level_maskf = sb("level_maskf", [P, P])
        cols = sb("cols", [P, PACK_ROWS + 2 * CONV_ROWS])
        small = sb("small", [P, 964])
        tri = sb("tri", [P, P])
        extra = sb("extra", [P, 1], I32)
        iota_i = sb("iota_i", [P, SLOTS], mybir.dt.int32)
        bias36 = sb("bias36", [P, 36])
        w_router = sb("w_router", [P, KT, 36])
        w2 = sb("w2", [P, 2, 2, HD])
        arena = sb("arena", [P, ARENA])

        def view(at, n, *dims):
            v = arena[:, at:at + n]
            if len(dims) == 2:
                return v.rearrange("p (a b) -> p a b", b=dims[1])
            if len(dims) == 3:
                return v.rearrange("p (a b c) -> p a b c", b=dims[1], c=dims[2])
            return v

        used = [0]

        def take(n, *dims):
            used[0] += n
            assert used[0] <= ARENA, used
            return view(used[0] - n, n, *dims)

        hgk = take(4 * S1, 4, S1)
        logf = take(4 * S1, 4, S1)
        hgq = take(4 * T, 4, T)
        bcum = take(4 * T, 4, T)
        bmeta = take(64, 4, META)
        fmeta = take(64, 4, META)
        at_lev = used[0]
        lev = [take(4 * T, 4, T) for _ in range(2)]
        at_score = used[0]
        score = take(8 * P, 8, P)
        at_hgi = used[0]
        hgi = take(3 * HALF, 3, HALF)
        hgg = take(2 * HALF, 2, HALF)
        S0 = take(HALF)
        S1t = take(HALF)
        sbk = take(4 * S1, 4, S1)
        at_beta = used[0]
        beta = [take(S1) for _ in range(2)]
        keep = [take(S1 + 1) for _ in range(2)]
        meta = arena[0:META, at_beta:at_beta + D]
        pack = view(at_score, 3 * P, 3, P)
        junk = view(at_lev, D)
        zm = [view(at_lev + 4 * T + i * S1, S1) for i in range(2)]
        rflat = R[:, :, :].rearrange("p a b -> p (a b)")
        sbq = rflat[:, 0:4 * T].rearrange("p (a b) -> p a b", b=T)
        sbmask = rflat[:, 4 * T:4 * T + 2 * S1].rearrange("p (a b) -> p a b", b=S1)
        wTs = [view(at_lev + 4 * T + 2 * S1, 3 * P), rflat[:, 4 * T + 2 * S1:4 * T + 2 * S1 + 3 * P]]
        vflat = rowvec[:, :, :].rearrange("p a b -> p (a b)")
        sbv = vflat[:, 0:3 * HALF].rearrange("p (a b) -> p a b", b=HALF)
        kT_rows = vflat[:, 3 * HALF:4 * HALF]
        dist_sb = arena[0:BUCKETS + 1, at_hgi:at_hgi + DIST_REV + DIST_FWD]
        dist_rel = arena[0:BUCKETS + 1, at_hgi + 900:at_hgi + 900 + HEADS]
        dist_out = arena[0:HEADS, at_hgi + 1000:at_hgi + 1000 + DIST_REV + DIST_FWD]

        used[0] = 0
        btab = take(HEADS * T, HEADS, T)
        cbias = take(2 * HEADS * CMP_PAD, 2, HEADS * CMP_PAD)
        at_hb = used[0]
        hb = [take(2 * T, 2, T) for _ in range(2)]
        work = [take(T) for _ in range(4)]
        ctmp = view(at_hb, 2 * T, 2, T)
        late = used[0]
        used[0] = at_hb + 2 * T
        pick = take(TB * EXPERTS * SLOTS, TB, EXPERTS * SLOTS)
        xg = take(2 * KT * SLOTS, 2, KT * SLOTS)
        gact = [take(256) for _ in range(2)]
        hid = [take(256) for _ in range(2)]
        turned_sb = [take(HALF) for _ in range(2)]
        hidden_T = [v[:, 0:256] for v in turned_sb]
        give = [v[:, 256:HALF] for v in turned_sb]
        gated = take(TB * 4 * SLOTS, TB, 4 * SLOTS)
        yrow = [take(HALF) for _ in range(2)]
        used[0] = late
        qT = take(6 * T, 6, T)
        qmT = take(2 * T, 2, T)
        at_k = used[0]
        kT = take(6 * T, 6, T)
        at_v = used[0]
        vrow = take(2 * 768, 2, 768)
        logit = [take(2 * T, 2, T) for _ in range(3)]
        at_pT = used[0]
        pT = [take(4 * P) for _ in range(2)]
        vrow0 = view(at_v, 2 * P, 2, P)
        pcT = view(at_v + 2 * P, 3 * T, 3, T)
        vz = view(at_v + 2 * P + 3 * T, 4 * HD, 4, HD)
        pc = view(at_k + 2 * T, 2 * HEADS * 32, 2, HEADS * 32)
        hidT = view(at_k + 2 * T + 768, 4 * 32, 4, 32)
        kz = view(at_k + 2 * T + 896, 2 * CMP_PAD, 2, CMP_PAD)
        shift2 = view(at_pT, 2 * T, 2, T)
        mixT = XT[:, :, 0:T]
        memT = XT[:, :, 0:MEM]

        by_dist = nc.dram_tensor("by_dist", [HEADS, DIST_REV + DIST_FWD], F32).ap()
        by_token = nc.dram_tensor("by_token", [HEADS, P, T], F32).ap()
        by_block = nc.dram_tensor("by_block", [HEADS, CMP_PAD, T], F32).ap()
        expanded = sem("expanded")

        landed = [sem(f"landed{i}") for i in range(RING)]
        in_x, in_mem, in_small, in_dist = sem("in_x"), sem("in_mem"), sem("in_small"), sem("in_dist")
        in_pack = sem("in_pack")
        pool_const = sem("pool_const")
        pool_step, pool_chain, iota_done = sem("pool_step"), sem("pool_chain"), sem("iota_done")
        dve_step, act_step = sem("dve_step"), sem("act_step")
        job_done = sem("job_done")
        emptied_a, emptied_v = sem("emptied_a"), sem("emptied_v")
        dist_ready, dist_stored, tables_in = sem("dist_ready"), sem("dist_stored"), sem("tables_in")
        rows_ready = sem("rows_ready")
        sq_ready = sem("sq_ready")
        stat_ready = sem("stat_ready")
        lbound_ready = sem("lbound_ready")
        hg_sig, hg_f, hg_log, hg_q = sem("hg_sig"), sem("hg_f"), sem("hg_log"), sem("hg_q")
        hg_arg, hg_exp, hg_fac = sem("hg_arg"), sem("hg_exp"), sem("hg_fac")
        z_ready, sig_ready, w_ready, wT_ready, sb_out = (sem("z_ready"), sem("sig_ready"), sem("w_ready"),
                                                        sem("wT_ready"), sem("sb_out"))
        wT_used = sem("wT_used")
        router_arg, router_exp = sem("router_arg"), sem("router_exp")
        moe = {k: sem(f"moe_{k}") for k in ("picks", "gathered", "taken", "gate", "up", "silu", "hidden", "turned",
                                            "turned_copied", "down", "row", "extra_known", "gated", "combined")}
        ov = {k: sem(f"over_{k}") for k in ("picks", "loaded", "gathered", "taken", "up", "silu", "hidden", "turned",
                                            "turned_copied", "down", "row", "gated", "done")}
        ov_places, ov_through = sem("over_places"), sem("over_through")
        sums_ready = sem("sums_ready")
        phase_sems = {}
        for ph in ("ffn0", "ffn1"):
            phase_sems[ph] = {k: sem(f"{ph}_{k}") for k in ("tile", "act", "hidden", "used")}
        act2 = {ph: sem(f"{ph}_gelu") for ph in ("ffn0", "ffn1")}
        mulp = {ph: sem(f"{ph}_mul") for ph in ("ffn0", "ffn1")}
        rowvec_in = sem("rowvec_in")
        ln_done = sem("ln_done")
        mask_ready = sem("mask_ready")
        conv1 = {ph: sem(f"{ph}_conv1") for ph in ("ffn0", "ffn1")}
        y_used = sem("y_used")
        gate_ready = sem("gate_ready")
        cmp_in, cmp_x, cmp_e = sem("cmp_in"), sem("cmp_x"), sem("cmp_e")
        at_l, at_m, at_x, at_e, at_r, at_p, at_t, at_tc, at_o, at_oc = (
            sem("at_logits"), sem("at_biased"), sem("at_max"), sem("at_exp"), sem("at_scale"), sem("at_probs"),
            sem("at_trans"), sem("at_transcopied"), sem("at_out"), sem("at_outcopied"))
        stored = sem("stored")
        zero_ready = sem("zero_ready")

        def weights(n):
            return ring[:, n % RING, :]

        w_at = {}
        for n, key in enumerate(units):
            w_at[key] = n

        def arrivals(n):
            return 32 if units[n][0][:-1] == "ffn_in" else 16

        def use_count(n):
            return sum(arrivals(m) for m in range(n % RING, n + 1, RING))

        emptied = {"A": emptied_a, "V": emptied_v}

        def to_fill(pe, name, i=0):
            n = jobs.number(name, i)
            if n >= jobs.banks:
                engine, count = jobs.emptied(n - jobs.banks)
                pe.wait_ge(emptied[engine], count)
            return bank[n % jobs.banks]

        def filled(engine, name, i=0):
            n = jobs.number(name, i)
            engine.wait_ge(job_done, n + 1)
            return bank[n % jobs.banks]

        def wait_emptied(engine, name, i=0):
            who, count = jobs.emptied(jobs.number(name, i))
            engine.wait_ge(emptied[who], count)

        def wait_weights(pe, key):
            n = w_at[key]
            pe.wait_ge(landed[n % RING], use_count(n))
            return ring[:, n % RING, :]

        def chained(engine, semaphore):
            count = [0]

            def step(instruction):
                count[0] += 1
                instruction.then_inc(semaphore, 1)
                engine.wait_ge(semaphore, count[0])
            return step

        def width(u):
            _, kind, _, tb, _ = att[u]
            return MEM if kind == "mem" else P * (tb + 1)

        groups = []
        for u, key in enumerate(att):
            if not groups or att[groups[-1][-1]][:3] != key[:3]:
                groups.append([])
            groups[-1].append(u)

        def group_of(u):
            g = next(g for g, members in enumerate(groups) if u in members)
            return g, groups[g][0] == u

        def sm(at, n):
            return small[:, at:at + n]

        def pair_pick(tb, i):
            return pick[:, tb, bass.ds(i * (2 * SLOTS), 2 * SLOTS)]

        def xg_tile(r, k):
            return xg[:, r, k * SLOTS:(k + 1) * SLOTS]

        block = ctx.enter_context(nc.Block())

        @block.sync
        def _(sp):
            kmaj = lambda w: w.rearrange("(k p) n -> p k n", p=P)
            simple = {
                "mem_kv_a": lambda c: kmaj(a_w_mem_kv_2[0]),
                "mem_kv_b": lambda c: kmaj(b_w_mem_kv_2[0]),
                "w_in": lambda c: kmaj(w_in[0, :, c * HALF:(c + 1) * HALF]),
                "w_out": lambda c: kmaj(w_out[0, :, c * HALF:(c + 1) * HALF]),
                "a_in": lambda c: kmaj(a_w_in_2[0, :, c * HALF:min((c + 1) * HALF, 1444)]),
                "cmp_k": lambda c: kmaj(a_cmp_w1_k_2[0]),
                "cmp_v": lambda c: kmaj(a_cmp_w1_v_2[0]),
                "a_out": lambda c: kmaj(a_w_out_2[0, :, c * HALF:(c + 1) * HALF]),
                "kv": lambda c: kmaj(shared_w_kv_2[:, c * HALF:(c + 1) * HALF]),
                "b_in": lambda c: kmaj(b_w_in_2[0, :, c * HALF:(c + 1) * HALF]),
                "b_out": lambda c: kmaj(b_w_out_2[0, :, c * HALF:(c + 1) * HALF]),
            }

            def slot(n, a, b):
                return ring[:, n % RING, 0:a * b].rearrange("p (a b) -> p a b", b=b)

            last_job = {("mem_kv_a", 0): ("mem_a", 1), ("mem_kv_b", 0): ("mem_b", 1),
                        ("cmp_k", 0): ("cmp_h", 0), ("cmp_v", 0): ("cmp_h", 1)}
            for c, job in ((4, ("hgf", 3)), (3, ("hgq", 1)), (5, ("hgi", 2)), (6, ("hgg", 1)), (0, ("sbq", 1)),
                           (1, ("sbk", 3)), (2, ("sbv", 2))):
                last_job["w_in", c] = job
            for c, job in ((0, ("a_q", 1)), (1, ("a_v", 0)), (2, ("a_qm", 0))):
                last_job["a_in", c] = job
            for c, job in ((0, ("b_k", 1)), (1, ("b_v", 1)), (2, ("b_v", 3))):
                last_job["kv", c] = job
            for c, job in ((0, ("b_q", 1)), (1, ("b_qm", 0))):
                last_job["b_in", c] = job
            for c in range(2):
                for w in ("w_out", "a_out", "b_out"):
                    last_job[w, c] = (w, 2 * c + 1)

            def wait_read(n):
                what, c = units[n]
                if (what, c) in last_job:
                    sp.wait_ge(job_done, jobs.number(*last_job[what, c]) + 1)
                elif what in experts:
                    sp.wait_ge(moe[what], c + 1)
                elif what[:-1] == "ffn_in":
                    sp.wait_ge(phase_sems["ffn" + what[-1]]["tile"], 2 * c + 2)
                else:
                    sp.wait_ge(phase_sems["ffn" + what[-1]]["used"], min(2 * c + 2, STEPS_F))

            def load(n):
                what, c = units[n]
                if n >= RING:
                    wait_read(n - RING)
                if what[:-1] == "ffn_in":
                    w = ffn_w_in_2[int(what[-1])].rearrange("(k p) (h n) -> p k h n", p=P, h=2)
                    dst = ring[:, n % RING, :].rearrange("p (k h n) -> p k h n", h=2, n=256)
                    for h in range(2):
                        sp.dma_start(dst[:, :, h, :], w[:, :, h, c * 256:(c + 1) * 256]).then_inc(landed[n % RING], 16)
                    return
                elif what[:-1] == "ffn_out":
                    rows = slice(c * 4 * P, min((c + 1) * 4 * P, D_FF))
                    src = kmaj(ffn_w_out_2[int(what[-1]), rows, :])
                    dst = slot(n, src.shape[1], src.shape[2])
                elif what in experts:
                    src = kmaj(experts[what][0, c])
                    dst = slot(n, src.shape[1], src.shape[2])
                else:
                    src = simple[what](c)
                    dst = slot(n, src.shape[1], src.shape[2])
                sp.dma_start(dst, src).then_inc(landed[n % RING], 16)

            experts = {"gate": w_expert_gate, "up": w_expert_up, "down": w_expert_down}

            sp.dma_start(X[:, :, :], x[0].rearrange("(b p) d -> p b d", p=P)).then_inc(in_x, 16)
            sp.dma_start(meta[:, :], meta_tokens).then_inc(in_x, 16)
            sp.dma_start(R[:, :, :], mem_2[0].rearrange("(b p) d -> p b d", p=P)).then_inc(in_mem, 16)
            load(0)
            packed = [(g_mix, "l (t p) -> (l t) p", "g_mix"), (g_ffn, "l (t p) -> (l t) p", "g_ffn"),
                      (lb_logits, "l (t p) -> (l t) p", "lb"), (sb_gain, "l (t p) -> (l t) p", "sb_gain"),
                      (hg_gain, "l (t p) -> (l t) p", "hg_gain"), (ffn_conv_b_2, "l (t p) -> (l t) p", "conv_b")]
            for v, how, name in packed:
                at, n = PACK[name]
                sp.dma_start(pack[at:at + n, 0, :], v.rearrange(how, p=P)).then_inc(in_pack, 16)
            for v, name in ((a_cmp_pe_k_2, "pe_k"), (a_cmp_pe_v_2, "pe_v")):
                at, n = PACK[name]
                sp.dma_start(pack[at:at + n, 0, :], v[0].rearrange("(j l) d -> j (l d)", l=2)).then_inc(in_pack, 16)
            for layer in range(2):
                sp.dma_start(pack[0:CONV_ROWS, 1 + layer, :],
                             ffn_conv_w_2[layer].rearrange("k (t p) -> (k t) p", p=P)).then_inc(in_pack, 16)
            sp.dma_start(dist_sb, dist_onehot).then_inc(in_dist, 16)
            sp.dma_start(dist_rel[0:BUCKETS, :], rel_bias_2).then_inc(in_dist, 16)
            load(1)
            load(2)
            sp.dma_start(w_router[:, :, 0:GROUPS], kmaj(w_router_group[0])).then_inc(in_small, 16)
            sp.dma_start(w_router[:, :, GROUPS:36], kmaj(w_router_expert[0])).then_inc(in_small, 16)
            for v, at, n in ((b_router_group, 0, GROUPS), (b_router_expert, GROUPS, EXPERTS)):
                sp.dma_start(bias36[:, at:at + n], bass.AP(tensor=v.tensor, offset=v.offset, ap=[[0, P], [1, n]])).then_inc(in_small, 16)
            for kv, v in enumerate((a_cmp_w2_k_2, a_cmp_w2_v_2)):
                sp.dma_start(w2[:, kv, :, :], kmaj(v[0])).then_inc(in_small, 16)
            for n in range(3, first_unit["moe"]):
                load(n)

            base = first_unit["moe"]
            for n in range(base, base + 6):
                load(n)
            with sp.Fori(1, EXPERTS // 2) as i:
                for u in range(6):
                    n = base + u
                    w = (w_expert_gate, w_expert_up, w_expert_down)[u % 3]
                    rows = w.shape[2]
                    src = w[0].rearrange("e k n -> (e k) n")[bass.ds(i * (2 * rows) + (u // 3) * rows, rows), :]
                    sp.wait_ge(moe[("gate", "up", "down")[u % 3]], i * 2 + (u // 3 - 1))
                    src = kmaj(src)
                    sp.dma_start(slot(n, src.shape[1], src.shape[2]), src).then_inc(landed[n % RING], 16)
            sp.wait_ge(moe["extra_known"], 1)
            more = sp.value_load(extra[0:1, 0:1], min_val=0, max_val=PASSES - 1)
            with sp.If(more > 0):
                for k in ("gate", "up", "down"):
                    sp.wait_ge(moe[k], EXPERTS)
                with sp.Fori(0, more) as p:
                    with sp.Fori(0, EXPERTS // 2) as i:
                        sp.wait_ge(ov["done"], p * EXPERTS + i * 2 + 1)
                        for u in range(6):
                            w = (w_expert_gate, w_expert_up, w_expert_down)[u % 3]
                            rows = w.shape[2]
                            src = kmaj(w[0].rearrange("e k n -> (e k) n")[bass.ds(i * (2 * rows) + (u // 3) * rows, rows), :])
                            sp.dma_start(slot(base + u, src.shape[1], src.shape[2]), src).then_inc(ov["loaded"], 16)
                sp.wait_ge(ov_through, 1)
            for n in range(base + 3 * EXPERTS, len(units)):
                load(n)
            for tb in range(TB):
                sp.wait_ge(ln_done, 8 + tb)
                sp.dma_start(out[0, tb * P:(tb + 1) * P, :], X[:, tb, :]).then_inc(stored, 16)
            sp.wait_ge(stored, 16 * TB)

        @block.tensor
        def _(pe):
            def transposes(name, i, pairs):
                out_bank = to_fill(pe, name, i)
                for (rows, at, n), src in pairs:
                    last = pe.transpose(out_bank[0:rows, at:at + n], src, ident[0:n, 0:n])
                last.then_inc(job_done, 1)

            def product(dst, pairs):
                for k, (lhsT, rhs) in enumerate(pairs):
                    last = pe.matmul(dst, lhsT, rhs, start=k == 0, stop=k == len(pairs) - 1)
                return last

            def to_cols(name, rows, tiles=KT):
                for j in range(tiles // 2):
                    transposes(name, j, [((P, r * T + tb * P, P), rows[:, tb, (2 * j + r) * P:(2 * j + r + 1) * P])
                                         for r in range(2) for tb in range(TB)])

            pe.wait_ge(pool_const, 3)
            pe.wait_ge(in_pack, 16 * 10)
            transposes("pack", 0, [((P, 0, PACK_ROWS), pack[0:PACK_ROWS, 0, :]),
                                   ((P, PACK_ROWS, CONV_ROWS), pack[0:CONV_ROWS, 1, :]),
                                   ((P, PACK_ROWS + CONV_ROWS, CONV_ROWS), pack[0:CONV_ROWS, 2, :])])
            pe.wait_ge(in_mem, 16)
            to_cols("memT", R)

            wait_emptied(pe, "memT", 3)
            for key, name in (("mem_kv_a", "mem_a"), ("mem_kv_b", "mem_b")):
                w = wait_weights(pe, (key, 0)).rearrange("p (k n) -> p k n", n=HALF)
                b = to_fill(pe, name, 0)
                for m in range(2):
                    last = product(b[:, m * MEM:(m + 1) * MEM], [(w[:, k, m * P:(m + 1) * P], memT[:, k, :]) for k in range(KT)])
                last.then_inc(job_done, 1)
                b = to_fill(pe, name, 1)
                for m in range(2):
                    last = product(b[:, m * MEM:(m + 1) * MEM], [(memT[:, k, m * P:(m + 1) * P], w[:, k, MEM:2 * MEM]) for k in range(KT)])
                last.then_inc(job_done, 1)

            pe.wait_ge(dist_ready, 1)
            pe.wait_ge(in_dist, 32)
            for i, (at, n) in enumerate(((0, DIST_REV), (DIST_REV, DIST_FWD))):
                b = to_fill(pe, "dist", i)
                pe.matmul(b[0:HEADS, 0:n], dist_rel, dist_sb[:, at:at + n], start=True, stop=True).then_inc(job_done, 1)

            pe.wait_ge(rows_ready, 1)
            wait_emptied(pe, "mem_b", 1)
            for k in range(KT):
                cut = slice(k * P, (k + 1) * P)
                transposes("aT", k, [((P, 0, META), meta[:, cut])] + [((P, META + tb * P, P), R[:, tb, cut]) for tb in range(TB)])
            for k in range(KT):
                wait_emptied(pe, "aT", k)

            def w_in_unit(c):
                return wait_weights(pe, ("w_in", c)).rearrange("p (k n) -> p k n", n=HALF)

            def cols_out(name, c, wide):
                w = w_in_unit(c)
                for m in range(4):
                    if wide:
                        b, at, src = to_fill(pe, name, m), 0, slice(0, S1)
                    else:
                        b, at, src = (to_fill(pe, name, m // 2) if m % 2 == 0 else b), (m % 2) * T, slice(META, S1)
                    n = src.stop - src.start
                    last = product(b[:, at:at + n], [(w[:, k, m * P:(m + 1) * P], XT[:, k, src]) for k in range(KT)])
                    if wide or m % 2:
                        last.then_inc(job_done, 1)

            def rows_out(name, c, with_meta):
                w = w_in_unit(c)
                for i, (at, n) in enumerate([(META, P), (META + P, P)] + [(0, META)] * with_meta):
                    b = to_fill(pe, name, i)
                    product(b[0:n, :], [(XT[:, k, at:at + n], w[:, k, :]) for k in range(KT)]).then_inc(job_done, 1)

            cols_out("hgf", 4, True)
            cols_out("hgq", 3, False)
            rows_out("hgi", 5, True)
            rows_out("hgg", 6, False)
            cols_out("sbq", 0, False)
            cols_out("sbk", 1, True)
            rows_out("sbv", 2, True)

            pe.wait_ge(hg_fac, 1)
            b = to_fill(pe, "kmT")
            for h in range(HG_HEADS):
                last = pe.transpose(b[0:META, h * P:(h + 1) * P], fmeta[:, h, :], ident[:, :])
            last.then_inc(job_done, 1)
            b = to_fill(pe, "s0")
            wait_emptied(pe, "kmT")
            for h in range(HG_HEADS):
                cut = slice(h * P, (h + 1) * P)
                last = pe.matmul(b[:, cut], kT_rows[0:META, cut], hgi[0:META, 2, cut], start=True, stop=True)
            last.then_inc(job_done, 1)
            pe.wait_ge(hg_fac, 2)
            b = to_fill(pe, "k1T")
            for h in range(HG_HEADS):
                last = pe.transpose(b[:, h * P:(h + 1) * P], lev[1][:, h, 0:P], ident[:, :])
            last.then_inc(job_done, 1)
            b = to_fill(pe, "s1")
            wait_emptied(pe, "k1T")
            for h in range(HG_HEADS):
                cut = slice(h * P, (h + 1) * P)
                last = pe.matmul(b[:, cut], kT_rows[:, cut], hgi[:, 0, cut], start=True, stop=True)
            last.then_inc(job_done, 1)

            for level in range(8):
                if level < 7:
                    pe.wait_ge(hg_fac, level + 3)
                for i in range(2):
                    b = to_fill(pe, f"level{level}", i)
                    for c in range(4):
                        h, tb = (4 * i + c) // 2, c % 2
                        cut = slice(tb * P, (tb + 1) * P)
                        if level < 7:
                            left = right = lev[level % 2][:, h, cut]
                        else:
                            left, right = hgk[:, h, META + tb * P:META + (tb + 1) * P], hgq[:, h, cut]
                        last = pe.matmul(b[:, c * P:(c + 1) * P], left, right, start=True, stop=True)
                    last.then_inc(job_done, 1)

            def sb_unit(i):
                tb, h = divmod(i, SB_HEADS)
                return tb, h, META + (tb + 1) * P, slice(SB_D * (h % 2), SB_D * (h % 2) + SB_D)

            def sb_scores(i):
                tb, h, w, half = sb_unit(i)
                b = to_fill(pe, f"z{i}")
                pe.matmul(b[:, 0:w], sbq[half, h // 2, tb * P:(tb + 1) * P], sbk[half, h // 2, 0:w],
                          start=True, stop=True).then_inc(job_done, 1)

            def sb_transpose(i):
                tb, h, w, half = sb_unit(i)
                pe.wait_ge(w_ready, i + 1)
                src = beta[i % 2]
                b = to_fill(pe, f"wT{i}")
                last = pe.transpose(b[0:META, 0:P], src[:, 0:META], ident[:, :])
                for k in range(tb + 1):
                    last = pe.transpose(b[:, (k + 1) * P:(k + 2) * P], src[:, META + k * P:META + (k + 1) * P], ident[:, :])
                last.then_inc(job_done, 1)

            def sb_values(i):
                tb, h, w, half = sb_unit(i)
                wait_emptied(pe, f"wT{i}")
                dst = bank[4 + tb][:, h * SB_D:(h + 1) * SB_D]
                cut = slice(h * SB_D, (h + 1) * SB_D)
                wT = wTs[i % 2]
                product(dst, [(wT[0:META, 0:P], sbv[0:META, 2, cut])] +
                        [(wT[:, (k + 1) * P:(k + 2) * P], sbv[:, k, cut]) for k in range(tb + 1)]).then_inc(wT_used, 1)

            for i in range(16 + 3):
                if i < 16:
                    sb_scores(i)
                if 2 <= i < 18:
                    sb_transpose(i - 2)
                if i >= 3:
                    sb_values(i - 3)

            pe.wait_ge(hg_fac, 10)
            for tb in range(TB):
                b = to_fill(pe, "ohg", tb)
                state = (S0, S1t)[tb]
                for h in range(HG_HEADS):
                    cut = slice(h * P, (h + 1) * P)
                    last = product(b[:, cut], [(score[:, 2 * h + tb, :], hgi[:, tb, cut]),
                                               (lev[0][:, h, tb * P:(tb + 1) * P], state[:, cut])])
                last.then_inc(job_done, 1)

            pe.wait_ge(rows_ready, 2)
            to_cols("mT", R)

            def rows_from(name, keys, lhs):
                for n, key in enumerate(keys):
                    w = wait_weights(pe, key).rearrange("p (k n) -> p k n", n=HALF)
                    for tb in range(TB):
                        b = to_fill(pe, name, 2 * n + tb)
                        product(b[:, :], [(lhs[:, k, tb * P:(tb + 1) * P], w[:, k, :]) for k in range(KT)]).then_inc(job_done, 1)

            wait_emptied(pe, "mT", 3)
            rows_from("w_out", [("w_out", 0), ("w_out", 1)], mixT)

            pe.wait_ge(rows_ready, 3)
            to_cols("x2T", R)
            wait_emptied(pe, "x2T", 3)
            pe.wait_ge(in_small, 16 * 6)
            b = to_fill(pe, "router")
            for tb in range(TB):
                last = product(b[:, tb * 64:tb * 64 + 36], [(XT[:, k, tb * P:(tb + 1) * P], w_router[:, k, :]) for k in range(KT)])
            last.then_inc(job_done, 1)
            pe.wait_ge(gate_ready, 1)
            b = to_fill(pe, "pos")
            sel = [sm(650 + EXPERTS * tb, EXPERTS) for tb in range(TB)]
            everyone = ones[:, 0:P]
            product(b[:, 0:EXPERTS], [(tri[:, :], sel[0])])
            product(b[:, EXPERTS:2 * EXPERTS], [(everyone, sel[0]), (tri[:, :], sel[1])])
            product(b[:, 2 * EXPERTS:3 * EXPERTS], [(everyone, sel[0]), (everyone, sel[1])]).then_inc(job_done, 1)
            pe.wait_ge(tables_in, 16 * 3)
            b = to_fill(pe, "cbT")
            for tb in range(TB):
                at = tb * HEADS * CMP_PAD
                pe.transpose(b[:, at:at + P], ctmp[:, 0, tb * P:(tb + 1) * P], ident[:, :])
                last = pe.transpose(b[:, at + P:at + P + 64], ctmp[0:64, 1, tb * P:(tb + 1) * P], ident[0:64, 0:64])
            last.then_inc(job_done, 1)
            for name in ("router", "pos", "cbT"):
                wait_emptied(pe, name)

            def clear_y():
                for y in range(4):
                    pe.matmul(bank[4 + y][:, :], zeros[:, 0:P], zeros[:, :], start=True, stop=False)

            def down(hidden, w, dst_last):
                for tb in range(TB):
                    for n in range(2):
                        for q in range(2):
                            last = pe.matmul(bank[4 + 2 * tb + n][:, :], hidden[:, q, tb * P:(tb + 1) * P],
                                             w[:, q, n * HALF:(n + 1) * HALF], start=False, stop=dst_last and q == 1)
                return last

            def up(bank_at, tiles):
                for ab, weights_of in enumerate(tiles):
                    last = product(bank[bank_at][:, ab * T:(ab + 1) * T],
                                   [(weights_of(k), XT[:, k, 0:T]) for k in range(KT)])
                return last

            base = first_unit["moe"]

            def gather(i):
                for k in range(KT):
                    dst = bank[2 + k // 4][:, (k % 4) * P:(k % 4 + 1) * P]
                    last = product(dst, [(R[:, tb, k * P:(k + 1) * P], pair_pick(tb, i)) for tb in range(TB)])
                return last

            def halves(e, at, w):
                for k in range(KT):
                    for j in range(2):
                        last = pe.matmul(bank[e % 2][64 * j:64 * j + 64, at:at + 256], xg_tile(e % 2, k),
                                         w[:, k, 256 * j:256 * j + 256], start=k == 0, stop=k == KT - 1)
                return last

            def turn(e):
                for q in range(2):
                    pe.transpose(bank[e % 2][:, q * P:(q + 1) * P], hid[e % 2][:, q * P:(q + 1) * P], ident[:, :])
                for tb in range(TB):
                    last = pe.transpose(bank[e % 2][:, 256 + tb * P:256 + (tb + 1) * P], gated[:, tb, e % 2 * P:(e % 2 + 1) * P], ident[:, :])
                return last

            def outputs(e, w):
                for f in range(4):
                    j, q = divmod(f, 2)
                    lhsT = hidden_T[e % 2][:, q * P + 64 * j:q * P + 64 * j + 64]
                    for n in range(2):
                        last = pe.matmul(bank[e % 2][64 * n:64 * n + 64, :], lhsT, w[:, f, n * HALF:(n + 1) * HALF],
                                         start=f == 0, stop=f == 3)
                return last

            def combine(e, start=False):
                for tb in range(TB):
                    for n in range(2):
                        half = slice(64 * n, 64 * n + 64)
                        last = pe.matmul(bank[4 + 2 * tb + n][:, :], give[e % 2][half, tb * P:(tb + 1) * P], yrow[e % 2][half, :],
                                         start=start, stop=False)
                return last

            def weights_of(e, which):
                n = base + 3 * e + which
                return ring[:, n % RING, :].rearrange("p (k n) -> p k n", n=D if which == 2 else HALF)

            def arrived(e, which, i):
                n = base + 3 * e + which
                pe.wait_ge(landed[n % RING], i * 16 + use_count(n))
                return weights_of(e, which)

            def moe_gather(pair, i):
                pe.wait_ge(moe["taken"], i * 2 + 2 * pair)
                gather(i + pair).then_inc(moe["gathered"], 1)

            def moe_gate(e, i, first=False):
                w = arrived(e, 0, i)
                pe.wait_ge(moe["taken"], i * 2 + 2 * (e // 2) + 2)
                if not first:
                    pe.wait_ge(moe["row"], i * 2 + (e - 1))
                halves(e, 0, w).then_inc(moe["gate"], 1)

            def moe_up(e, i):
                halves(e, 256, arrived(e, 1, i)).then_inc(moe["up"], 1)

            def moe_turn(e, i):
                pe.wait_ge(moe["gated"], i + (e // 2 + 1))
                pe.wait_ge(moe["hidden"], i * 2 + (e + 1))
                turn(e).then_inc(moe["turned"], 1)

            def moe_down(e, i):
                w = arrived(e, 2, i)
                pe.wait_ge(moe["turned_copied"], i * 2 + (e + 1))
                outputs(e, w).then_inc(moe["down"], 1)

            def moe_combine(e, i, start=False):
                pe.wait_ge(moe["row"], i * 2 + (e + 1))
                combine(e, start).then_inc(moe["combined"], 1)

            def moe_pair(i, first=False):
                moe_gate(1, i, first)
                moe_turn(0, i)
                moe_up(1, i)
                moe_gather(1, i)
                moe_down(0, i)
                if not first:
                    moe_combine(-1, i)
                moe_gate(2, i)
                moe_turn(1, i)
                moe_up(2, i)
                moe_down(1, i)
                moe_combine(0, i, start=first)

            pe.wait_ge(moe["picks"], 1)
            gather(0).then_inc(moe["gathered"], 1)
            moe_gate(0, 0, first=True)
            moe_up(0, 0)
            pe.wait_ge(moe["picks"], 2)
            moe_pair(0, first=True)
            with pe.Fori(1, EXPERTS // 2 - 1) as i:
                moe_pair(i)
            e = EXPERTS - 1
            moe_gate(e, 0)
            moe_turn(e - 1, 0)
            moe_up(e, 0)
            moe_down(e - 1, 0)
            moe_combine(e - 2, 0)
            moe_turn(e, 0)
            moe_combine(e - 1, 0)
            moe_down(e, 0)
            moe_combine(e, 0)

            pe.wait_ge(moe["combined"], EXPERTS)
            pe.wait_ge(moe["extra_known"], 1)
            more = pe.value_load(extra[0:1, 0:1], min_val=0, max_val=PASSES - 1)
            with pe.If(more > 0):
                with pe.Fori(0, more) as p:
                    with pe.Fori(0, EXPERTS // 2) as i:
                        pe.wait_ge(ov["picks"], p + 1)
                        pe.wait_ge(ov["done"], p * EXPERTS + i * 2 + 1)
                        gather(i).then_inc(ov["gathered"], 1)
                        pe.wait_ge(ov["taken"], p * (EXPERTS // 2) + i + 1)
                        pe.wait_ge(ov["loaded"], p * (48 * EXPERTS) + i * 96 + 96)
                        for r in range(2):
                            halves(r, 0, weights_of(r, 0))
                            halves(r, 256, weights_of(r, 1)).then_inc(ov["up"], 1)
                            pe.wait_ge(ov["gated"], p * (EXPERTS // 2) + i + 1)
                            pe.wait_ge(ov["hidden"], p * EXPERTS + i * 2 + (r + 1))
                            turn(r).then_inc(ov["turned"], 1)
                            pe.wait_ge(ov["turned_copied"], p * EXPERTS + i * 2 + (r + 1))
                            outputs(r, weights_of(r, 2)).then_inc(ov["down"], 1)
                            pe.wait_ge(ov["row"], p * EXPERTS + i * 2 + (r + 1))
                            combine(r).then_inc(ov["done"], 1)
            for y in range(4):
                last = pe.matmul(bank[4 + y][:, :], zeros[:, 0:P], zeros[:, :], start=False, stop=True)
            last.then_inc(sums_ready, 1)

            attention = [0]

            def attend(layer):
                mine = [u for u, key in enumerate(att) if key[0] == layer]

                def scores(u):
                    _, kind, pair, tb, h = att[u]
                    if u - mine[0] >= 2:
                        pe.wait_ge(at_m, 2 * (u - 1))
                    for seg in range(2):
                        r = h % 2 if kind == "nsa" else seg
                        half = slice(64 * r, 64 * r + 64)
                        if kind == "mem":
                            q, k, w = qmT[half, pair, :], km[layer][half, pair, :], MEM
                        else:
                            q, k, w = qT[half, pair, :], kT[half, seg if kind == "nsa" else pair, :], P * (tb + 1)
                        last = pe.matmul(bank[2 * (u % 2) + seg][:, 0:w], q[:, tb * P:(tb + 1) * P], k[:, 0:w], start=True, stop=True)
                        last.then_inc(at_l, 1)

                def blocks_of(u):
                    _, kind, pair, tb, h = att[u]
                    return 2 if kind == "mem" else tb + 1

                def trans(u):
                    pe.wait_ge(at_p, u + 1)
                    if u >= 2:
                        pe.wait_ge(at_tc, u - 1)
                    nb = blocks_of(u)
                    for seg in range(2):
                        for b in range(nb):
                            at = (seg * nb + b) * P
                            last = pe.transpose(bank[4 + u % 2][:, at:at + P], logit[u % 3][:, seg, b * P:(b + 1) * P], ident[:, :])
                    last.then_inc(at_t, 1)

                def values(u):
                    _, kind, pair, tb, h = att[u]
                    g, first = group_of(u)
                    pe.wait_ge(at_tc, u + 1)
                    if first and g >= 2:
                        pe.wait_ge(at_oc, g - 1)
                    nb = blocks_of(u)
                    o = bank[6 + g % 2]
                    for seg in range(2):
                        r = h % 2 if kind == "nsa" else seg
                        dst = o[64 * r:64 * r + 64, tb * P:(tb + 1) * P]
                        pairs = []
                        if kind == "nsa" and seg == 0:
                            pairs.append((vz[:, h % 4, :], pcT[:, h // 4, tb * P:(tb + 1) * P]))
                        for b in range(nb):
                            at = (seg * nb + b) * P
                            if kind == "nsa":
                                v = vrow0[:, b, 64 * seg:64 * seg + 64]
                            elif kind == "moba":
                                v = vrow[:, b, 64 * (h + seg):64 * (h + seg) + 64]
                            else:
                                v = vm[layer][:, b, 64 * (h + seg):64 * (h + seg) + 64]
                            pairs.append((v, pT[u % 2][:, at:at + P]))
                        for k, (lhsT, rhs) in enumerate(pairs):
                            last = pe.matmul(dst, lhsT, rhs, start=k == 0 and not (kind == "nsa" and seg == 1),
                                             stop=k == len(pairs) - 1 and not (kind == "nsa" and seg == 0))
                    last.then_inc(at_o, 1)

                n = len(mine)
                for i in range(n + 3):
                    if i < n:
                        scores(mine[i])
                    if 2 <= i < n + 2:
                        trans(mine[i - 2])
                    if i >= 3:
                        values(mine[i - 3])

            pe.wait_ge(ln_done, 1)
            to_cols("xTa", X)
            wait_emptied(pe, "xTa", 3)
            wa = [wait_weights(pe, ("a_in", c))[:, 0:KT * n].rearrange("p (k n) -> p k n", n=n)
                  for c, n in ((0, HALF), (1, HALF), (2, 1444 - 2 * HALF))]

            def a_cols(at, n):
                c = at // HALF
                return lambda k: wa[c][:, k, at - c * HALF:at - c * HALF + n]

            def twice(b, at, w_of):
                for r in range(2):
                    last = product(b[64 * r:64 * r + 64, at:at + T], [(w_of(k), XT[:, k, 0:T]) for k in range(KT)])
                return last

            def tiles(name, job, w_of_tiles):
                b = to_fill(pe, name, job)
                for i, w_of in enumerate(w_of_tiles):
                    last = product(b[:, i * T:(i + 1) * T], [(w_of(k), XT[:, k, 0:T]) for k in range(KT)])
                last.then_inc(job_done, 1)

            for j in range(3):
                tiles("a_q", j, [a_cols((2 * j + r) * P, P) for r in range(2)])
            b = to_fill(pe, "a_kv", 0)
            twice(b, 0, a_cols(768, 64))
            twice(b, T, a_cols(832, 64)).then_inc(job_done, 1)
            b = to_fill(pe, "a_kv", 1)
            twice(b, 0, a_cols(896, 64))
            twice(b, T, a_cols(1024, 64)).then_inc(job_done, 1)
            b = to_fill(pe, "a_kv", 2)
            for tb in range(TB):
                last = product(b[:, tb * 64:tb * 64 + 36], [(XT[:, k, tb * P:(tb + 1) * P], a_cols(1152, 36)(k)) for k in range(KT)])
            last.then_inc(job_done, 1)
            b = to_fill(pe, "a_v")
            for tb in range(TB):
                for i, at in enumerate((960, 1088)):
                    last = product(b[:, tb * P + 64 * i:tb * P + 64 * i + 64],
                                   [(XT[:, k, tb * P:(tb + 1) * P], a_cols(at, 64)(k)) for k in range(KT)])
            last.then_inc(job_done, 1)
            tiles("a_qm", 0, [a_cols(1188 + r * P, P) for r in range(2)])

            pe.wait_ge(cmp_in, 1)
            for kv in range(2):
                w = wait_weights(pe, (("cmp_k", "cmp_v")[kv], 0)).rearrange("p (j n) -> p j n", n=CMP_HID)
                b = to_fill(pe, "cmp_h", kv)
                for m in range(2):
                    last = product(b[:, m * CMP_PAD:m * CMP_PAD + N_CMP],
                                   [(w[:, j, m * P:(m + 1) * P], logit[2][:, kv, j * N_CMP:(j + 1) * N_CMP]) for j in range(16)])
                last.then_inc(job_done, 1)
            wait_emptied(pe, "cmp_h", 1)
            pe.wait_ge(in_small, 16 * 6)
            b = to_fill(pe, "cmp_kv")
            for r in range(2):
                product(b[64 * r:64 * r + 64, 0:CMP_PAD], [(w2[:, 0, m, :], hidT[:, m, 0:CMP_PAD]) for m in range(2)])
            for r in range(4):
                last = product(b[32 * r:32 * r + 32, 64:128], [(hidT[:, 2 + m, :], w2[:, 1, m, :]) for m in range(2)])
            last.then_inc(job_done, 1)
            wait_emptied(pe, "cmp_kv")
            for tb in range(TB):
                b = to_fill(pe, "cmp_l", tb)
                for pair in range(PAIRS):
                    last = pe.matmul(b[:, pair * 32:pair * 32 + 32], qT[:, pair, tb * P:(tb + 1) * P],
                                     kz[:, :, :].rearrange("p a b -> p (a b)"), start=True, stop=True)
                last.then_inc(job_done, 1)
            pe.wait_ge(cmp_x, 2)
            for j, n in enumerate((2, 1)):
                b = to_fill(pe, "cmp_pT", j)
                for i in range(n):
                    for tb in range(TB):
                        last = pe.transpose(b[:, i * T + tb * P:i * T + (tb + 1) * P],
                                            pc[:, tb, (2 * j + i) * P:(2 * j + i + 1) * P], ident[:, :])
                last.then_inc(job_done, 1)
            for name, i in (("cmp_l", 0), ("cmp_l", 1), ("cmp_pT", 0), ("cmp_pT", 1)):
                wait_emptied(pe, name, i)
            attend(0)
            pe.wait_ge(at_oc, 8)
            rows_from("a_out", [("a_out", 0), ("a_out", 1)], mixT)

            def ffn(layer):
                ph = phase_sems[f"ffn{layer}"]
                base = first_unit[f"ffn{layer}"]

                def ffn_up(j, k):
                    n = base + 3 * (j // 2) + j % 2
                    pe.wait_ge(landed[n % RING], k * 32 + use_count(n))
                    w = ring[:, n % RING, :].rearrange("p (k h n) -> p k h n", h=2, n=256)
                    if j >= 1:
                        pe.wait_ge(ph["hidden"], k * 8 + max(2 * j - 2, 1))
                    for q in range(2):
                        last = up(2 * (j % 2) + q, [lambda kk, h=h, q=q: w[:, kk, h, q * P:(q + 1) * P] for h in range(2)])
                        last.then_inc(ph["tile"], 1)

                def ffn_down(j, k, final=False):
                    n = base + 3 * (j // 2) + (2 if j < STEPS_F - 1 else 1)
                    if j % 2 == 0:
                        pe.wait_ge(landed[n % RING], k * 16 + use_count(n))
                    w = ring[:, n % RING, :].rearrange("p (k n) -> p k n", n=D)[:, 2 * (j % 2):2 * (j % 2) + 2, :]
                    pe.wait_ge(ph["hidden"], k * 8 + (2 * j + 2))
                    down(hb[j % 2], w, final).then_inc(ph["used"], 1)

                clear_y()
                ffn_up(0, 0)
                with pe.Fori(0, 2) as i:
                    for u in range(4):
                        ffn_up(u + 1, i)
                        ffn_down(u, i)
                for j in (8, 9):
                    ffn_up(j + 1, 0)
                    ffn_down(j, 0)
                ffn_down(10, 0, final=True)

            pe.wait_ge(zero_ready, 1)
            pe.wait_ge(ln_done, 3)
            to_cols("xTf0", X)
            for j in range(4):
                wait_emptied(pe, "xTf0", j)
            ffn(0)

            pe.wait_ge(ln_done, 5)
            to_cols("xTb", X)
            wait_emptied(pe, "xTb", 3)
            wk = [wait_weights(pe, ("kv", c)).rearrange("p (k n) -> p k n", n=HALF) for c in range(3)]

            def kv_cols(at, n):
                return lambda k: wk[at // HALF][:, k, at % HALF:at % HALF + n]

            for j in range(3):
                tiles("b_k", j, [kv_cols((2 * j + r) * P, P) for r in range(2)])
            for i, (tb, at, n) in enumerate([(tb, at, n) for at, n in ((768, 256), (1024, 512)) for tb in range(TB)]):
                b = to_fill(pe, "b_v", i)
                product(b[:, 0:n], [(XT[:, k, tb * P:(tb + 1) * P], kv_cols(at, n)(k)) for k in range(KT)]).then_inc(job_done, 1)
            wq = [wait_weights(pe, ("b_in", c)).rearrange("p (k n) -> p k n", n=HALF) for c in range(2)]

            def b_cols(at):
                return lambda k: wq[at // HALF][:, k, at % HALF:at % HALF + P]

            for j in range(3):
                tiles("b_q", j, [b_cols((2 * j + r) * P) for r in range(2)])
            tiles("b_qm", 0, [b_cols(768 + r * P) for r in range(2)])
            for j in range(3):
                wait_emptied(pe, "b_q", j)
            wait_emptied(pe, "b_qm")
            attend(1)
            pe.wait_ge(at_oc, 16)
            rows_from("b_out", [("b_out", 0), ("b_out", 1)], mixT)
            pe.wait_ge(ln_done, 7)
            to_cols("xTf1", X)
            for j in range(4):
                wait_emptied(pe, "xTf1", j)
            ffn(1)

        @block.scalar
        def _(act):
            step = chained(act, act_step)

            def empty(name, i, *moves):
                b = filled(act, name, i)
                for dst, src, func in moves:
                    last = act.activation(dst, src(b), func)
                last.then_inc(emptied_a, 1)

            act.wait_ge(pool_const, 1)
            act.wait_ge(in_x, 32)
            step(act.activation(junk, X[:, 0, :], ACT.Square, accum_out=sm(0, 1)))
            step(act.activation(junk, X[:, 1, :], ACT.Square, accum_out=sm(1, 1)))
            act.activation(junk[0:META, :], meta, ACT.Square, accum_out=small[0:META, 2:3]).then_inc(sq_ready, 1)

            empty("pack", 0, (cols[:, :], lambda b: b[:, 0:PACK_ROWS + 2 * CONV_ROWS], ACT.Copy))
            for j in range(4):
                empty("memT", j, (memT[:, 2 * j:2 * j + 2, :], lambda b: b[:, :].rearrange("p (a t) -> p a t", t=T), ACT.Copy))
            act.wait_ge(stat_ready, 1)
            act.activation(sm(3, 3), sm(3, 3), ACT.Sqrt).then_inc(sq_ready, 1)
            for l, name in enumerate(("mem_a", "mem_b")):
                for i, dst in enumerate((km[l], vm[l])):
                    empty(name, i, (dst[:, :, :].rearrange("p a b -> p (a b)"), lambda b: b[:, :], ACT.Copy))
            for i, (at, n) in enumerate(((0, DIST_REV), (DIST_REV, DIST_FWD))):
                empty("dist", i, (dist_out[:, at:at + n], lambda b, n=n: b[0:HEADS, 0:n], ACT.Copy))

            act.wait_ge(lbound_ready, 1)
            act.activation(sm(16, 8), sm(16, 8), ACT.Exp).then_inc(lbound_ready, 1)

            for h in range(HG_HEADS):
                b = filled(act, "hgf", h)
                act.activation(logf[:, h, :], b[:, 0:S1], ACT.Sigmoid)
                act.activation(hgk[:, h, :], b[:, 0:S1], ACT.Sigmoid, scale=-1.0).then_inc(emptied_a, 1)
            pair = lambda b: b[:, :].rearrange("p (a t) -> p a t", t=T)
            for i in range(2):
                empty("hgq", i, (hgq[:, 2 * i:2 * i + 2, :], pair, ACT.Silu))
            act.wait_ge(dist_stored, 16)
            act.wait_ge(hg_f, 1)
            act.activation(logf[:, :, :], logf[:, :, :], ACT.Ln).then_inc(hg_log, 1)
            for i in range(3):
                n = META if i == 2 else P
                empty("hgi", i, (hgi[0:n, i, :], lambda b, n=n: b[0:n, :], ACT.Copy))
            for i in range(2):
                empty("hgg", i, (hgg[:, i, :], lambda b: b[:, :], ACT.Silu))

            def decay(k):
                dst = [fmeta[:, :, :], lev[1][:, :, 0:P]] + [lev[level % 2][:, :, :] for level in range(7)] + [lev[0][:, :, :]]
                act.wait_ge(hg_arg, k + 1)
                act.activation(dst[k], dst[k], ACT.Exp).then_inc(hg_exp, 1)

            decay(0)
            decay(1)
            act.activation(sm(24, 4), bcum[:, :, P - 1], ACT.Exp).then_inc(hg_q, 1)
            for i in range(2):
                empty("sbq", i, (sbq[:, 2 * i:2 * i + 2, :], pair, ACT.Copy))
            for i in range(4):
                empty("sbk", i, (sbk[:, i, :], lambda b: b[:, 0:S1], ACT.Copy))
            for i in range(3):
                n = META if i == 2 else P
                empty("sbv", i, (sbv[0:n, i, :], lambda b, n=n: b[0:n, :], ACT.Copy))
            empty("kmT", 0, (kT_rows[0:META, :], lambda b: b[0:META, :], ACT.Copy))
            empty("s0", 0, (S0, lambda b: b[:, :], ACT.Copy))
            empty("k1T", 0, (kT_rows, lambda b: b[:, :], ACT.Copy))
            for k in range(2, 10):
                decay(k)

            def sb_sigmoids(i):
                w = META + (i // SB_HEADS + 1) * P
                wait_emptied(act, f"z{i}")
                if i >= 2:
                    act.wait_ge(w_ready, i - 1)
                    act.wait_ge(job_done, jobs.number(f"wT{i - 2}") + 1)
                act.activation(beta[i % 2][:, 0:w], zm[i % 2][:, 0:w], ACT.Sigmoid)
                act.activation(keep[i % 2][:, 0:w], zm[i % 2][:, 0:w], ACT.Sigmoid, scale=-1.0).then_inc(sig_ready, 1)

            def sb_transposed(i):
                tb = i // SB_HEADS
                b = filled(act, f"wT{i}")
                if i >= 2:
                    act.wait_ge(wT_used, i - 1)
                act.activation(wTs[i % 2][0:META, 0:P], b[0:META, 0:P], ACT.Copy)
                act.activation(wTs[i % 2][:, P:P * (tb + 2)], b[:, P:P * (tb + 2)], ACT.Copy).then_inc(emptied_a, 1)

            for i in range(16 + 2):
                if i >= 2:
                    sb_transposed(i - 2)
                if i < 16:
                    sb_sigmoids(i)

            act.wait_ge(stat_ready, 2)
            act.activation(sm(30, 24), sm(30, 24), ACT.Sqrt).then_inc(sq_ready, 1)

            def empty_gained(name, gain_at):
                for j in range(4):
                    b = filled(act, name, j)
                    for r in range(2):
                        k = 2 * j + r
                        last = act.activation(XT[:, k, 0:T], b[:, r * T:(r + 1) * T], ACT.Copy, scale=cols[:, gain_at + k:gain_at + k + 1])
                    last.then_inc(emptied_a, 1)

            empty_gained("mT", PACK["sb_gain"][0])
            wait_emptied(act, "w_out", 3)
            for tb in range(TB):
                last = act.activation(R[:, tb, :], X[:, tb, :], ACT.Square, accum_out=sm(6 + tb, 1))
            last.then_inc(sq_ready, 1)
            act.wait_ge(stat_ready, 3)
            act.activation(sm(8, 2), sm(8, 2), ACT.Sqrt).then_inc(sq_ready, 1)
            empty_gained("x2T", PACK["g_ffn"][0])

            act.wait_ge(router_arg, 1)
            act.activation(sm(200, 8), sm(200, 8), ACT.Exp).then_inc(router_exp, 1)
            act.wait_ge(router_arg, 2)
            act.activation(sm(240, 2), sm(240, 2), ACT.Exp).then_inc(router_exp, 1)

            def silu(e):
                return act.activation(gact[e % 2], bank[e % 2][:, 0:256], ACT.Silu)

            def turned(e):
                return act.activation(turned_sb[e % 2], bank[e % 2][:, :], ACT.Copy)

            def moe_silu(e, i, first=False):
                act.wait_ge(moe["up"], i * 2 + (e + 1))
                if not first:
                    act.wait_ge(moe["hidden"], i * 2 + (e - 1))
                silu(e).then_inc(moe["silu"], 1)

            def moe_turned(e, i, first=False):
                act.wait_ge(moe["turned"], i * 2 + (e + 1))
                if not first:
                    act.wait_ge(moe["combined"], i * 2 + (e - 1))
                turned(e).then_inc(moe["turned_copied"], 1)

            def moe_pair(i, first=False):
                moe_turned(0, i, first)
                moe_silu(1, i, first)
                moe_turned(1, i, first)
                moe_silu(2, i)

            moe_silu(0, 0, first=True)
            moe_pair(0, first=True)
            with act.Fori(1, EXPERTS // 2 - 1) as i:
                moe_pair(i)
            e = EXPERTS - 1
            moe_turned(e - 1, 0)
            moe_silu(e, 0)
            moe_turned(e, 0)

            act.wait_ge(moe["extra_known"], 1)
            more = act.value_load(extra[0:1, 0:1], min_val=0, max_val=PASSES - 1)
            with act.If(more > 0):
                with act.Fori(0, more) as p:
                    with act.Fori(0, EXPERTS // 2) as i:
                        for r in range(2):
                            count = p * EXPERTS + i * 2 + (r + 1)
                            act.wait_ge(ov["up"], count)
                            silu(r).then_inc(ov["silu"], 1)
                            act.wait_ge(ov["turned"], count)
                            turned(r).then_inc(ov["turned_copied"], 1)

            act.wait_ge(y_used, 1)
            for tb in range(TB):
                last = act.activation(R[:, tb, :], X[:, tb, :], ACT.Square, accum_out=sm(10 + tb, 1))
            last.then_inc(sq_ready, 1)
            act.wait_ge(stat_ready, 4)
            act.activation(sm(12, 2), sm(12, 2), ACT.Sqrt).then_inc(sq_ready, 1)

            def empty_cols(name):
                for j in range(4):
                    empty(name, j, (XT[:, 2 * j:2 * j + 2, 0:T], pair, ACT.Copy))

            empty_cols("xTa")
            for j in range(3):
                empty("a_q", j, (qT[:, 2 * j:2 * j + 2, :], pair, ACT.Copy))
            b = filled(act, "a_kv", 0)
            for kv in range(2):
                act.activation(shift2[0:64, kv, :], b[0:64, kv * T:(kv + 1) * T], ACT.Copy)
                last = act.activation(shift2[64:128, kv, 0:T - 1], b[64:128, kv * T + 1:(kv + 1) * T], ACT.Copy)
            last.then_inc(emptied_a, 1)
            empty("a_kv", 1, (kT[:, 0:2, :], pair, ACT.Copy))
            empty("a_kv", 2, (sm(260, 72).rearrange("p (b g) -> p b g", b=2),
                              lambda b: b[:, 0:128].rearrange("p (b g) -> p b g", b=2)[:, :, 0:36], ACT.Sigmoid))
            empty("a_v", 0, (vrow0[:, :, :], lambda b: b[:, 0:2 * P].rearrange("p (b n) -> p b n", b=2), ACT.Copy))
            empty("a_qm", 0, (qmT[:, :, :], pair, ACT.Copy))
            act.wait_ge(pool_step, 1)
            for kv in range(2):
                empty("cmp_h", kv, (hidT[:, 2 * kv:2 * kv + 2, 0:N_CMP],
                                    lambda b: b[:, 0:2 * CMP_PAD].rearrange("p (m n) -> p m n", m=2)[:, :, 0:N_CMP], ACT.Gelu_apprx_tanh))
            b = filled(act, "cmp_kv")
            for r in range(2):
                act.activation(kz[64 * r:64 * r + 64, r, :], b[64 * r:64 * r + 64, 0:CMP_PAD], ACT.Copy)
            for r in range(4):
                last = act.activation(vz[32 * r:32 * r + 32, r, :], b[32 * r:32 * r + 32, 64:128], ACT.Copy)
            last.then_inc(emptied_a, 1)
            act.wait_ge(cmp_e, 1)
            act.activation(sm(340, 12 * 16 + 0), sm(340, 192), ACT.Exp).then_inc(cmp_e, 1)
            act.wait_ge(cmp_e, 3)
            act.activation(sm(340, 192), sm(340, 192), ACT.Exp).then_inc(cmp_e, 1)
            for j, n in enumerate((2, 1)):
                empty("cmp_pT", j, (pcT[:, 2 * j:2 * j + n, :], lambda b, n=n: b[:, 0:n * T].rearrange("p (a t) -> p a t", t=T), ACT.Copy))

            def attend(layer):
                mine = [u for u, key in enumerate(att) if key[0] == layer]

                def exps(u):
                    act.wait_ge(at_x, u + 1)
                    w = width(u)
                    for seg in range(2):
                        last = act.activation(logit[u % 3][:, seg, 0:w], logit[u % 3][:, seg, 0:w], ACT.Exp,
                                              bias=sm(540 + 8 * (u % 3) + seg, 1), accum_out=sm(542 + 8 * (u % 3) + seg, 1))
                    last.then_inc(at_e, 1)

                def trans(u):
                    act.wait_ge(at_t, u + 1)
                    if u >= 2:
                        act.wait_ge(at_o, u - 1)
                    n = 2 * width(u)
                    act.activation(pT[u % 2][:, 0:n], bank[4 + u % 2][:, 0:n], ACT.Copy).then_inc(at_tc, 1)

                for i in range(len(mine) + 2):
                    if i < len(mine):
                        exps(mine[i])
                    if i >= 2:
                        trans(mine[i - 2])

            attend(0)

            def norm_root(k):
                act.wait_ge(stat_ready, 5 + k)
                act.activation(sm(600, 2), sm(600, 2), ACT.Sqrt).then_inc(sq_ready, 1)

            def ffn(layer):
                ph = phase_sems[f"ffn{layer}"]
                at_w = PACK_ROWS + layer * CONV_ROWS
                at_b = PACK["conv_b"][0] + layer * FFT

                def gelu_step(j, k):
                    for q in range(2):
                        act.wait_ge(ph["tile"], k * 8 + (2 * j + q + 1))
                        if j >= 1:
                            act.wait_ge(ph["hidden"], k * 8 + max(2 * j - 2 + q, 1))
                        act.activation(work[(2 * j + q) % 4], bank[2 * (j % 2) + q][:, 0:T], ACT.Identity,
                                       scale=cols[:, bass.ds(k * 8 + (at_w + 2 * FFT + 2 * j + q), 1)],
                                       bias=cols[:, bass.ds(k * 8 + (at_b + 2 * j + q), 1)]).then_inc(ph["act"], 1)
                    for q in range(2):
                        act.wait_ge(mulp[f"ffn{layer}"], k * 8 + (2 * j + q + 1))
                        w = work[(2 * j + q) % 4]
                        act.activation(w, w, ACT.Gelu_apprx_tanh).then_inc(act2[f"ffn{layer}"], 1)

                gelu_step(0, 0)
                with act.Fori(0, 2) as i:
                    for u in range(4):
                        gelu_step(u + 1, i)
                for j in (9, 10):
                    gelu_step(j, 0)

            norm_root(0)
            empty_cols("xTf0")
            ffn(0)
            norm_root(1)
            empty_cols("xTb")
            for j in range(3):
                empty("b_k", j, (kT[:, 2 * j:2 * j + 2, :], pair, ACT.Copy))
            for i, (tb, at, n) in enumerate([(tb, at, n) for at, n in ((0, 256), (256, 512)) for tb in range(TB)]):
                empty("b_v", i, (vrow[:, tb, at:at + n], lambda b, n=n: b[:, 0:n], ACT.Copy))
            for j in range(3):
                empty("b_q", j, (qT[:, 2 * j:2 * j + 2, :], pair, ACT.Copy))
            empty("b_qm", 0, (qmT[:, :, :], pair, ACT.Copy))
            attend(1)
            norm_root(2)
            empty_cols("xTf1")
            ffn(1)
            norm_root(3)

        @block.vector
        def _(dve):
            step = chained(dve, dve_step)
            tt, ts, stt = dve.tensor_tensor, dve.tensor_scalar, dve.scalar_tensor_tensor

            def emptied_self():
                dve.wait_ge(emptied_v, emptied_self.count)
            emptied_self.count = 0

            def count_emptied(instruction):
                emptied_self.count += 1
                instruction.then_inc(emptied_v, 1)

            dve.memset(arena[BUCKETS:BUCKETS + 1, at_hgi + 900:at_hgi + 900 + HEADS], NEG).then_inc(dist_ready, 1)

            dve.wait_ge(sq_ready, 1)
            step(ts(sm(3, 2), sm(0, 2), 1.0 / D, EPS, ALU.mult, ALU.add))
            ts(small[0:META, 5:6], small[0:META, 2:3], 1.0 / D, EPS, ALU.mult, ALU.add).then_inc(stat_ready, 1)
            dve.wait_ge(sq_ready, 2)
            step(dve.reciprocal(sm(3, 3), sm(3, 3)))
            dve.wait_ge(job_done, jobs.number("memT", 3) + 1)
            ts(meta, meta, small[0:META, 5:6], None, ALU.mult)
            for tb in range(TB):
                last = ts(R[:, tb, :], X[:, tb, :], sm(3 + tb, 1), None, ALU.mult)
            last.then_inc(rows_ready, 1)

            wait_emptied(dve, "pack")
            l0, l1 = (cols[:, PACK["lb"][0] + 4 * i:PACK["lb"][0] + 4 * i + 4] for i in range(2))
            step(tt(sm(650, 4), l0, l1, ALU.max))
            tt(sm(16, 4), l0, sm(650, 4), ALU.subtract)
            tt(sm(20, 4), l1, sm(650, 4), ALU.subtract).then_inc(lbound_ready, 1)

            for k in range(KT):
                b = filled(dve, "aT", k)
                at = PACK["g_mix"][0] + k
                count_emptied(ts(XT[:, k, :], b[:, 0:S1], cols[:, at:at + 1], None, ALU.mult))

            dve.wait_ge(lbound_ready, 2)
            step(tt(sm(650, 4), sm(16, 4), sm(20, 4), ALU.add))
            step(dve.reciprocal(sm(650, 4), sm(650, 4)))
            step(tt(sm(16, 4), sm(16, 4), sm(650, 4), ALU.mult))
            step(ts(sm(20, 4), sm(16, 4), -1.0, 1.0, ALU.mult, ALU.add))

            for h in range(HG_HEADS):
                wait_emptied(dve, "hgf", h)
                ts(logf[:, h, :], logf[:, h, :], sm(20 + h, 1), sm(16 + h, 1), ALU.mult, ALU.add)
                last = ts(hgk[:, h, :], hgk[:, h, :], sm(20 + h, 1), None, ALU.mult)
            last.then_inc(hg_f, 1)
            dve.wait_ge(hg_log, 1)
            dve.wait_ge(pool_const, 3)
            for h in range(HG_HEADS):
                dve.tensor_tensor_scan(bmeta[:, h, :], ones[:, 0:META], logf[:, h, 0:META], 0.0, ALU.mult, ALU.add)
                for c in range(TB):
                    last = dve.tensor_tensor_scan(bcum[:, h, c * P:(c + 1) * P], ones[:, 0:P],
                                                  logf[:, h, META + c * P:META + (c + 1) * P], 0.0, ALU.mult, ALU.add)
            step(last)
            tt(fmeta[:, :, :], bmeta[:, :, META - 1:META].broadcast_to([P, 4, META]), bmeta[:, :, :], ALU.subtract).then_inc(hg_arg, 1)
            tt(lev[1][:, :, 0:P], bcum[:, :, P - 1:P].broadcast_to([P, 4, P]), bcum[:, :, 0:P], ALU.subtract).then_inc(hg_arg, 1)

            def sides(t, half):
                v = t.rearrange("p h (x two r) -> p h x two r", two=2, r=half)
                return v[:, :, :, 0, :], v[:, :, :, 1, :]

            def flat_sides(t, half):
                v = t.rearrange("p h t -> p (h t)").rearrange("p (x two r) -> p x two r", two=2, r=half)
                return v[:, :, 0, :], v[:, :, 1, :]

            def level_args(level):
                half = P >> (level + 1)
                left, right = flat_sides(bcum[:, :, :], half)
                to_left, to_right = flat_sides(lev[level % 2][:, :, :], half)
                shape = list(left.shape)
                ref = left[:, :, half - 1:half].broadcast_to(shape)
                tt(to_left, ref, left, ALU.subtract)
                tt(to_right, right, ref, ALU.subtract).then_inc(hg_arg, 1)

            def level_factors(level):
                half = P >> (level + 1)
                dve.wait_ge(hg_exp, level + 3)
                to_left, to_right = sides(lev[level % 2][:, :, :], half)
                tt(to_left, to_left, sides(hgk[:, :, META:S1], half)[0], ALU.mult)
                tt(to_right, to_right, sides(hgq[:, :, :], half)[1], ALU.mult).then_inc(hg_fac, 1)

            def level_scores(level):
                for i in range(2):
                    b = filled(dve, f"level{level}", i)
                    count_emptied(dve.copy_predicated(score[:, 4 * i:4 * i + 4, :],
                                                      level_mask[:, level:level + 1, :].broadcast_to([P, 4, P]),
                                                      b[:, :].rearrange("p (a t) -> p a t", t=P)))

            dve.wait_ge(hg_exp, 1)
            tt(fmeta[:, :, :], fmeta[:, :, :], hgk[:, :, 0:META], ALU.mult).then_inc(hg_fac, 1)
            level_args(0)
            dve.wait_ge(hg_exp, 2)
            tt(lev[1][:, :, 0:P], lev[1][:, :, 0:P], hgk[:, :, META:META + P], ALU.mult).then_inc(hg_fac, 1)
            wait_emptied(dve, "hgq", 1)
            b = filled(dve, "s1")
            wait_emptied(dve, "s0")
            dve.wait_ge(hg_q, 1)
            for h in range(HG_HEADS):
                cut = slice(h * P, (h + 1) * P)
                last = stt(S1t[:, cut], S0[:, cut], sm(24 + h, 1), b[:, cut], ALU.mult, ALU.add)
            count_emptied(last)
            dve.wait_ge(mask_ready, 1)
            for level in range(7):
                if level < 6:
                    if level == 0:
                        dve.wait_ge(job_done, jobs.number("k1T") + 1)
                    else:
                        dve.wait_ge(job_done, jobs.number(f"level{level - 1}", 1) + 1)
                    level_args(level + 1)
                level_factors(level)
                if level >= 1:
                    level_scores(level - 1)
                    emptied_self()
            level_scores(6)
            emptied_self()
            level_scores(7)
            dve.wait_ge(job_done, jobs.number("level6", 1) + 1)
            dve.tensor_copy(lev[0][:, :, :], bcum[:, :, :]).then_inc(hg_arg, 1)
            dve.wait_ge(hg_exp, 10)
            tt(lev[0][:, :, :], lev[0][:, :, :], hgq[:, :, :], ALU.mult).then_inc(hg_fac, 1)

            def sb_masked(i):
                tb = i // SB_HEADS
                w = META + (tb + 1) * P
                b = filled(dve, f"z{i}")
                count_emptied(stt(zm[i % 2][:, 0:w], b[:, 0:w], SCALE, sbmask[:, tb, 0:w], ALU.mult, ALU.add))

            def sb_shares(i):
                tb = i // SB_HEADS
                w = META + (tb + 1) * P
                if i % SB_HEADS < 2:
                    step(dve.memset(keep[i % 2][:, w:w + 1], 1.0))
                dve.wait_ge(sig_ready, i + 1)
                step(dve.tensor_tensor_scan(zm[i % 2][:, w - 1::-1], keep[i % 2][:, w:0:-1], ones[:, 0:w], 1.0, ALU.mult, ALU.mult))
                tt(beta[i % 2][:, 0:w], beta[i % 2][:, 0:w], zm[i % 2][:, 0:w], ALU.mult).then_inc(w_ready, 1)

            dve.wait_ge(mask_ready, 3)
            for i in range(17):
                if i < 16:
                    if i >= 2:
                        dve.wait_ge(w_ready, i - 1)
                    sb_masked(i)
                if i >= 1:
                    sb_shares(i - 1)

            dve.wait_ge(wT_used, 16)
            for tb in range(TB):
                last = dve.tensor_copy(R[:, tb, 0:HALF], bank[4 + tb][:, :])
            last.then_inc(sb_out, 1)
            for tb in range(TB):
                b = filled(dve, "ohg", tb)
                count_emptied(dve.tensor_copy(R[:, tb, HALF:D], b[:, :]))
            emptied_self()
            for tb in range(TB):
                last = tt(lev[tb][:, :, :].rearrange("p a b -> p (a b)"), R[:, tb, :], R[:, tb, :], ALU.mult)
            step(last)
            for tb in range(TB):
                sq = lev[tb][:, :, :].rearrange("p a b -> p (a b)")
                dve.reduce_sum(sm(30 + 12 * tb, 8), sq[:, 0:HALF].rearrange("p (h d) -> p h d", d=SB_D), axis=AX.X)
                last = dve.reduce_sum(sm(38 + 12 * tb, 4), sq[:, HALF:D].rearrange("p (h d) -> p h d", d=P), axis=AX.X)
            step(last)
            for tb in range(TB):
                ts(sm(30 + 12 * tb, 8), sm(30 + 12 * tb, 8), 1.0 / SB_D, EPS, ALU.mult, ALU.add)
                last = ts(sm(38 + 12 * tb, 4), sm(38 + 12 * tb, 4), 1.0 / P, EPS, ALU.mult, ALU.add)
            last.then_inc(stat_ready, 1)
            dve.wait_ge(sq_ready, 3)
            step(dve.reciprocal(sm(30, 24), sm(30, 24)))
            wait_emptied(dve, "hgg", 1)
            for tb in range(TB):
                for at, n, d, r in ((0, SB_HEADS, SB_D, 30), (HALF, HG_HEADS, P, 38)):
                    v = R[:, tb, at:at + HALF].rearrange("p (h d) -> p h d", d=d)
                    last = tt(v, v, sm(r + 12 * tb, n).unsqueeze(2).broadcast_to([P, n, d]), ALU.mult)
            step(last)
            for tb in range(TB):
                last = tt(R[:, tb, HALF:D], R[:, tb, HALF:D], hgg[:, tb, :], ALU.mult)
            last.then_inc(rows_ready, 1)

            def add_rows(name, scale):
                for n in range(2):
                    for tb in range(TB):
                        b = filled(dve, name, 2 * n + tb)
                        v = X[:, tb, n * HALF:(n + 1) * HALF]
                        count_emptied(stt(v, v, scale, b[:, :], ALU.mult, ALU.add))
                emptied_self()

            def rms(at, k):
                dve.wait_ge(sq_ready, k + 1)
                ts(sm(at + 2, 2), sm(at, 2), 1.0 / D, EPS, ALU.mult, ALU.add).then_inc(stat_ready, 1)
                dve.wait_ge(sq_ready, k + 2)
                step(dve.reciprocal(sm(at + 2, 2), sm(at + 2, 2)))

            add_rows("w_out", 1.0)
            rms(6, 3)
            for tb in range(TB):
                last = ts(R[:, tb, :], X[:, tb, :], sm(8 + tb, 1), None, ALU.mult)
            last.then_inc(rows_ready, 1)

            per_tb = lambda v: v.rearrange("p (b n) -> p b n", b=TB)
            dve.wait_ge(in_small, 16 * 6)
            b = filled(dve, "router")
            rl = per_tb(sm(650, 72))
            count_emptied(tt(rl, per_tb(b[:, 0:128])[:, :, 0:36], bias36[:, :].unsqueeze(1).broadcast_to([P, TB, 36]), ALU.add))
            emptied_self()
            wide = lambda v, n: v.unsqueeze(2).broadcast_to([P, TB, n])
            iota = lambda n: sm(900, n).unsqueeze(1).broadcast_to([P, TB, n])

            def first_best(dst, src, best, n, scratch, index):
                step(tt(per_tb(scratch), src, wide(best, n), ALU.is_lt))
                step(stt(per_tb(scratch), per_tb(scratch), 100.0, iota(n), ALU.mult, ALU.add))
                step(dve.tensor_reduce(index, per_tb(scratch), axis=AX.X, op=ALU.min))
                step(tt(dst, iota(n), wide(index, n), ALU.is_equal))

            step(dve.reduce_max(sm(722, 2), rl[:, :, 0:GROUPS], axis=AX.X))
            tt(per_tb(sm(200, 8)), rl[:, :, 0:GROUPS], wide(sm(722, 2), GROUPS), ALU.subtract).then_inc(router_arg, 1)
            first_best(per_tb(sm(736, 8)), rl[:, :, 0:GROUPS], sm(722, 2), GROUPS, sm(726, 8), sm(734, 2))
            step(ts(sm(736, 8), sm(736, 8), -1.0, -NEG, ALU.add, ALU.mult))
            el = sm(744, 64).rearrange("p (b g e) -> p b g e", b=TB, g=GROUPS)
            for tb in range(TB):
                last = tt(el[:, tb], rl[:, tb, GROUPS:36].rearrange("p (g e) -> p g e", g=GROUPS),
                          sm(736 + 4 * tb, 4).unsqueeze(2).broadcast_to([P, GROUPS, PER_GROUP]), ALU.add)
            step(last)
            elf = per_tb(sm(744, 64))
            step(dve.reduce_max(sm(808, 2), elf, axis=AX.X))
            oh1, oh2 = per_tb(sm(64, 64)), per_tb(sm(128, 64))
            first_best(oh1, elf, sm(808, 2), EXPERTS, sm(128, 64), sm(810, 2))
            step(stt(elf, oh1, 3 * NEG, elf, ALU.mult, ALU.add))
            step(dve.reduce_max(sm(812, 2), elf, axis=AX.X))
            tt(sm(240, 2), sm(812, 2), sm(808, 2), ALU.subtract).then_inc(router_arg, 1)
            first_best(oh2, elf, sm(812, 2), EXPERTS, sm(128, 64), sm(814, 2))
            dve.wait_ge(router_exp, 1)
            step(dve.reduce_sum(sm(816, 2), per_tb(sm(200, 8)), axis=AX.X))
            step(dve.reciprocal(sm(816, 2), sm(816, 2)))
            dve.wait_ge(router_exp, 2)
            step(ts(sm(870, 2), sm(240, 2), 1.0, None, ALU.add))
            step(dve.reciprocal(sm(870, 2), sm(870, 2)))
            step(tt(sm(870, 2), sm(870, 2), sm(816, 2), ALU.mult))
            step(tt(sm(872, 2), sm(870, 2), sm(240, 2), ALU.mult))
            tt(sm(650, 64), sm(64, 64), sm(128, 64), ALU.add).then_inc(gate_ready, 1)
            b = filled(dve, "pos")
            pos = sm(744, 64)
            count_emptied(dve.tensor_copy(sm(744, 96), b[:, 0:96]))
            emptied_self()
            step(dve.reduce_max(sm(840, 1), sm(808, 32), axis=AX.X))
            step(ts(sm(841, 1), sm(840, 1), SLOTS + 0.5, None, ALU.is_ge))
            for c in range(2, PASSES):
                step(stt(sm(841, 1), sm(840, 1), c * SLOTS + 0.5, sm(841, 1), ALU.is_ge, ALU.add))
            dve.tensor_copy(extra[:, :], sm(841, 1)).then_inc(moe["extra_known"], 1)
            step(ts(pos, pos, 1.0, None, ALU.add))
            step(tt(pos, pos, sm(650, 64), ALU.mult))
            step(ts(pos, pos, -1.0, None, ALU.add))

            def picks(experts):
                at = slice(experts.start * SLOTS, experts.stop * SLOTS)
                n = experts.stop - experts.start
                for tb in range(TB):
                    last = tt(pick[:, tb, at].rearrange("p (e s) -> p e s", s=SLOTS),
                              sm(900, SLOTS).unsqueeze(1).broadcast_to([P, n, SLOTS]),
                              pos[:, tb * EXPERTS + experts.start:tb * EXPERTS + experts.stop].unsqueeze(2).broadcast_to([P, n, SLOTS]),
                              ALU.is_equal)
                return last

            picks(slice(0, 2)).then_inc(moe["picks"], 1)
            picks(slice(2, EXPERTS)).then_inc(moe["picks"], 1)
            weight = sm(200, 64)
            for tb in range(TB):
                last = ts(sm(200 + EXPERTS * tb, EXPERTS), sm(64 + EXPERTS * tb, EXPERTS), sm(870 + tb, 1), None, ALU.mult)
            step(last)
            for tb in range(TB):
                at = EXPERTS * tb
                last = stt(sm(200 + at, EXPERTS), sm(128 + at, EXPERTS), sm(872 + tb, 1), sm(200 + at, EXPERTS), ALU.mult, ALU.add)
            step(last)
            b = filled(dve, "cbT")
            count_emptied(dve.tensor_copy(cbias[:, :, :].rearrange("p a b -> p (a b)"), b[:, 0:2 * HEADS * CMP_PAD]))

            gains = cols[:, PACK["g_ffn"][0]:PACK["g_ffn"][0] + KT]

            def take_gathered(j):
                dst = xg[:, :, :].rearrange("p r (k s) -> p k r s", s=SLOTS)
                for r in range(2):
                    last = tt(dst[:, 4 * j:4 * j + 4, r, :],
                              bank[2 + j][:, :].rearrange("p (k r s) -> p k r s", r=2, s=SLOTS)[:, :, r, :],
                              gains[:, 4 * j:4 * j + 4].unsqueeze(2).broadcast_to([P, 4, SLOTS]), ALU.mult)
                return last

            def hidden(e):
                return tt(hid[e % 2], gact[e % 2], bank[e % 2][:, 256:512], ALU.mult)

            def row(e):
                return dve.tensor_copy(yrow[e % 2], bank[e % 2][:, :])

            def gates_of(i):
                for tb in range(TB):
                    last = tt(gated[:, tb, :].rearrange("p (r c s) -> p r c s", r=2, c=2),
                              pair_pick(tb, i).rearrange("p (r s) -> p r s", r=2).unsqueeze(2).broadcast_to([P, 2, 2, SLOTS]),
                              weight[:, bass.ds(i * 2 + tb * EXPERTS, 2)].unsqueeze(2).unsqueeze(3).broadcast_to([P, 2, 2, SLOTS]),
                              ALU.mult)
                return last

            def moe_taken(pair, i):
                dve.wait_ge(moe["gathered"], i + (pair + 1))
                for j in range(2):
                    take_gathered(j).then_inc(moe["taken"], 1)

            def moe_gated(pair, i):
                dve.wait_ge(moe["turned"], i * 2 + 2 * pair)
                gates_of(i + pair).then_inc(moe["gated"], 1)

            def moe_hidden(e, i, first=False):
                dve.wait_ge(moe["silu"], i * 2 + (e + 1))
                if not first:
                    dve.wait_ge(moe["turned"], i * 2 + (e - 1))
                hidden(e).then_inc(moe["hidden"], 1)

            def moe_row(e, i, first=False):
                dve.wait_ge(moe["down"], i * 2 + (e + 1))
                if not first:
                    dve.wait_ge(moe["combined"], i * 2 + (e - 1))
                row(e).then_inc(moe["row"], 1)

            def moe_pair(i, first=False):
                moe_hidden(1, i, first)
                moe_taken(1, i)
                moe_row(0, i, first)
                moe_gated(1, i)
                moe_hidden(2, i)
                moe_row(1, i, first)

            moe_taken(0, 0)
            gates_of(0).then_inc(moe["gated"], 1)
            moe_hidden(0, 0, first=True)
            moe_pair(0, first=True)
            with dve.Fori(1, EXPERTS // 2 - 1) as i:
                moe_pair(i)
            e = EXPERTS - 1
            moe_hidden(e, 0)
            moe_row(e - 1, 0)
            moe_row(e, 0)

            dve.wait_ge(moe["combined"], EXPERTS)
            more = dve.value_load(extra[0:1, 0:1], min_val=0, max_val=PASSES - 1)
            with dve.If(more > 0):
                dve.memset(sm(860, 1), 0.0).then_inc(ov["done"], 1)
                with dve.Fori(0, more) as p:
                    dve.wait_ge(ov["done"], p * EXPERTS + 1)
                    ts(pos, pos, -float(SLOTS), None, ALU.add).then_inc(ov_places, 1)
                    dve.wait_ge(ov_places, p + 1)
                    picks(slice(0, EXPERTS)).then_inc(ov["picks"], 1)
                    with dve.Fori(0, EXPERTS // 2) as i:
                        dve.wait_ge(ov["gathered"], p * (EXPERTS // 2) + i + 1)
                        take_gathered(0)
                        take_gathered(1).then_inc(ov["taken"], 1)
                        dve.wait_ge(ov["picks"], p + 1)
                        dve.wait_ge(ov["done"], p * EXPERTS + i * 2 + 1)
                        gates_of(i).then_inc(ov["gated"], 1)
                        for r in range(2):
                            count = p * EXPERTS + i * 2 + (r + 1)
                            dve.wait_ge(ov["silu"], count)
                            hidden(r).then_inc(ov["hidden"], 1)
                            dve.wait_ge(ov["down"], count)
                            row(r).then_inc(ov["row"], 1)
                dve.wait_ge(ov["done"], more * EXPERTS + 1)
                dve.memset(sm(861, 1), 0.0).then_inc(ov_through, 1)
            dve.wait_ge(sums_ready, 1)
            for tb in range(TB):
                for n in range(2):
                    v = X[:, tb, n * HALF:(n + 1) * HALF]
                    last = tt(v, v, bank[4 + 2 * tb + n][:, :], ALU.add)
            last.then_inc(y_used, 1)

            def add_y(ph, steps, scale):
                dve.wait_ge(phase_sems[ph]["used"], steps)
                for tb in range(TB):
                    for n in range(2):
                        v = X[:, tb, n * HALF:(n + 1) * HALF]
                        last = stt(v, v, scale, bank[4 + 2 * tb + n][:, :], ALU.mult, ALU.add)
                return last

            rms(10, 5)
            dve.wait_ge(rowvec_in, 16)
            for tb in range(TB):
                last = stt(X[:, tb, :], X[:, tb, :], sm(12 + tb, 1), rowvec[:, 0, :], ALU.mult, ALU.mult)
            last.then_inc(ln_done, 1)

            wait_emptied(dve, "a_kv", 0)
            for kv, pe_at in enumerate((PACK["pe_k"][0], PACK["pe_v"][0])):
                v = shift2[:, kv, :]
                v = bass.AP(tensor=v.tensor, offset=v.offset, ap=[list(v.ap[0]), [2, 16], [CMP_STRIDE, N_CMP]])
                last = tt(logit[2][:, kv, 0:16 * N_CMP].rearrange("p (j n) -> p j n", n=N_CMP), v,
                          cols[:, pe_at:pe_at + 16].unsqueeze(2).broadcast_to([P, 16, N_CMP]), ALU.add)
            last.then_inc(cmp_in, 1)
            dve.wait_ge(pool_step, 1)
            wait_emptied(dve, "a_kv", 2)
            for tb in range(TB):
                heads = lambda v: v.rearrange("p (h n) -> p h n", n=CMP_PAD)
                lc = sm(340, HEADS * CMP_PAD)
                b = filled(dve, "cmp_l", tb)
                count_emptied(stt(lc, b[:, 0:HEADS * CMP_PAD], SCALE, cbias[:, tb, :], ALU.mult, ALU.add))
                emptied_self()
                step(dve.reduce_max(sm(564, HEADS), heads(lc), axis=AX.X))
                tt(heads(lc), heads(lc), sm(564, HEADS).unsqueeze(2).broadcast_to([P, HEADS, CMP_PAD]), ALU.subtract).then_inc(cmp_e, 1)
                dve.wait_ge(cmp_e, 2 * tb + 2)
                step(stt(lc, cbias[:, tb, :], NEG / 10, lc, ALU.is_gt, ALU.mult))
                step(dve.reduce_sum(sm(576, HEADS), heads(lc), axis=AX.X))
                step(ts(sm(576, HEADS), sm(576, HEADS), TINY, None, ALU.max))
                step(dve.reciprocal(sm(576, HEADS), sm(576, HEADS)))
                gates = sm(260 + 36 * tb, 36).rearrange("p (h g) -> p h g", g=3)
                step(tt(sm(576, HEADS), sm(576, HEADS), gates[:, :, 0], ALU.mult))
                tt(pc[:, tb, :].rearrange("p (h n) -> p h n", n=32)[:, :, 0:CMP_PAD], heads(lc),
                   sm(576, HEADS).unsqueeze(2).broadcast_to([P, HEADS, CMP_PAD]), ALU.mult).then_inc(cmp_x, 1)
                dve.wait_ge(cmp_x, tb + 1)

            def attend(layer):
                mine = [u for u, key in enumerate(att) if key[0] == layer]

                def biased(u):
                    _, kind, pair, tb, h = att[u]
                    w = width(u)
                    if u >= 3:
                        dve.wait_ge(at_t, u - 2)
                    for seg in range(2):
                        dve.wait_ge(at_l, 2 * u + seg + 1)
                        dst, src = logit[u % 3][:, seg, 0:w], bank[2 * (u % 2) + seg][:, 0:w]
                        if kind == "mem":
                            last = ts(dst, src, SCALE, None, ALU.mult)
                        else:
                            head = h if kind == "nsa" else h + seg
                            last = stt(dst, src, SCALE, btab[:, head, T - w:T], ALU.mult, ALU.add)
                        last.then_inc(at_m, 1)
                    dve.wait_ge(at_m, 2 * u + 2)
                    dve.tensor_reduce(sm(540 + 8 * (u % 3), 2), logit[u % 3][:, :, 0:w], axis=AX.X, op=ALU.max,
                                      negate=True).then_inc(at_x, 1)

                def row_scale(u):
                    _, kind, pair, tb, h = att[u]
                    dve.wait_ge(at_e, u + 1)
                    r = sm(544 + 8 * (u % 3), 2)
                    ins = dve.reciprocal(r, sm(542 + 8 * (u % 3), 2))
                    if kind == "nsa":
                        step(ins)
                        ins = tt(r, r, sm(260 + 36 * tb + 3 * h + 1, 2), ALU.mult)
                    ins.then_inc(at_r, 1)

                def outputs(u):
                    g, _ = group_of(u)
                    if groups[g][-1] != u:
                        return
                    _, kind, pair, _, _ = att[u]
                    dve.wait_ge(at_o, u + 1)
                    k = (PAIRS if kind == "mem" else 0) + pair
                    dve.tensor_copy(mixT[:, k, :], bank[6 + g % 2][:, 0:T]).then_inc(at_oc, 1)

                n = len(mine)
                for i in range(n + 4):
                    if i < n:
                        biased(mine[i])
                    if 1 <= i < n + 1:
                        row_scale(mine[i - 1])
                    if i >= 4:
                        outputs(mine[i - 4])

            def layer_norm(k):
                last = None
                for tb in range(TB):
                    for n in range(2):
                        last = dve.bn_stats(sm(604 + 12 * tb + 6 * n, 6), X[:, tb, n * HALF:(n + 1) * HALF])
                step(last)
                for tb in range(TB):
                    last = dve.bn_aggr(sm(628 + 2 * tb, 2), sm(604 + 12 * tb, 12).rearrange("p (a s) -> p a s", s=6))
                step(last)
                ts(sm(600, 2), sm(628, 4).rearrange("p (b s) -> p b s", s=2)[:, :, 1], LN_EPS, None, ALU.add).then_inc(stat_ready, 1)
                dve.wait_ge(sq_ready, 8 + k)
                step(dve.reciprocal(sm(600, 2), sm(600, 2)))
                dve.wait_ge(rowvec_in, 16 * (3 + 2 * k))
                for tb in range(TB):
                    v = X[:, tb, :]
                    step(ts(v, v, sm(628 + 2 * tb, 1), sm(600 + tb, 1), ALU.subtract, ALU.mult))
                    step(tt(v, v, rowvec[:, 0, :], ALU.mult))
                    tt(v, v, rowvec[:, 1, :], ALU.add).then_inc(ln_done, 1)

            def ffn(layer):
                name = f"ffn{layer}"
                ph = phase_sems[name]
                at_w = PACK_ROWS + layer * CONV_ROWS

                def conv_step(j, k):
                    tap = lambda t, q: cols[:, bass.ds(k * 8 + (at_w + t * FFT + 2 * j + q), 1)]
                    for q in range(2):
                        w, a = work[(2 * j + q) % 4], bank[2 * (j % 2) + q]
                        dve.wait_ge(ph["act"], k * 8 + (2 * j + q + 1))
                        stt(w[:, 1:T], a[:, 0:T - 1], tap(1, q), w[:, 1:T], ALU.mult, ALU.add).then_inc(conv1[name], 1)
                        dve.wait_ge(conv1[name], k * 8 + (2 * j + q + 1))
                        stt(w[:, 2:T], a[:, 0:T - 2], tap(0, q), w[:, 2:T], ALU.mult, ALU.add).then_inc(mulp[name], 1)
                    for q in range(2):
                        dve.wait_ge(act2[name], k * 8 + (2 * j + q + 1))
                        if j >= 1:
                            dve.wait_ge(ph["used"], k * 4 + max(j - 1, 1))
                        tt(hb[j % 2][:, q, :], work[(2 * j + q) % 4], bank[2 * (j % 2) + q][:, T:2 * T], ALU.mult).then_inc(ph["hidden"], 1)

                conv_step(0, 0)
                with dve.Fori(0, 2) as i:
                    for u in range(4):
                        conv_step(u + 1, i)
                for j in (9, 10):
                    conv_step(j, 0)
                step(add_y(name, STEPS_F, ALPHA))

            attend(0)
            add_rows("a_out", ALPHA)
            layer_norm(0)
            ffn(0)
            layer_norm(1)
            attend(1)
            add_rows("b_out", ALPHA)
            layer_norm(2)
            ffn(1)
            layer_norm(3)

        @block.gpsimd
        def _(pool):
            step = chained(pool, pool_chain)

            pool.memset(small[:, :], 1.0).then_inc(pool_const, 1)
            step(pool.memset(ident[:, :], 0.0))
            pool.affine_select(out=ident[:, :], in_=ident[:, :], compare_op=ALU.not_equal, fill=1.0, base=0,
                               pattern=[[-1, P]], channel_multiplier=1).then_inc(pool_const, 1)
            pool.memset(ones[:, :], 1.0).then_inc(pool_const, 1)
            pool.memset(zeros[:, :], 0.0).then_inc(zero_ready, 1)
            step(pool.memset(tri[:, :], 1.0))
            step(pool.affine_select(out=tri[:, :], in_=tri[:, :], compare_op=ALU.is_ge, fill=0.0, base=-1,
                                    pattern=[[1, P]], channel_multiplier=-1))
            pool.wait_ge(pool_const, 3)
            pool.iota(iota_i[:, :], pattern=[[1, SLOTS]], base=0, channel_multiplier=0).then_inc(iota_done, 1)
            pool.wait_ge(iota_done, 1)
            step(pool.tensor_copy(sm(900, SLOTS), iota_i[:, :]))
            for level in range(7):
                half = P >> (level + 1)
                nb = P // (2 * half)
                v = level_maskf[:, :].rearrange("p (b r) -> p b r", b=nb)
                step(pool.memset(level_maskf[:, :], 1.0))
                for base, pattern, mult in ((0, [[-2 * half, nb], [0, 2 * half]], 1),
                                            (half - 1, [[2 * half, nb], [0, 2 * half]], -1),
                                            (-half, [[0, nb], [1, 2 * half]], 0)):
                    step(pool.affine_select(out=v, in_=v, compare_op=ALU.is_ge, fill=0.0, base=base,
                                            pattern=pattern, channel_multiplier=mult))
                step(pool.tensor_copy(level_mask[:, level, :], level_maskf[:, :]))
            step(pool.tensor_copy(level_mask[:, 7, :], ident[:, :]))
            wait_emptied(pool, "pack")
            pool.memset(score[:, :, :], 0.0).then_inc(mask_ready, 1)

            wait_emptied(pool, "dist", 1)
            pool.dma_start(by_dist, dist_out).then_inc(dist_stored, 16)
            pool.wait_ge(dist_stored, 16)
            row = DIST_REV + DIST_FWD
            pool.dma_start(by_token, bass.AP(tensor=by_dist.tensor, offset=P - 1,
                                             ap=[[row, HEADS], [-1, P], [1, T]])).then_inc(expanded, 16)
            pool.dma_start(by_block, bass.AP(tensor=by_dist.tensor, offset=DIST_REV + FWD_ZERO - (CMP_LEN - 1),
                                             ap=[[row, HEADS], [-CMP_STRIDE, CMP_PAD], [1, T]])).then_inc(expanded, 16)
            pool.wait_ge(job_done, jobs.number("aT", KT - 1) + 1)
            step(pool.memset(sbmask[:, :, :], 0.0))
            for tb in range(TB):
                v = sbmask[:, tb, META:S1]
                pool.affine_select(out=v, in_=v, compare_op=ALU.is_ge, fill=NEG, base=tb * P - 1,
                                   pattern=[[-1, T]], channel_multiplier=1).then_inc(mask_ready, 1)

            pool.wait_ge(job_done, jobs.number("mT", 3) + 1)
            pool.wait_ge(rows_ready, 2)
            pool.wait_ge(expanded, 32)
            pool.dma_start(btab[:, :, :], by_token.rearrange("h p j -> p h j")).then_inc(tables_in, 16)
            blocks_flat = by_block.rearrange("h n t -> (h n) t")
            pool.dma_start(ctmp[:, 0, :], blocks_flat[0:P, :]).then_inc(tables_in, 16)
            pool.dma_start(ctmp[0:64, 1, :], blocks_flat[P:P + 64, :]).then_inc(tables_in, 16)

            def load_rowvec(*vectors):
                for i, v in enumerate(vectors):
                    src = bass.AP(tensor=v.tensor, offset=v.offset, ap=[[0, P], [1, D]])
                    pool.dma_start(rowvec[:, i, :], src).then_inc(rowvec_in, 16)

            load_rowvec(g_final)

            pool.wait_ge(y_used, 1)
            for t in (pc, vz, hidT):
                pool.memset(t[:, :, :], 0.0)
            pool.memset(kz[:, :, :], 0.0).then_inc(pool_step, 1)
            pool.wait_ge(ln_done, 1)
            load_rowvec(ln1_g_2[0], ln1_b_2[0])

            def attend(layer):
                for u in [u for u, key in enumerate(att) if key[0] == layer]:
                    pool.wait_ge(at_r, u + 1)
                    w = width(u)
                    v = logit[u % 3][:, :, 0:w]
                    pool.tensor_tensor(v, v, sm(544 + 8 * (u % 3), 2).unsqueeze(2).broadcast_to([P, 2, w]), ALU.mult).then_inc(at_p, 1)

            attend(0)
            pool.wait_ge(ln_done, 3)
            load_rowvec(ln2_g_2[0], ln2_b_2[0])
            pool.wait_ge(ln_done, 5)
            load_rowvec(ln1_g_2[1], ln1_b_2[1])
            attend(1)
            pool.wait_ge(ln_done, 7)
            load_rowvec(ln2_g_2[1], ln2_b_2[1])
    return nc


_INS = ("x", "meta_tokens", "lb_logits", "g_mix", "w_in", "sb_gain", "hg_gain", "w_out", "g_ffn", "w_router_group",
        "b_router_group", "w_router_expert", "b_router_expert", "w_expert_gate", "w_expert_up", "w_expert_down",
        "g_final", "mem_2", "rel_bias_2", "a_w_in_2", "a_cmp_pe_k_2", "a_cmp_w1_k_2", "a_cmp_w2_k_2", "a_cmp_pe_v_2",
        "a_cmp_w1_v_2", "a_cmp_w2_v_2", "a_w_mem_kv_2", "a_w_out_2", "shared_w_kv_2", "b_w_in_2", "b_w_mem_kv_2",
        "b_w_out_2", "ln1_g_2", "ln1_b_2", "ln2_g_2", "ln2_b_2", "ffn_w_in_2", "ffn_conv_w_2", "ffn_conv_b_2",
        "ffn_w_out_2")


def kernel(**inputs):
    import numpy as _np
    import concourse.bacc as _bacc
    from concourse import mybir as _mybir
    from concourse.bass_utils import run_bass_kernel_spmd as _run

    nc = _bacc.Bacc("TRN2", target_bir_lowering=False, num_devices=1)
    arrays, args = {}, {}
    for name in _INS + ("dist_onehot",):
        a = bucket_table() if name == "dist_onehot" else _np.ascontiguousarray(inputs[name])
        arrays[f"in_{name}"] = a
        args[name] = nc.dram_tensor(f"in_{name}", a.shape, _mybir.dt.from_np(a.dtype), kind="ExternalInput").ap()
    args["out"] = nc.dram_tensor("out_0", (1, T, D), F32, kind="ExternalOutput").ap()
    build(nc, **args)
    r = _run(nc, [arrays], core_ids=[0])
    return r.results[0]["out_0"]
```

```python
from contextlib import ExitStack

import concourse.bass as bass
import numpy as np
from concourse import mybir

F32 = mybir.dt.float32
BF16 = mybir.dt.bfloat16
U8 = mybir.dt.uint8
I32 = mybir.dt.int32
ALU = mybir.AluOpType
ACT = mybir.ActivationFunctionType
AX = mybir.AxisListType

P = 128
T = 256
TB = T // P
D = 1024
KT = D // P
META = 16
S1 = META + T
UNIT = 4096
RING = 6
HALF = 512

SB_HEADS, SB_D = 8, 64
HG_HEADS = 4
GROUPS, PER_GROUP = 4, 8
EXPERTS = GROUPS * PER_GROUP
FF_E = 512

HEADS, HD = 12, 64
PAIRS = HEADS // 2
MEM = 256
MEM_PAIRS = 2
SCALE = HD ** -0.5
CMP_LEN, CMP_STRIDE, CMP_HID = 32, 16, 256
N_CMP = (T - CMP_LEN) // CMP_STRIDE + 1
CMP_PAD = 16
BUCKETS, MAX_DIST = 32, 128
D_FF = 2816
FFT = D_FF // P
STEPS_F = FFT // 2
SLOTS = 64
PASSES = T // SLOTS
ALPHA = 4.0 ** 0.25
EPS, LN_EPS = 1e-6, 1e-5
NEG = -1e30
TINY = 1e-30
ARENA = 13700
HG_OUT = (4, 8)
LOGITS = 4
A_CUTS = (0, 512, 960, 1444)

DIST_REV = 384
DIST_FWD = 512
FWD_ZERO = (CMP_PAD - 1) * CMP_STRIDE + CMP_LEN - 1

PACK = {"g_mix": (0, 8), "g_ffn": (8, 8), "lb": (16, 8), "sb_gain": (24, 4), "hg_gain": (28, 4),
        "pe_k": (32, 16), "pe_v": (48, 16), "conv_b": (64, 44), "g_final": (108, 8)}
PACK_ROWS = 116
CONV_ROWS = 3 * FFT
LAYER_PACK = {"ln1_g": (CONV_ROWS, 8), "ln1_b": (CONV_ROWS + 8, 8), "ln2_g": (CONV_ROWS + 16, 8), "ln2_b": (CONV_ROWS + 24, 8)}
LAYER_ROWS = CONV_ROWS + 32


def bucket_table():
    def rows(dist):
        n = np.maximum(dist, 0)
        half = BUCKETS // 2
        nf = np.maximum(n, 1).astype(np.float32)
        large = half + (np.log(nf / half) / np.float32(np.log(MAX_DIST / half)) * (BUCKETS - half)).astype(np.int32)
        bucket = np.where(n < half, n, np.minimum(large, BUCKETS - 1))
        out = np.zeros((BUCKETS + 1, len(dist)), np.float32)
        out[bucket, np.arange(len(dist))] = dist >= 0
        out[BUCKETS] = dist < 0
        return out
    return np.concatenate([rows(T - 1 - np.arange(DIST_REV)), rows(np.arange(DIST_FWD) - FWD_ZERO)], 1)


def ring_units():
    order = [("mem_kv_a", 0), ("mem_kv_b", 0)]
    order += [("w_in", c) for c in (4, 3, 5, 6, 0, 1, 2)]
    order += [("w_out", c) for c in range(2)]
    first = {"moe": len(order)}
    order += [(w, e) for e in range(EXPERTS) for w in ("gate", "up", "down")]
    order += [("a_in", c) for c in range(3)] + [("cmp_k", 0), ("cmp_v", 0)]
    order += [("a_out", c) for c in range(2)]

    def ffn(layer):
        first[f"ffn{layer}"] = len(order)
        for j in range(0, STEPS_F - 1, 2):
            order.extend([(f"ffn_in{layer}", j), (f"ffn_in{layer}", j + 1), (f"ffn_out{layer}", j // 2)])
        order.extend([(f"ffn_in{layer}", STEPS_F - 1), (f"ffn_out{layer}", STEPS_F // 2)])

    ffn(0)
    order += [("kv", c) for c in range(3)] + [("b_in", c) for c in range(2)] + [("b_out", c) for c in range(2)]
    ffn(1)
    return order, first


class Jobs:

    def __init__(self, banks):
        self.jobs, self.at, self.banks = [], {}, banks

    def add(self, name, engine, n):
        self.at[name] = len(self.jobs)
        self.jobs += [engine] * n

    def add_part(self, name, i, engine):
        self.at[name, i] = len(self.jobs)
        self.jobs.append(engine)

    def number(self, name, i=0):
        return self.at[name, i] if (name, i) in self.at else self.at[name] + i

    def bank(self, name, i=0):
        return self.number(name, i) % self.banks

    def emptied(self, number):
        e = self.jobs[number]
        return e, self.jobs[:number + 1].count(e)


def first_block_order():
    return [("hgg", 0), ("kmT", 0), ("s0", 0), ("hgg", 1), ("k1T", 0), ("s1", 0),
            ("sbq", 0), ("level", 0), ("sbq", 1), ("level", 1), ("sbk", 0), ("level", 2), ("sbk", 1), ("level", 3),
            ("sbk", 2), ("level", 4), ("sbk", 3), ("level", 5), ("sbv", 0), ("level", 6), ("sbv", 1), ("level", 7),
            ("sbv", 2)]


def plan_jobs():
    j = Jobs(4)
    j.add("memT", "A", 4)
    j.add("mem_a", "A", 2)
    j.add("mem_b", "A", 2)
    j.add("pack", "A", 1)
    j.add("dist", "A", 2)
    j.add("aT", "V", KT)
    j.add("hgf", "A", 4)
    j.add("hgq", "A", 2)
    j.add("hgi", "A", 3)
    for what, i in first_block_order():
        if what in ("kmT", "s0", "k1T", "s1"):
            j.add(what, "V" if what == "s1" else "A", 1)
        elif what == "level":
            j.add(f"level{i}", "V", 2)
        else:
            j.add_part(what, i, "A")
    for i in range(16 + 2):
        if i < 16:
            j.add(f"z{i}", "V", 1)
        if i >= 2:
            j.add(f"wT{i - 2}", "A", 1)
        if i in HG_OUT:
            j.add_part("ohg", HG_OUT.index(i), "V")
    j.add("mT", "A", 4)
    j.add("w_out", "V", 4)
    j.add("cbT", "A", 1)
    j.add("x2T", "A", 3)
    j.add("x2T_last", "V", 1)
    j.add("router", "V", 1)
    j.add("pos", "V", 1)
    j.add("xTa", "A", 3)
    j.add("xTa_last", "V", 1)
    j.add("a_q", "A", 3)
    j.add("a_kv", "A", 2)
    j.add("a_v", "A", 1)
    j.add("cmp_h", "A", 1)
    j.add("cmp_hT", "A", 2)
    j.add("cmp_kv", "A", 1)
    j.add("cmp_l", "V", 2)
    j.add("a_qm", "A", 1)
    j.add("cmp_pT", "A", 2)
    j.add("a_out", "V", 4)
    j.add("xTf0", "A", 3)
    j.add("xTf0_last", "V", 1)
    j.add("xTb", "A", 3)
    j.add("xTb_last", "V", 1)
    j.add("b_k", "A", 3)
    j.add("b_v", "A", 4)
    j.add("b_q", "A", 3)
    j.add("b_qm", "A", 1)
    j.add("b_out", "V", 4)
    j.add("xTf1", "A", 3)
    j.add("xTf1_last", "V", 1)
    return j


def attention_units():
    units = []
    for layer in range(2):
        for pair in range(PAIRS):
            for tb in range(TB):
                if layer == 0:
                    units += [(layer, "nsa", pair, tb, 2 * pair + r) for r in range(2)]
                else:
                    units.append((layer, "moba", pair, tb, 2 * pair))
        for pair in range(MEM_PAIRS):
            units += [(layer, "mem", pair, tb, 2 * pair) for tb in range(TB)]
    return units


def build(nc, x, meta_tokens, lb_logits, g_mix, w_in, sb_gain, hg_gain, w_out, g_ffn, w_router_group,
          b_router_group, w_router_expert, b_router_expert, w_expert_gate, w_expert_up, w_expert_down,
          g_final, mem_2, rel_bias_2, a_w_in_2, a_cmp_pe_k_2, a_cmp_w1_k_2, a_cmp_w2_k_2, a_cmp_pe_v_2,
          a_cmp_w1_v_2, a_cmp_w2_v_2, a_w_mem_kv_2, a_w_out_2, shared_w_kv_2, b_w_in_2, b_w_mem_kv_2,
          b_w_out_2, ln1_g_2, ln1_b_2, ln2_g_2, ln2_b_2, ffn_w_in_2, ffn_conv_w_2, ffn_conv_b_2,
          ffn_w_out_2, dist_onehot, out):
    units, first_unit = ring_units()
    jobs = plan_jobs()
    att = attention_units()

    with ExitStack() as ctx:
        def sb(name, shape, dt=F32):
            return ctx.enter_context(nc.sbuf_tensor(name, shape, dt))

        def sem(name):
            return ctx.enter_context(nc.semaphore(name))

        bank = [ctx.enter_context(nc.psum_tensor(f"bank{i}", [P, HALF], F32)) for i in range(8)]

        ring = sb("ring", [P, RING, UNIT])
        X = sb("X", [P, TB, D])
        R = sb("R", [P, TB, D])
        XT = sb("XT", [P, KT, S1])
        rowvec = sb("rowvec", [P, 2, D])
        km = [sb(f"km{i}", [P, 2, MEM]) for i in range(2)]
        vm = [sb(f"vm{i}", [P, 2, MEM]) for i in range(2)]
        ident = sb("ident", [P, P])
        ones = sb("ones", [P, S1])
        zeros = sb("zeros", [P, HALF], BF16)
        level_mask = sb("level_mask", [P, 8, P], U8)
        level_maskf = sb("level_maskf", [P, P])
        cols = sb("cols", [P, PACK_ROWS + 2 * LAYER_ROWS])
        small = sb("small", [P, 964])
        tri = sb("tri", [P, P])
        extra = sb("extra", [P, 1], I32)
        iota_i = sb("iota_i", [P, SLOTS], mybir.dt.int32)
        bias36 = sb("bias36", [P, 36])
        w_router = sb("w_router", [P, KT, 36])
        w2 = sb("w2", [P, 2, 2, HD])
        arena = sb("arena", [P, ARENA])

        def view(at, n, *dims):
            v = arena[:, at:at + n]
            if len(dims) == 2:
                return v.rearrange("p (a b) -> p a b", b=dims[1])
            if len(dims) == 3:
                return v.rearrange("p (a b c) -> p a b c", b=dims[1], c=dims[2])
            return v

        used = [0]

        def take(n, *dims):
            used[0] += n
            assert used[0] <= ARENA, used
            return view(used[0] - n, n, *dims)

        hgk = take(4 * S1, 4, S1)
        logf = take(4 * S1, 4, S1)
        hgq = take(4 * T, 4, T)
        bcum = take(4 * T, 4, T)
        bmeta = take(64, 4, META)
        fmeta = take(64, 4, META)
        at_lev = used[0]
        lev = [take(4 * T, 4, T) for _ in range(2)]
        at_score = used[0]
        score = take(8 * P, 8, P)
        at_hgi = used[0]
        hgi = take(3 * HALF, 3, HALF)
        hgg = take(2 * HALF, 2, HALF)
        S0 = take(HALF)
        S1t = take(HALF)
        sbk = take(4 * S1, 4, S1)
        at_beta = used[0]
        beta = [take(S1) for _ in range(2)]
        keep = [take(S1 + 1) for _ in range(2)]
        meta = arena[0:META, at_beta:at_beta + D]
        pack = view(at_score, 3 * P, 3, P)
        junk = view(at_lev, D)
        zm = [view(at_lev + 4 * T + i * S1, S1) for i in range(2)]
        rflat = R[:, :, :].rearrange("p a b -> p (a b)")
        sbq = rflat[:, 0:4 * T].rearrange("p (a b) -> p a b", b=T)
        sbmask = rflat[:, 4 * T:4 * T + 2 * S1].rearrange("p (a b) -> p a b", b=S1)
        wTs = [view(at_lev + 4 * T + 2 * S1, 3 * P), rflat[:, 4 * T + 2 * S1:4 * T + 2 * S1 + 3 * P]]
        vflat = rowvec[:, :, :].rearrange("p a b -> p (a b)")
        sbv = vflat[:, 0:3 * HALF].rearrange("p (a b) -> p a b", b=HALF)
        kT_rows = vflat[:, 3 * HALF:4 * HALF]
        dist_sb = arena[0:BUCKETS + 1, at_hgi:at_hgi + DIST_REV + DIST_FWD]
        dist_rel = arena[0:BUCKETS + 1, at_hgi + 900:at_hgi + 900 + HEADS]
        dist_out = arena[0:HEADS, at_hgi + 1000:at_hgi + 1000 + DIST_REV + DIST_FWD]

        used[0] = 0
        btab = take(HEADS * T, HEADS, T)
        cbias = take(2 * HEADS * CMP_PAD, 2, HEADS * CMP_PAD)
        at_hb = used[0]
        hb = [take(2 * T, 2, T) for _ in range(2)]
        work = [take(T) for _ in range(4)]
        ctmp = view(at_hb, 2 * T, 2, T)
        late = used[0]
        used[0] = at_hb + 2 * T
        pick = take(TB * EXPERTS * SLOTS, TB, EXPERTS * SLOTS)
        xg = take(2 * KT * SLOTS, 2, KT * SLOTS)
        gact = [take(256) for _ in range(2)]
        hid = [take(256) for _ in range(2)]
        turned_sb = [take(HALF) for _ in range(2)]
        hidden_T = [v[:, 0:256] for v in turned_sb]
        give = [v[:, 256:HALF] for v in turned_sb]
        gated = take(TB * 4 * SLOTS, TB, 4 * SLOTS)
        yrow = [take(HALF) for _ in range(2)]
        used[0] = late
        qT = take(6 * T, 6, T)
        qmT = take(2 * T, 2, T)
        at_k = used[0]
        kT = take(6 * T, 6, T)
        at_v = used[0]
        vrow = take(2 * 768, 2, 768)
        logit = [take(2 * T, 2, T) for _ in range(LOGITS)]
        at_pT = used[0]
        pT = [take(4 * P) for _ in range(2)]
        vrow0 = view(at_v, 2 * P, 2, P)
        pcT = view(at_v + 2 * P, 3 * T, 3, T)
        vz = view(at_v + 2 * P + 3 * T, 4 * HD, 4, HD)
        pc = view(at_k + 2 * T, 2 * HEADS * 32, 2, HEADS * 32)
        hidT = view(at_k + 2 * T + 768, 4 * 32, 4, 32)
        kz = view(at_k + 2 * T + 896, 2 * CMP_PAD, 2, CMP_PAD)
        hrow = logit[0][:, 0, :]
        shift2 = view(at_pT, 2 * T, 2, T)
        mixT = XT[:, :, 0:T]
        memT = XT[:, :, 0:MEM]

        by_dist = nc.dram_tensor("by_dist", [HEADS, DIST_REV + DIST_FWD], F32).ap()
        by_token = nc.dram_tensor("by_token", [HEADS, P, T], F32).ap()
        by_block = nc.dram_tensor("by_block", [HEADS, CMP_PAD, T], F32).ap()
        expanded = sem("expanded")

        landed = [sem(f"landed{i}") for i in range(RING)]
        in_x, in_mem, in_small, in_dist = sem("in_x"), sem("in_mem"), sem("in_small"), sem("in_dist")
        in_pack = sem("in_pack")
        pool_const = sem("pool_const")
        pool_step, pool_chain, iota_done = sem("pool_step"), sem("pool_chain"), sem("iota_done")
        dve_step, act_step = sem("dve_step"), sem("act_step")
        job_done = sem("job_done")
        emptied_a, emptied_v = sem("emptied_a"), sem("emptied_v")
        dist_ready, dist_stored, tables_in = sem("dist_ready"), sem("dist_stored"), sem("tables_in")
        rows_ready = sem("rows_ready")
        sq_ready = sem("sq_ready")
        stat_ready = sem("stat_ready")
        lbound_ready = sem("lbound_ready")
        hg_sig, hg_f, hg_log, hg_q = sem("hg_sig"), sem("hg_f"), sem("hg_log"), sem("hg_q")
        hg_arg, hg_exp, hg_fac = sem("hg_arg"), sem("hg_exp"), sem("hg_fac")
        sig_ready, w_ready = sem("sig_ready"), sem("w_ready")
        wT_used = sem("wT_used")
        router_arg, router_exp = sem("router_arg"), sem("router_exp")
        moe = {k: sem(f"moe_{k}") for k in ("picks", "gathered", "taken", "gate", "up", "silu", "hidden", "turned",
                                            "turned_copied", "down", "row", "extra_known", "gated", "combined")}
        ov = {k: sem(f"over_{k}") for k in ("picks", "loaded", "gathered", "taken", "up", "silu", "hidden", "turned",
                                            "turned_copied", "down", "row", "gated", "done")}
        ov_places, ov_through = sem("over_places"), sem("over_through")
        sums_ready = sem("sums_ready")
        phase_sems = {}
        for ph in ("ffn0", "ffn1"):
            phase_sems[ph] = {k: sem(f"{ph}_{k}") for k in ("tile", "act", "hidden", "used", "first")}
        act2 = {ph: sem(f"{ph}_gelu") for ph in ("ffn0", "ffn1")}
        mulp = {ph: sem(f"{ph}_mul") for ph in ("ffn0", "ffn1")}
        rowvec_in = sem("rowvec_in")
        ln_done, normed = sem("ln_done"), sem("normed")
        mask_ready = sem("mask_ready")
        conv1 = {ph: sem(f"{ph}_conv1") for ph in ("ffn0", "ffn1")}
        y_used = sem("y_used")
        gate_ready = sem("gate_ready")
        cmp_in, cmp_x, cmp_e = sem("cmp_in"), sem("cmp_x"), sem("cmp_e")
        at_l, at_m, at_x, at_e, at_r, at_p, at_t, at_tc, at_o, at_oc = (
            sem("at_logits"), sem("at_biased"), sem("at_max"), sem("at_exp"), sem("at_scale"), sem("at_probs"),
            sem("at_trans"), sem("at_transcopied"), sem("at_out"), sem("at_outcopied"))
        stored = sem("stored")
        zero_ready = sem("zero_ready")

        def weights(n):
            return ring[:, n % RING, :]

        w_at = {}
        for n, key in enumerate(units):
            w_at[key] = n

        def arrivals(n):
            return 32 if units[n][0][:-1] == "ffn_in" else 16

        def use_count(n):
            return sum(arrivals(m) for m in range(n % RING, n + 1, RING))

        emptied = {"A": emptied_a, "V": emptied_v}

        def to_fill(pe, name, i=0):
            n = jobs.number(name, i)
            if n >= jobs.banks:
                engine, count = jobs.emptied(n - jobs.banks)
                pe.wait_ge(emptied[engine], count)
            return bank[n % jobs.banks]

        def filled(engine, name, i=0):
            n = jobs.number(name, i)
            engine.wait_ge(job_done, n + 1)
            return bank[n % jobs.banks]

        def wait_emptied(engine, name, i=0):
            who, count = jobs.emptied(jobs.number(name, i))
            engine.wait_ge(emptied[who], count)

        def wait_weights(pe, key):
            n = w_at[key]
            pe.wait_ge(landed[n % RING], use_count(n))
            return ring[:, n % RING, :]

        def chained(engine, semaphore):
            count = [0]

            def step(instruction):
                count[0] += 1
                instruction.then_inc(semaphore, 1)
                engine.wait_ge(semaphore, count[0])
            return step

        def width(u):
            _, kind, _, tb, _ = att[u]
            return MEM if kind == "mem" else P * (tb + 1)

        def halves_by(u):
            return sum(1 if key[1] == "nsa" else 2 for key in att[:u + 1])

        groups = []
        for u, key in enumerate(att):
            if not groups or att[groups[-1][-1]][:3] != key[:3]:
                groups.append([])
            groups[-1].append(u)

        def group_of(u):
            g = next(g for g, members in enumerate(groups) if u in members)
            return g, groups[g][0] == u

        def sm(at, n):
            return small[:, at:at + n]

        def pair_pick(tb, i):
            return pick[:, tb, bass.ds(i * (2 * SLOTS), 2 * SLOTS)]

        def xg_tile(r, k):
            return xg[:, r, k * SLOTS:(k + 1) * SLOTS]

        block = ctx.enter_context(nc.Block())

        @block.sync
        def _(sp):
            kmaj = lambda w: w.rearrange("(k p) n -> p k n", p=P)
            simple = {
                "mem_kv_a": lambda c: kmaj(a_w_mem_kv_2[0]),
                "mem_kv_b": lambda c: kmaj(b_w_mem_kv_2[0]),
                "w_in": lambda c: kmaj(w_in[0, :, c * HALF:(c + 1) * HALF]),
                "w_out": lambda c: kmaj(w_out[0, :, c * HALF:(c + 1) * HALF]),
                "a_in": lambda c: kmaj(a_w_in_2[0, :, A_CUTS[c]:A_CUTS[c + 1]]),
                "cmp_k": lambda c: kmaj(a_cmp_w1_k_2[0]),
                "cmp_v": lambda c: kmaj(a_cmp_w1_v_2[0]),
                "a_out": lambda c: kmaj(a_w_out_2[0, :, c * HALF:(c + 1) * HALF]),
                "kv": lambda c: kmaj(shared_w_kv_2[:, c * HALF:(c + 1) * HALF]),
                "b_in": lambda c: kmaj(b_w_in_2[0, :, c * HALF:(c + 1) * HALF]),
                "b_out": lambda c: kmaj(b_w_out_2[0, :, c * HALF:(c + 1) * HALF]),
            }

            def slot(n, a, b):
                return ring[:, n % RING, 0:a * b].rearrange("p (a b) -> p a b", b=b)

            last_job = {("mem_kv_a", 0): ("mem_a", 1), ("mem_kv_b", 0): ("mem_b", 1),
                        ("cmp_k", 0): ("cmp_h", 0), ("cmp_v", 0): ("cmp_h", 0)}
            for c, job in ((4, ("hgf", 3)), (3, ("hgq", 1)), (5, ("hgi", 2)), (6, ("hgg", 1)), (0, ("sbq", 1)),
                           (1, ("sbk", 3)), (2, ("sbv", 2))):
                last_job["w_in", c] = job
            for c, job in ((0, ("a_q", 1)), (1, ("a_kv", 1)), (2, ("a_qm", 0))):
                last_job["a_in", c] = job
            for c, job in ((0, ("b_k", 1)), (1, ("b_v", 1)), (2, ("b_v", 3))):
                last_job["kv", c] = job
            for c, job in ((0, ("b_q", 1)), (1, ("b_qm", 0))):
                last_job["b_in", c] = job
            for c in range(2):
                for w in ("w_out", "a_out", "b_out"):
                    last_job[w, c] = (w, 2 + c)

            def wait_read(n):
                what, c = units[n]
                if (what, c) in last_job:
                    sp.wait_ge(job_done, jobs.number(*last_job[what, c]) + 1)
                elif what in experts:
                    sp.wait_ge(moe[what], c + 1)
                elif what[:-1] == "ffn_in":
                    sp.wait_ge(phase_sems["ffn" + what[-1]]["tile"], 2 * c + 2)
                else:
                    sp.wait_ge(phase_sems["ffn" + what[-1]]["used"], min(2 * c + 2, STEPS_F))

            def load(n):
                what, c = units[n]
                if n >= RING:
                    wait_read(n - RING)
                if what[:-1] == "ffn_in":
                    w = ffn_w_in_2[int(what[-1])].rearrange("(k p) (h n) -> p k h n", p=P, h=2)
                    dst = ring[:, n % RING, :].rearrange("p (k h n) -> p k h n", h=2, n=256)
                    for h in range(2):
                        sp.dma_start(dst[:, :, h, :], w[:, :, h, c * 256:(c + 1) * 256]).then_inc(landed[n % RING], 16)
                    return
                elif what[:-1] == "ffn_out":
                    rows = slice(c * 4 * P, min((c + 1) * 4 * P, D_FF))
                    src = kmaj(ffn_w_out_2[int(what[-1]), rows, :])
                    dst = slot(n, src.shape[1], src.shape[2])
                elif what in experts:
                    src = kmaj(experts[what][0, c])
                    dst = slot(n, src.shape[1], src.shape[2])
                else:
                    src = simple[what](c)
                    dst = slot(n, src.shape[1], src.shape[2])
                sp.dma_start(dst, src).then_inc(landed[n % RING], 16)

            experts = {"gate": w_expert_gate, "up": w_expert_up, "down": w_expert_down}

            sp.dma_start(R[:, :, :], mem_2[0].rearrange("(b p) d -> p b d", p=P)).then_inc(in_mem, 16)
            load(0)
            sp.dma_start(X[:, :, :], x[0].rearrange("(b p) d -> p b d", p=P)).then_inc(in_x, 16)
            sp.dma_start(meta[:, :], meta_tokens).then_inc(in_x, 16)
            packed = [(g_mix, "l (t p) -> (l t) p", "g_mix"), (g_ffn, "l (t p) -> (l t) p", "g_ffn"),
                      (lb_logits, "l (t p) -> (l t) p", "lb"), (sb_gain, "l (t p) -> (l t) p", "sb_gain"),
                      (hg_gain, "l (t p) -> (l t) p", "hg_gain"), (ffn_conv_b_2, "l (t p) -> (l t) p", "conv_b"),
                      (g_final, "(t p) -> t p", "g_final")]
            for v, how, name in packed:
                at, n = PACK[name]
                sp.dma_start(pack[at:at + n, 0, :], v.rearrange(how, p=P)).then_inc(in_pack, 16)
            for v, name in ((a_cmp_pe_k_2, "pe_k"), (a_cmp_pe_v_2, "pe_v")):
                at, n = PACK[name]
                sp.dma_start(pack[at:at + n, 0, :], v[0].rearrange("(j l) d -> j (l d)", l=2)).then_inc(in_pack, 16)
            for layer in range(2):
                sp.dma_start(pack[0:CONV_ROWS, 1 + layer, :],
                             ffn_conv_w_2[layer].rearrange("k (t p) -> (k t) p", p=P)).then_inc(in_pack, 16)
                for v, name in ((ln1_g_2, "ln1_g"), (ln1_b_2, "ln1_b"), (ln2_g_2, "ln2_g"), (ln2_b_2, "ln2_b")):
                    at, n = LAYER_PACK[name]
                    sp.dma_start(pack[at:at + n, 1 + layer, :], v[layer].rearrange("(t p) -> t p", p=P)).then_inc(in_pack, 16)
            sp.dma_start(dist_sb, dist_onehot).then_inc(in_dist, 16)
            sp.dma_start(dist_rel[0:BUCKETS, :], rel_bias_2).then_inc(in_dist, 16)
            load(1)
            load(2)
            sp.dma_start(w_router[:, :, 0:GROUPS], kmaj(w_router_group[0])).then_inc(in_small, 16)
            sp.dma_start(w_router[:, :, GROUPS:36], kmaj(w_router_expert[0])).then_inc(in_small, 16)
            for v, at, n in ((b_router_group, 0, GROUPS), (b_router_expert, GROUPS, EXPERTS)):
                sp.dma_start(bias36[:, at:at + n], bass.AP(tensor=v.tensor, offset=v.offset, ap=[[0, P], [1, n]])).then_inc(in_small, 16)
            for kv, v in enumerate((a_cmp_w2_k_2, a_cmp_w2_v_2)):
                sp.dma_start(w2[:, kv, :, :], kmaj(v[0])).then_inc(in_small, 16)
            for n in range(3, first_unit["moe"]):
                load(n)

            base = first_unit["moe"]
            for n in range(base, base + 6):
                load(n)
            with sp.Fori(1, EXPERTS // 2) as i:
                for u in range(6):
                    n = base + u
                    w = (w_expert_gate, w_expert_up, w_expert_down)[u % 3]
                    rows = w.shape[2]
                    src = w[0].rearrange("e k n -> (e k) n")[bass.ds(i * (2 * rows) + (u // 3) * rows, rows), :]
                    sp.wait_ge(moe[("gate", "up", "down")[u % 3]], i * 2 + (u // 3 - 1))
                    src = kmaj(src)
                    sp.dma_start(slot(n, src.shape[1], src.shape[2]), src).then_inc(landed[n % RING], 16)
            sp.wait_ge(moe["extra_known"], 1)
            more = sp.value_load(extra[0:1, 0:1], min_val=0, max_val=PASSES - 1)
            with sp.If(more > 0):
                for k in ("gate", "up", "down"):
                    sp.wait_ge(moe[k], EXPERTS)
                with sp.Fori(0, more) as p:
                    with sp.Fori(0, EXPERTS // 2) as i:
                        sp.wait_ge(ov["done"], p * EXPERTS + i * 2 + 1)
                        for u in range(6):
                            w = (w_expert_gate, w_expert_up, w_expert_down)[u % 3]
                            rows = w.shape[2]
                            src = kmaj(w[0].rearrange("e k n -> (e k) n")[bass.ds(i * (2 * rows) + (u // 3) * rows, rows), :])
                            sp.dma_start(slot(base + u, src.shape[1], src.shape[2]), src).then_inc(ov["loaded"], 16)
                sp.wait_ge(ov_through, 1)
            for n in range(base + 3 * EXPERTS, len(units)):
                load(n)
            for tb in range(TB):
                sp.wait_ge(ln_done, 8 + tb)
                sp.dma_start(out[0, tb * P:(tb + 1) * P, :], X[:, tb, :]).then_inc(stored, 16)
            sp.wait_ge(stored, 16 * TB)

        @block.tensor
        def _(pe):
            def transposes(name, i, pairs):
                out_bank = to_fill(pe, name, i)
                for (rows, at, n), src in pairs:
                    last = pe.transpose(out_bank[0:rows, at:at + n], src, ident[0:n, 0:n])
                last.then_inc(job_done, 1)

            def product(dst, pairs):
                for k, (lhsT, rhs) in enumerate(pairs):
                    last = pe.matmul(dst, lhsT, rhs, start=k == 0, stop=k == len(pairs) - 1)
                return last

            def to_cols(name, rows, tiles=KT):
                for j in range(tiles // 2):
                    transposes(name, j, [((P, r * T + tb * P, P), rows[:, tb, (2 * j + r) * P:(2 * j + r + 1) * P])
                                         for r in range(2) for tb in range(TB)])

            def normed_to_cols(name, before, rows=X, ready=normed):
                for tb in range(TB):
                    pe.wait_ge(ready, before + tb + 1)
                    for j in range(2):
                        transposes(*((name + "_last", 0) if (tb, j) == (1, 1) else (name, 2 * tb + j)), [((P, r * P, P), rows[:, tb, (4 * j + r) * P:(4 * j + r + 1) * P]) for r in range(4)])
                for j in range(3):
                    wait_emptied(pe, name, j)
                wait_emptied(pe, name + "_last")

            pe.wait_ge(pool_const, 3)
            pe.wait_ge(in_mem, 16)
            to_cols("memT", R)

            wait_emptied(pe, "memT", 3)
            for key, name in (("mem_kv_a", "mem_a"), ("mem_kv_b", "mem_b")):
                w = wait_weights(pe, (key, 0)).rearrange("p (k n) -> p k n", n=HALF)
                b = to_fill(pe, name, 0)
                for m in range(2):
                    last = product(b[:, m * MEM:(m + 1) * MEM], [(w[:, k, m * P:(m + 1) * P], memT[:, k, :]) for k in range(KT)])
                last.then_inc(job_done, 1)
                b = to_fill(pe, name, 1)
                for m in range(2):
                    last = product(b[:, m * MEM:(m + 1) * MEM], [(memT[:, k, m * P:(m + 1) * P], w[:, k, MEM:2 * MEM]) for k in range(KT)])
                last.then_inc(job_done, 1)

            pe.wait_ge(in_pack, 16 * (len(PACK) + 2 * (1 + len(LAYER_PACK))))
            transposes("pack", 0, [((P, 0, PACK_ROWS), pack[0:PACK_ROWS, 0, :]),
                                   ((P, PACK_ROWS, LAYER_ROWS), pack[0:LAYER_ROWS, 1, :]),
                                   ((P, PACK_ROWS + LAYER_ROWS, LAYER_ROWS), pack[0:LAYER_ROWS, 2, :])])

            pe.wait_ge(dist_ready, 1)
            pe.wait_ge(in_dist, 32)
            for i, (at, n) in enumerate(((0, DIST_REV), (DIST_REV, DIST_FWD))):
                b = to_fill(pe, "dist", i)
                pe.matmul(b[0:HEADS, 0:n], dist_rel, dist_sb[:, at:at + n], start=True, stop=True).then_inc(job_done, 1)

            pe.wait_ge(rows_ready, 1)
            wait_emptied(pe, "mem_b", 1)
            for k in range(KT):
                cut = slice(k * P, (k + 1) * P)
                transposes("aT", k, [((P, 0, META), meta[:, cut])] + [((P, META + tb * P, P), R[:, tb, cut]) for tb in range(TB)])
            for k in range(KT):
                wait_emptied(pe, "aT", k)

            def w_in_unit(c):
                return wait_weights(pe, ("w_in", c)).rearrange("p (k n) -> p k n", n=HALF)

            def cols_job(name, i, c, wide):
                w = w_in_unit(c)
                b = to_fill(pe, name, i)
                for r in range(1 if wide else 2):
                    m, n, src = (i, S1, slice(0, S1)) if wide else (2 * i + r, T, slice(META, S1))
                    last = product(b[:, r * T:r * T + n], [(w[:, k, m * P:(m + 1) * P], XT[:, k, src]) for k in range(KT)])
                last.then_inc(job_done, 1)

            def rows_job(name, i, c):
                w = w_in_unit(c)
                b = to_fill(pe, name, i)
                at, n = ((META, P), (META + P, P), (0, META))[i]
                product(b[0:n, :], [(XT[:, k, at:at + n], w[:, k, :]) for k in range(KT)]).then_inc(job_done, 1)

            for i in range(4):
                cols_job("hgf", i, 4, True)
            for i in range(2):
                cols_job("hgq", i, 3, False)
            for i in range(3):
                rows_job("hgi", i, 5)

            def meta_keys():
                pe.wait_ge(hg_fac, 1)
                b = to_fill(pe, "kmT")
                for h in range(HG_HEADS):
                    last = pe.transpose(b[0:META, h * P:(h + 1) * P], fmeta[:, h, :], ident[:, :])
                last.then_inc(job_done, 1)

            def meta_state():
                b = to_fill(pe, "s0")
                wait_emptied(pe, "kmT")
                for h in range(HG_HEADS):
                    cut = slice(h * P, (h + 1) * P)
                    last = pe.matmul(b[:, cut], kT_rows[0:META, cut], hgi[0:META, 2, cut], start=True, stop=True)
                last.then_inc(job_done, 1)

            def block_keys():
                pe.wait_ge(hg_fac, 2)
                b = to_fill(pe, "k1T")
                for h in range(HG_HEADS):
                    last = pe.transpose(b[:, h * P:(h + 1) * P], lev[1][:, h, 0:P], ident[:, :])
                last.then_inc(job_done, 1)

            def block_state():
                b = to_fill(pe, "s1")
                wait_emptied(pe, "k1T")
                for h in range(HG_HEADS):
                    cut = slice(h * P, (h + 1) * P)
                    last = pe.matmul(b[:, cut], kT_rows[:, cut], hgi[:, 0, cut], start=True, stop=True)
                last.then_inc(job_done, 1)

            def level_products(level):
                if level < 7:
                    pe.wait_ge(hg_fac, level + 3)
                for i in range(2):
                    b = to_fill(pe, f"level{level}", i)
                    for c in range(4):
                        h, tb = (4 * i + c) // 2, c % 2
                        cut = slice(tb * P, (tb + 1) * P)
                        if level < 7:
                            left = right = lev[level % 2][:, h, cut]
                        else:
                            left, right = hgk[:, h, META + tb * P:META + (tb + 1) * P], hgq[:, h, cut]
                        last = pe.matmul(b[:, c * P:(c + 1) * P], left, right, start=True, stop=True)
                    last.then_inc(job_done, 1)

            for what, i in first_block_order():
                if what == "kmT":
                    meta_keys()
                elif what == "s0":
                    meta_state()
                elif what == "k1T":
                    block_keys()
                elif what == "s1":
                    block_state()
                elif what == "level":
                    level_products(i)
                elif what == "sbq":
                    cols_job("sbq", i, 0, False)
                elif what == "sbk":
                    cols_job("sbk", i, 1, True)
                elif what == "hgg":
                    rows_job("hgg", i, 6)
                elif what == "sbv":
                    rows_job("sbv", i, 2)

            def sb_unit(i):
                tb, h = divmod(i, SB_HEADS)
                return tb, h, META + (tb + 1) * P, slice(SB_D * (h % 2), SB_D * (h % 2) + SB_D)

            def sb_scores(i):
                tb, h, w, half = sb_unit(i)
                b = to_fill(pe, f"z{i}")
                pe.matmul(b[:, 0:w], sbq[half, h // 2, tb * P:(tb + 1) * P], sbk[half, h // 2, 0:w],
                          start=True, stop=True).then_inc(job_done, 1)

            def sb_transpose(i):
                tb, h, w, half = sb_unit(i)
                pe.wait_ge(w_ready, i + 1)
                src = beta[i % 2]
                b = to_fill(pe, f"wT{i}")
                last = pe.transpose(b[0:META, 0:P], src[:, 0:META], ident[:, :])
                for k in range(tb + 1):
                    last = pe.transpose(b[:, (k + 1) * P:(k + 2) * P], src[:, META + k * P:META + (k + 1) * P], ident[:, :])
                last.then_inc(job_done, 1)

            def sb_values(i):
                tb, h, w, half = sb_unit(i)
                wait_emptied(pe, f"wT{i}")
                dst = bank[4 + tb][:, h * SB_D:(h + 1) * SB_D]
                cut = slice(h * SB_D, (h + 1) * SB_D)
                wT = wTs[i % 2]
                product(dst, [(wT[0:META, 0:P], sbv[0:META, 2, cut])] +
                        [(wT[:, (k + 1) * P:(k + 2) * P], sbv[:, k, cut]) for k in range(tb + 1)]).then_inc(wT_used, 1)

            def hg_outputs(tb):
                pe.wait_ge(hg_fac, 10)
                b = to_fill(pe, "ohg", tb)
                state = (S0, S1t)[tb]
                for h in range(HG_HEADS):
                    cut = slice(h * P, (h + 1) * P)
                    last = product(b[:, cut], [(score[:, 2 * h + tb, :], hgi[:, tb, cut]),
                                               (lev[0][:, h, tb * P:(tb + 1) * P], state[:, cut])])
                last.then_inc(job_done, 1)

            for i in range(16 + 3):
                if i < 16:
                    sb_scores(i)
                if 2 <= i < 18:
                    sb_transpose(i - 2)
                if i >= 3:
                    sb_values(i - 3)
                if i in HG_OUT:
                    hg_outputs(HG_OUT.index(i))

            pe.wait_ge(rows_ready, 2)
            to_cols("mT", R)

            def rows_from(name, keys, lhs):
                for tb in range(TB):
                    for n, key in enumerate(keys):
                        w = wait_weights(pe, key).rearrange("p (k n) -> p k n", n=HALF)
                        b = to_fill(pe, name, 2 * tb + n)
                        product(b[:, :], [(lhs[:, k, tb * P:(tb + 1) * P], w[:, k, :]) for k in range(KT)]).then_inc(job_done, 1)

            wait_emptied(pe, "mT", 3)
            rows_from("w_out", [("w_out", 0), ("w_out", 1)], mixT)

            pe.wait_ge(tables_in, 16 * 3)
            b = to_fill(pe, "cbT")
            for tb in range(TB):
                at = tb * HEADS * CMP_PAD
                pe.transpose(b[:, at:at + P], ctmp[:, 0, tb * P:(tb + 1) * P], ident[:, :])
                last = pe.transpose(b[:, at + P:at + P + 64], ctmp[0:64, 1, tb * P:(tb + 1) * P], ident[0:64, 0:64])
            last.then_inc(job_done, 1)
            normed_to_cols("x2T", 2, R, rows_ready)
            pe.wait_ge(in_small, 16 * 6)
            b = to_fill(pe, "router")
            for tb in range(TB):
                last = product(b[:, tb * 64:tb * 64 + 36], [(XT[:, k, tb * P:(tb + 1) * P], w_router[:, k, :]) for k in range(KT)])
            last.then_inc(job_done, 1)
            pe.wait_ge(gate_ready, 1)
            b = to_fill(pe, "pos")
            sel = [sm(650 + EXPERTS * tb, EXPERTS) for tb in range(TB)]
            everyone = ones[:, 0:P]
            product(b[:, 0:EXPERTS], [(tri[:, :], sel[0])])
            product(b[:, EXPERTS:2 * EXPERTS], [(everyone, sel[0]), (tri[:, :], sel[1])])
            product(b[:, 2 * EXPERTS:3 * EXPERTS], [(everyone, sel[0]), (everyone, sel[1])]).then_inc(job_done, 1)
            for name in ("router", "pos"):
                wait_emptied(pe, name)

            def clear_y():
                for y in range(4):
                    pe.matmul(bank[4 + y][:, :], zeros[:, 0:P], zeros[:, :], start=True, stop=False)

            def down(hidden, w, first_block=None):
                for tb in range(TB):
                    for n in range(2):
                        for q in range(2):
                            last = pe.matmul(bank[4 + 2 * tb + n][:, :], hidden[:, q, tb * P:(tb + 1) * P],
                                             w[:, q, n * HALF:(n + 1) * HALF], start=False, stop=first_block is not None and q == 1)
                    if first_block is not None and tb == 0:
                        last.then_inc(first_block, 1)
                return last

            def up(bank_at, tiles):
                for ab, weights_of in enumerate(tiles):
                    last = product(bank[bank_at][:, ab * T:(ab + 1) * T],
                                   [(weights_of(k), XT[:, k, 0:T]) for k in range(KT)])
                return last

            base = first_unit["moe"]

            def gather(i):
                for k in range(KT):
                    dst = bank[2 + k // 4][:, (k % 4) * P:(k % 4 + 1) * P]
                    last = product(dst, [(R[:, tb, k * P:(k + 1) * P], pair_pick(tb, i)) for tb in range(TB)])
                return last

            def halves(e, at, w):
                for k in range(KT):
                    for j in range(2):
                        last = pe.matmul(bank[e % 2][64 * j:64 * j + 64, at:at + 256], xg_tile(e % 2, k),
                                         w[:, k, 256 * j:256 * j + 256], start=k == 0, stop=k == KT - 1)
                return last

            def turn(e):
                for q in range(2):
                    pe.transpose(bank[e % 2][:, q * P:(q + 1) * P], hid[e % 2][:, q * P:(q + 1) * P], ident[:, :])
                for tb in range(TB):
                    last = pe.transpose(bank[e % 2][:, 256 + tb * P:256 + (tb + 1) * P], gated[:, tb, e % 2 * P:(e % 2 + 1) * P], ident[:, :])
                return last

            def outputs(e, w):
                for f in range(4):
                    j, q = divmod(f, 2)
                    lhsT = hidden_T[e % 2][:, q * P + 64 * j:q * P + 64 * j + 64]
                    for n in range(2):
                        last = pe.matmul(bank[e % 2][64 * n:64 * n + 64, :], lhsT, w[:, f, n * HALF:(n + 1) * HALF],
                                         start=f == 0, stop=f == 3)
                return last

            def combine(e, start=False):
                for tb in range(TB):
                    for n in range(2):
                        half = slice(64 * n, 64 * n + 64)
                        last = pe.matmul(bank[4 + 2 * tb + n][:, :], give[e % 2][half, tb * P:(tb + 1) * P], yrow[e % 2][half, :],
                                         start=start, stop=False)
                return last

            def weights_of(e, which):
                n = base + 3 * e + which
                return ring[:, n % RING, :].rearrange("p (k n) -> p k n", n=D if which == 2 else HALF)

            def arrived(e, which, i):
                n = base + 3 * e + which
                pe.wait_ge(landed[n % RING], i * 16 + use_count(n))
                return weights_of(e, which)

            def moe_gather(pair, i):
                pe.wait_ge(moe["taken"], i * 2 + 2 * pair)
                gather(i + pair).then_inc(moe["gathered"], 1)

            def moe_gate(e, i, first=False):
                w = arrived(e, 0, i)
                pe.wait_ge(moe["taken"], i * 2 + 2 * (e // 2) + 2)
                if not first:
                    pe.wait_ge(moe["row"], i * 2 + (e - 1))
                halves(e, 0, w).then_inc(moe["gate"], 1)

            def moe_up(e, i):
                halves(e, 256, arrived(e, 1, i)).then_inc(moe["up"], 1)

            def moe_turn(e, i):
                pe.wait_ge(moe["gated"], i + (e // 2 + 1))
                pe.wait_ge(moe["hidden"], i * 2 + (e + 1))
                turn(e).then_inc(moe["turned"], 1)

            def moe_down(e, i):
                w = arrived(e, 2, i)
                pe.wait_ge(moe["turned_copied"], i * 2 + (e + 1))
                outputs(e, w).then_inc(moe["down"], 1)

            def moe_combine(e, i, start=False):
                pe.wait_ge(moe["row"], i * 2 + (e + 1))
                combine(e, start).then_inc(moe["combined"], 1)

            def moe_pair(i, first=False):
                moe_gate(1, i, first)
                moe_turn(0, i)
                moe_up(1, i)
                moe_down(0, i)
                moe_gather(1, i)
                if not first:
                    moe_combine(-1, i)
                moe_gate(2, i)
                moe_turn(1, i)
                moe_up(2, i)
                moe_down(1, i)
                moe_combine(0, i, start=first)

            pe.wait_ge(moe["picks"], 1)
            gather(0).then_inc(moe["gathered"], 1)
            moe_gate(0, 0, first=True)
            moe_up(0, 0)
            pe.wait_ge(moe["picks"], 2)
            moe_pair(0, first=True)
            with pe.Fori(1, EXPERTS // 2 - 1) as i:
                moe_pair(i)
            e = EXPERTS - 1
            moe_gate(e, 0)
            moe_turn(e - 1, 0)
            moe_up(e, 0)
            moe_down(e - 1, 0)
            moe_combine(e - 2, 0)
            moe_turn(e, 0)
            moe_combine(e - 1, 0)
            moe_down(e, 0)
            moe_combine(e, 0)

            pe.wait_ge(moe["combined"], EXPERTS)
            pe.wait_ge(moe["extra_known"], 1)
            more = pe.value_load(extra[0:1, 0:1], min_val=0, max_val=PASSES - 1)
            with pe.If(more > 0):
                with pe.Fori(0, more) as p:
                    with pe.Fori(0, EXPERTS // 2) as i:
                        pe.wait_ge(ov["picks"], p + 1)
                        pe.wait_ge(ov["done"], p * EXPERTS + i * 2 + 1)
                        gather(i).then_inc(ov["gathered"], 1)
                        pe.wait_ge(ov["taken"], p * (EXPERTS // 2) + i + 1)
                        pe.wait_ge(ov["loaded"], p * (48 * EXPERTS) + i * 96 + 96)
                        for r in range(2):
                            halves(r, 0, weights_of(r, 0))
                            halves(r, 256, weights_of(r, 1)).then_inc(ov["up"], 1)
                            pe.wait_ge(ov["gated"], p * (EXPERTS // 2) + i + 1)
                            pe.wait_ge(ov["hidden"], p * EXPERTS + i * 2 + (r + 1))
                            turn(r).then_inc(ov["turned"], 1)
                            pe.wait_ge(ov["turned_copied"], p * EXPERTS + i * 2 + (r + 1))
                            outputs(r, weights_of(r, 2)).then_inc(ov["down"], 1)
                            pe.wait_ge(ov["row"], p * EXPERTS + i * 2 + (r + 1))
                            combine(r).then_inc(ov["done"], 1)
            for y in range(4):
                last = pe.matmul(bank[4 + y][:, :], zeros[:, 0:P], zeros[:, :], start=False, stop=True)
            last.then_inc(sums_ready, 1)

            attention = [0]

            def attend(layer):
                mine = [u for u, key in enumerate(att) if key[0] == layer]

                def scores(u):
                    _, kind, pair, tb, h = att[u]
                    before = u - 4 if kind == "nsa" else u - 1 if kind == "mem" and att[u - 2][1] == "nsa" else u - 2
                    if before >= mine[0]:
                        pe.wait_ge(at_m, halves_by(before))
                    for seg in range(2):
                        r = h % 2 if kind == "nsa" else seg
                        half = slice(64 * r, 64 * r + 64)
                        if kind == "mem":
                            q, k, w = qmT[half, pair, :], km[layer][half, pair, :], MEM
                        else:
                            q, k, w = qT[half, pair, :], kT[half, seg if kind == "nsa" else pair, :], P * (tb + 1)
                        dst = bank[u % 4][:, seg * w:(seg + 1) * w] if kind == "nsa" else bank[2 * (u % 2) + seg][:, 0:w]
                        last = pe.matmul(dst, q[:, tb * P:(tb + 1) * P], k[:, 0:w], start=True, stop=True)
                        if kind != "nsa" or seg == 1:
                            last.then_inc(at_l, 1)

                def blocks_of(u):
                    _, kind, pair, tb, h = att[u]
                    return 2 if kind == "mem" else tb + 1

                def trans(u):
                    pe.wait_ge(at_p, u + 1)
                    if u >= 2:
                        pe.wait_ge(at_tc, u - 1)
                    nb = blocks_of(u)
                    for seg in range(2):
                        for b in range(nb):
                            at = (seg * nb + b) * P
                            last = pe.transpose(bank[4 + u % 2][:, at:at + P], logit[u % LOGITS][:, seg, b * P:(b + 1) * P], ident[:, :])
                    last.then_inc(at_t, 1)

                def values(u):
                    _, kind, pair, tb, h = att[u]
                    g, first = group_of(u)
                    pe.wait_ge(at_tc, u + 1)
                    if first and g >= 2:
                        pe.wait_ge(at_oc, g - 1)
                    nb = blocks_of(u)
                    o = bank[6 + g % 2]
                    for seg in range(2):
                        r = h % 2 if kind == "nsa" else seg
                        dst = o[64 * r:64 * r + 64, tb * P:(tb + 1) * P]
                        pairs = []
                        if kind == "nsa" and seg == 0:
                            pairs.append((vz[:, h % 4, :], pcT[:, h // 4, tb * P:(tb + 1) * P]))
                        for b in range(nb):
                            at = (seg * nb + b) * P
                            if kind == "nsa":
                                v = vrow0[:, b, 64 * seg:64 * seg + 64]
                            elif kind == "moba":
                                v = vrow[:, b, 64 * (h + seg):64 * (h + seg) + 64]
                            else:
                                v = vm[layer][:, b, 64 * (h + seg):64 * (h + seg) + 64]
                            pairs.append((v, pT[u % 2][:, at:at + P]))
                        for k, (lhsT, rhs) in enumerate(pairs):
                            last = pe.matmul(dst, lhsT, rhs, start=k == 0 and not (kind == "nsa" and seg == 1),
                                             stop=k == len(pairs) - 1 and not (kind == "nsa" and seg == 0))
                    last.then_inc(at_o, 1)

                n = len(mine)
                for i in range(n + LOGITS):
                    if i < n:
                        scores(mine[i])
                    if LOGITS - 1 <= i < n + LOGITS - 1:
                        trans(mine[i - (LOGITS - 1)])
                    if i >= LOGITS:
                        values(mine[i - LOGITS])

            normed_to_cols("xTa", 0)
            wa = [wait_weights(pe, ("a_in", c))[:, 0:KT * (A_CUTS[c + 1] - A_CUTS[c])].rearrange("p (k n) -> p k n", k=KT)
                  for c in range(3)]

            def a_cols(at, n):
                c = max(c for c in range(3) if A_CUTS[c] <= at)
                return lambda k: wa[c][:, k, at - A_CUTS[c]:at - A_CUTS[c] + n]

            def twice(b, at, w_of):
                for r in range(2):
                    last = product(b[64 * r:64 * r + 64, at:at + T], [(w_of(k), XT[:, k, 0:T]) for k in range(KT)])
                return last

            def tiles(name, job, w_of_tiles):
                b = to_fill(pe, name, job)
                for i, w_of in enumerate(w_of_tiles):
                    last = product(b[:, i * T:(i + 1) * T], [(w_of(k), XT[:, k, 0:T]) for k in range(KT)])
                last.then_inc(job_done, 1)

            for j in range(3):
                tiles("a_q", j, [a_cols((2 * j + r) * P, P) for r in range(2)])
            b = to_fill(pe, "a_kv", 0)
            twice(b, 0, a_cols(768, 64))
            twice(b, T, a_cols(832, 64)).then_inc(job_done, 1)
            b = to_fill(pe, "a_kv", 1)
            twice(b, 0, a_cols(896, 64))
            twice(b, T, a_cols(1024, 64)).then_inc(job_done, 1)
            b = to_fill(pe, "a_v")
            for tb in range(TB):
                last = product(b[:, tb * T:tb * T + 228], [(XT[:, k, tb * P:(tb + 1) * P], a_cols(960, 228)(k)) for k in range(KT)])
            last.then_inc(job_done, 1)

            pe.wait_ge(cmp_in, 1)
            wc = [wait_weights(pe, (key, 0)).rearrange("p (j n) -> p j n", n=CMP_HID) for key in ("cmp_k", "cmp_v")]
            b = to_fill(pe, "cmp_h")
            for j in range(16):
                for kv in range(2):
                    last = pe.matmul(b[32 * kv:32 * kv + N_CMP, 0:CMP_HID], logit[2][:, kv, j * N_CMP:(j + 1) * N_CMP], wc[kv][:, j, :],
                                     start=j == 0, stop=j == 15)
            last.then_inc(job_done, 1)
            wait_emptied(pe, "cmp_h")
            for kv in range(2):
                b = to_fill(pe, "cmp_hT", kv)
                rows = slice(32 * kv, 32 * kv + N_CMP)
                for m in range(2):
                    last = pe.transpose(b[:, m * CMP_PAD:m * CMP_PAD + N_CMP], hrow[rows, m * P:(m + 1) * P], ident[rows, rows])
                last.then_inc(job_done, 1)
            wait_emptied(pe, "cmp_hT", 1)
            pe.wait_ge(in_small, 16 * 6)
            b = to_fill(pe, "cmp_kv")
            for r in range(2):
                product(b[64 * r:64 * r + 64, 0:CMP_PAD], [(w2[:, 0, m, :], hidT[:, m, 0:CMP_PAD]) for m in range(2)])
            for r in range(4):
                last = product(b[32 * r:32 * r + 32, 64:128], [(hidT[:, 2 + m, :], w2[:, 1, m, :]) for m in range(2)])
            last.then_inc(job_done, 1)
            wait_emptied(pe, "cmp_kv")
            for tb in range(TB):
                b = to_fill(pe, "cmp_l", tb)
                for pair in range(PAIRS):
                    last = pe.matmul(b[:, pair * 32:pair * 32 + 32], qT[:, pair, tb * P:(tb + 1) * P],
                                     kz[:, :, :].rearrange("p a b -> p (a b)"), start=True, stop=True)
                last.then_inc(job_done, 1)
            tiles("a_qm", 0, [a_cols(1188 + r * P, P) for r in range(2)])
            pe.wait_ge(cmp_x, 2)
            for j, n in enumerate((2, 1)):
                b = to_fill(pe, "cmp_pT", j)
                for i in range(n):
                    for tb in range(TB):
                        last = pe.transpose(b[:, i * T + tb * P:i * T + (tb + 1) * P],
                                            pc[:, tb, (2 * j + i) * P:(2 * j + i + 1) * P], ident[:, :])
                last.then_inc(job_done, 1)
            for name, i in (("cmp_l", 0), ("cmp_l", 1), ("a_qm", 0), ("cmp_pT", 0), ("cmp_pT", 1)):
                wait_emptied(pe, name, i)
            attend(0)
            pe.wait_ge(at_oc, 8)
            rows_from("a_out", [("a_out", 0), ("a_out", 1)], mixT)

            def ffn(layer):
                ph = phase_sems[f"ffn{layer}"]
                base = first_unit[f"ffn{layer}"]

                def ffn_up(j, k):
                    n = base + 3 * (j // 2) + j % 2
                    pe.wait_ge(landed[n % RING], k * 32 + use_count(n))
                    w = ring[:, n % RING, :].rearrange("p (k h n) -> p k h n", h=2, n=256)
                    if j >= 1:
                        pe.wait_ge(ph["hidden"], k * 8 + max(2 * j - 2, 1))
                    for q in range(2):
                        last = up(2 * (j % 2) + q, [lambda kk, h=h, q=q: w[:, kk, h, q * P:(q + 1) * P] for h in range(2)])
                        last.then_inc(ph["tile"], 1)

                def ffn_down(j, k, final=False):
                    n = base + 3 * (j // 2) + (2 if j < STEPS_F - 1 else 1)
                    if j % 2 == 0:
                        pe.wait_ge(landed[n % RING], k * 16 + use_count(n))
                    w = ring[:, n % RING, :].rearrange("p (k n) -> p k n", n=D)[:, 2 * (j % 2):2 * (j % 2) + 2, :]
                    pe.wait_ge(ph["hidden"], k * 8 + (2 * j + 2))
                    down(hb[j % 2], w, ph["first"] if final else None).then_inc(ph["used"], 1)

                clear_y()
                ffn_up(0, 0)
                with pe.Fori(0, 2) as i:
                    for u in range(4):
                        ffn_up(u + 1, i)
                        ffn_down(u, i)
                for j in (8, 9):
                    ffn_up(j + 1, 0)
                    ffn_down(j, 0)
                ffn_down(10, 0, final=True)

            pe.wait_ge(zero_ready, 1)
            normed_to_cols("xTf0", 2)
            ffn(0)

            normed_to_cols("xTb", 4)
            wk = [wait_weights(pe, ("kv", c)).rearrange("p (k n) -> p k n", n=HALF) for c in range(3)]

            def kv_cols(at, n):
                return lambda k: wk[at // HALF][:, k, at % HALF:at % HALF + n]

            for j in range(3):
                tiles("b_k", j, [kv_cols((2 * j + r) * P, P) for r in range(2)])
            for i, (tb, at, n) in enumerate([(tb, at, n) for at, n in ((768, 256), (1024, 512)) for tb in range(TB)]):
                b = to_fill(pe, "b_v", i)
                product(b[:, 0:n], [(XT[:, k, tb * P:(tb + 1) * P], kv_cols(at, n)(k)) for k in range(KT)]).then_inc(job_done, 1)
            wq = [wait_weights(pe, ("b_in", c)).rearrange("p (k n) -> p k n", n=HALF) for c in range(2)]

            def b_cols(at):
                return lambda k: wq[at // HALF][:, k, at % HALF:at % HALF + P]

            for j in range(3):
                tiles("b_q", j, [b_cols((2 * j + r) * P) for r in range(2)])
            tiles("b_qm", 0, [b_cols(768 + r * P) for r in range(2)])
            for j in range(3):
                wait_emptied(pe, "b_q", j)
            wait_emptied(pe, "b_qm")
            attend(1)
            pe.wait_ge(at_oc, 16)
            rows_from("b_out", [("b_out", 0), ("b_out", 1)], mixT)
            normed_to_cols("xTf1", 6)
            ffn(1)

        @block.scalar
        def _(act):
            step = chained(act, act_step)

            def empty(name, i, *moves):
                b = filled(act, name, i)
                for dst, src, func in moves:
                    last = act.activation(dst, src(b), func)
                last.then_inc(emptied_a, 1)

            act.wait_ge(pool_const, 1)
            for j in range(4):
                empty("memT", j, (memT[:, 2 * j:2 * j + 2, :], lambda b: b[:, :].rearrange("p (a t) -> p a t", t=T), ACT.Copy))
            act.wait_ge(in_x, 32)
            step(act.activation(junk, X[:, 0, :], ACT.Square, accum_out=sm(0, 1)))
            step(act.activation(junk, X[:, 1, :], ACT.Square, accum_out=sm(1, 1)))
            act.activation(junk[0:META, :], meta, ACT.Square, accum_out=small[0:META, 2:3]).then_inc(sq_ready, 1)

            act.wait_ge(stat_ready, 1)
            act.activation(sm(3, 3), sm(3, 3), ACT.Sqrt).then_inc(sq_ready, 1)
            for l, name in enumerate(("mem_a", "mem_b")):
                for i, dst in enumerate((km[l], vm[l])):
                    empty(name, i, (dst[:, :, :].rearrange("p a b -> p (a b)"), lambda b: b[:, :], ACT.Copy))
            empty("pack", 0, (cols[:, :], lambda b: b[:, 0:PACK_ROWS + 2 * LAYER_ROWS], ACT.Copy))
            for i, (at, n) in enumerate(((0, DIST_REV), (DIST_REV, DIST_FWD))):
                empty("dist", i, (dist_out[:, at:at + n], lambda b, n=n: b[0:HEADS, 0:n], ACT.Copy))

            act.wait_ge(lbound_ready, 1)
            act.activation(sm(16, 8), sm(16, 8), ACT.Exp).then_inc(lbound_ready, 1)

            for h in range(HG_HEADS):
                b = filled(act, "hgf", h)
                act.activation(logf[:, h, :], b[:, 0:S1], ACT.Sigmoid)
                act.activation(hgk[:, h, :], b[:, 0:S1], ACT.Sigmoid, scale=-1.0).then_inc(emptied_a, 1)
            pair = lambda b: b[:, :].rearrange("p (a t) -> p a t", t=T)
            for i in range(2):
                empty("hgq", i, (hgq[:, 2 * i:2 * i + 2, :], pair, ACT.Silu))
            act.wait_ge(dist_stored, 16)
            act.wait_ge(hg_f, 1)
            act.activation(logf[:, :, :], logf[:, :, :], ACT.Ln).then_inc(hg_log, 1)
            for i in range(3):
                n = META if i == 2 else P
                empty("hgi", i, (hgi[0:n, i, :], lambda b, n=n: b[0:n, :], ACT.Copy))
            def decay(k):
                dst = [fmeta[:, :, :], lev[1][:, :, 0:P]] + [lev[level % 2][:, :, :] for level in range(7)] + [lev[0][:, :, :]]
                act.wait_ge(hg_arg, k + 1)
                act.activation(dst[k], dst[k], ACT.Exp).then_inc(hg_exp, 1)

            decay(0)
            decay(1)
            act.activation(sm(24, 4), bcum[:, :, P - 1], ACT.Exp).then_inc(hg_q, 1)
            decay(2)
            empty("hgg", 0, (hgg[:, 0, :], lambda b: b[:, :], ACT.Silu))
            empty("kmT", 0, (kT_rows[0:META, :], lambda b: b[0:META, :], ACT.Copy))
            empty("s0", 0, (S0, lambda b: b[:, :], ACT.Copy))
            empty("hgg", 1, (hgg[:, 1, :], lambda b: b[:, :], ACT.Silu))
            empty("k1T", 0, (kT_rows, lambda b: b[:, :], ACT.Copy))
            decay(3)
            for i in range(2):
                empty("sbq", i, (sbq[:, 2 * i:2 * i + 2, :], pair, ACT.Copy))
                decay(4 + i)
            for i in range(4):
                empty("sbk", i, (sbk[:, i, :], lambda b: b[:, 0:S1], ACT.Copy))
                if i < 3:
                    decay(6 + i)
            for i in range(3):
                n = META if i == 2 else P
                empty("sbv", i, (sbv[0:n, i, :], lambda b, n=n: b[0:n, :], ACT.Copy))
            decay(9)

            def sb_sigmoids(i):
                w = META + (i // SB_HEADS + 1) * P
                wait_emptied(act, f"z{i}")
                if i >= 2:
                    act.wait_ge(w_ready, i - 1)
                    act.wait_ge(job_done, jobs.number(f"wT{i - 2}") + 1)
                act.activation(beta[i % 2][:, 0:w], zm[i % 2][:, 0:w], ACT.Sigmoid)
                act.activation(keep[i % 2][:, 0:w], zm[i % 2][:, 0:w], ACT.Sigmoid, scale=-1.0).then_inc(sig_ready, 1)

            def sb_transposed(i):
                tb = i // SB_HEADS
                b = filled(act, f"wT{i}")
                if i >= 2:
                    act.wait_ge(wT_used, i - 1)
                act.activation(wTs[i % 2][0:META, 0:P], b[0:META, 0:P], ACT.Copy)
                act.activation(wTs[i % 2][:, P:P * (tb + 2)], b[:, P:P * (tb + 2)], ACT.Copy).then_inc(emptied_a, 1)

            for i in range(16 + 2):
                if i >= 2:
                    sb_transposed(i - 2)
                if i < 16:
                    sb_sigmoids(i)

            act.wait_ge(stat_ready, 2)
            act.activation(sm(30, 24), sm(30, 24), ACT.Sqrt).then_inc(sq_ready, 1)

            def empty_gained(name, gain_at):
                for j in range(4):
                    b = filled(act, name, j)
                    for r in range(2):
                        k = 2 * j + r
                        last = act.activation(XT[:, k, 0:T], b[:, r * T:(r + 1) * T], ACT.Copy, scale=cols[:, gain_at + k:gain_at + k + 1])
                    last.then_inc(emptied_a, 1)

            empty_gained("mT", PACK["sb_gain"][0])
            for tb in range(TB):
                wait_emptied(act, "w_out", 2 * tb + 1)
                act.activation(R[:, tb, :], X[:, tb, :], ACT.Square, accum_out=sm(6 + tb, 1)).then_inc(sq_ready, 1)
                act.wait_ge(stat_ready, 3 + tb)
                act.activation(sm(8 + tb, 1), sm(8 + tb, 1), ACT.Sqrt).then_inc(sq_ready, 1)
            empty("cbT", 0, (cbias[:, :, :].rearrange("p a b -> p (a b)"), lambda b: b[:, 0:2 * HEADS * CMP_PAD], ACT.Copy))

            def empty_normed(name, gain, bias):
                for tb in range(TB):
                    for j in range(2 - tb):
                        b = filled(act, name, 2 * tb + j)
                        for r in range(4):
                            k = 4 * j + r
                            dst, src = XT[:, k, tb * P:(tb + 1) * P], b[:, r * P:(r + 1) * P]
                            if bias is None:
                                last = act.activation(dst, src, ACT.Copy, scale=cols[:, gain + k:gain + k + 1])
                            else:
                                last = act.activation(dst, src, ACT.Identity, scale=cols[:, gain + k:gain + k + 1],
                                                      bias=cols[:, bias + k:bias + k + 1])
                        last.then_inc(emptied_a, 1)

            empty_normed("x2T", PACK["g_ffn"][0], None)

            act.wait_ge(router_arg, 1)
            act.activation(sm(200, 8), sm(200, 8), ACT.Exp).then_inc(router_exp, 1)
            act.wait_ge(router_arg, 2)
            act.activation(sm(240, 2), sm(240, 2), ACT.Exp).then_inc(router_exp, 1)

            def silu(e):
                return act.activation(gact[e % 2], bank[e % 2][:, 0:256], ACT.Silu)

            def turned(e):
                return act.activation(turned_sb[e % 2], bank[e % 2][:, :], ACT.Copy)

            def moe_silu(e, i, first=False):
                act.wait_ge(moe["up"], i * 2 + (e + 1))
                if not first:
                    act.wait_ge(moe["hidden"], i * 2 + (e - 1))
                silu(e).then_inc(moe["silu"], 1)

            def moe_turned(e, i, first=False):
                act.wait_ge(moe["turned"], i * 2 + (e + 1))
                if not first:
                    act.wait_ge(moe["combined"], i * 2 + (e - 1))
                turned(e).then_inc(moe["turned_copied"], 1)

            def moe_pair(i, first=False):
                moe_turned(0, i, first)
                moe_silu(1, i, first)
                moe_turned(1, i, first)
                moe_silu(2, i)

            moe_silu(0, 0, first=True)
            moe_pair(0, first=True)
            with act.Fori(1, EXPERTS // 2 - 1) as i:
                moe_pair(i)
            e = EXPERTS - 1
            moe_turned(e - 1, 0)
            moe_silu(e, 0)
            moe_turned(e, 0)

            act.wait_ge(moe["extra_known"], 1)
            more = act.value_load(extra[0:1, 0:1], min_val=0, max_val=PASSES - 1)
            with act.If(more > 0):
                with act.Fori(0, more) as p:
                    with act.Fori(0, EXPERTS // 2) as i:
                        for r in range(2):
                            count = p * EXPERTS + i * 2 + (r + 1)
                            act.wait_ge(ov["up"], count)
                            silu(r).then_inc(ov["silu"], 1)
                            act.wait_ge(ov["turned"], count)
                            turned(r).then_inc(ov["turned_copied"], 1)

            for tb in range(TB):
                act.wait_ge(y_used, tb + 1)
                act.activation(R[:, tb, :], X[:, tb, :], ACT.Square, accum_out=sm(10 + tb, 1)).then_inc(sq_ready, 1)
            for tb in range(TB):
                act.wait_ge(stat_ready, 5 + tb)
                act.activation(sm(12 + tb, 1), sm(12 + tb, 1), ACT.Sqrt).then_inc(sq_ready, 1)

            def empty_ln(name, layer, which):
                at = PACK_ROWS + layer * LAYER_ROWS
                empty_normed(name, at + LAYER_PACK[f"ln{which}_g"][0], at + LAYER_PACK[f"ln{which}_b"][0])

            empty_normed("xTa", PACK["g_final"][0], None)
            for j in range(3):
                empty("a_q", j, (qT[:, 2 * j:2 * j + 2, :], pair, ACT.Copy))
            b = filled(act, "a_kv", 0)
            for kv in range(2):
                act.activation(shift2[0:64, kv, :], b[0:64, kv * T:(kv + 1) * T], ACT.Copy)
                last = act.activation(shift2[64:128, kv, 0:T - 1], b[64:128, kv * T + 1:(kv + 1) * T], ACT.Copy)
            last.then_inc(emptied_a, 1)
            empty("a_kv", 1, (kT[:, 0:2, :], pair, ACT.Copy))
            empty("a_v", 0, (vrow0[:, :, :].rearrange("p b (c n) -> p b c n", c=2),
                             lambda b: b[:, :].rearrange("p (b c n) -> p b c n", b=2, n=64)[:, :, 0:3:2, :], ACT.Copy),
                  (sm(260, 72).rearrange("p (b g) -> p b g", b=2),
                   lambda b: b[:, :].rearrange("p (b n) -> p b n", b=2)[:, :, 192:228], ACT.Sigmoid))
            act.wait_ge(pool_step, 1)
            empty("cmp_h", 0, *[(hrow[32 * kv:32 * kv + N_CMP, :], lambda b, kv=kv: b[32 * kv:32 * kv + N_CMP, 0:CMP_HID],
                                 ACT.Gelu_apprx_tanh) for kv in range(2)])
            for kv in range(2):
                empty("cmp_hT", kv, (hidT[:, 2 * kv:2 * kv + 2, 0:N_CMP],
                                     lambda b: b[:, 0:2 * CMP_PAD].rearrange("p (m n) -> p m n", n=CMP_PAD)[:, :, 0:N_CMP], ACT.Copy))
            b = filled(act, "cmp_kv")
            for r in range(2):
                act.activation(kz[64 * r:64 * r + 64, r, :], b[64 * r:64 * r + 64, 0:CMP_PAD], ACT.Copy)
            for r in range(4):
                last = act.activation(vz[32 * r:32 * r + 32, r, :], b[32 * r:32 * r + 32, 64:128], ACT.Copy)
            last.then_inc(emptied_a, 1)
            act.wait_ge(cmp_e, 1)
            act.activation(sm(340, 12 * 16 + 0), sm(340, 192), ACT.Exp).then_inc(cmp_e, 1)
            act.wait_ge(cmp_e, 3)
            act.activation(sm(340, 192), sm(340, 192), ACT.Exp).then_inc(cmp_e, 1)
            empty("a_qm", 0, (qmT[:, :, :], pair, ACT.Copy))
            for j, n in enumerate((2, 1)):
                empty("cmp_pT", j, (pcT[:, 2 * j:2 * j + n, :], lambda b, n=n: b[:, 0:n * T].rearrange("p (a t) -> p a t", t=T), ACT.Copy))

            def attend(layer):
                mine = [u for u, key in enumerate(att) if key[0] == layer]

                def exps(u):
                    act.wait_ge(at_x, u + 1)
                    w = width(u)
                    for seg in range(2):
                        last = act.activation(logit[u % LOGITS][:, seg, 0:w], logit[u % LOGITS][:, seg, 0:w], ACT.Exp,
                                              bias=sm(540 + 8 * (u % LOGITS) + seg, 1), accum_out=sm(542 + 8 * (u % LOGITS) + seg, 1))
                    last.then_inc(at_e, 1)

                def trans(u):
                    act.wait_ge(at_t, u + 1)
                    if u >= 2:
                        act.wait_ge(at_o, u - 1)
                    n = 2 * width(u)
                    act.activation(pT[u % 2][:, 0:n], bank[4 + u % 2][:, 0:n], ACT.Copy).then_inc(at_tc, 1)

                for i in range(len(mine) + LOGITS - 1):
                    if i < len(mine):
                        exps(mine[i])
                    if i >= LOGITS - 1:
                        trans(mine[i - (LOGITS - 1)])

            attend(0)

            def norm_root(k):
                for tb in range(TB):
                    act.wait_ge(stat_ready, 7 + 2 * k + tb)
                    act.activation(sm(600 + tb, 1), sm(600 + tb, 1), ACT.Sqrt).then_inc(sq_ready, 1)

            def ffn(layer):
                ph = phase_sems[f"ffn{layer}"]
                at_w = PACK_ROWS + layer * LAYER_ROWS
                at_b = PACK["conv_b"][0] + layer * FFT

                def gelu_step(j, k):
                    for q in range(2):
                        act.wait_ge(ph["tile"], k * 8 + (2 * j + q + 1))
                        if j >= 1:
                            act.wait_ge(ph["hidden"], k * 8 + max(2 * j - 2 + q, 1))
                        act.activation(work[(2 * j + q) % 4], bank[2 * (j % 2) + q][:, 0:T], ACT.Identity,
                                       scale=cols[:, bass.ds(k * 8 + (at_w + 2 * FFT + 2 * j + q), 1)],
                                       bias=cols[:, bass.ds(k * 8 + (at_b + 2 * j + q), 1)]).then_inc(ph["act"], 1)
                    for q in range(2):
                        act.wait_ge(mulp[f"ffn{layer}"], k * 8 + (2 * j + q + 1))
                        w = work[(2 * j + q) % 4]
                        act.activation(w, w, ACT.Gelu_apprx_tanh).then_inc(act2[f"ffn{layer}"], 1)

                gelu_step(0, 0)
                with act.Fori(0, 2) as i:
                    for u in range(4):
                        gelu_step(u + 1, i)
                for j in (9, 10):
                    gelu_step(j, 0)

            norm_root(0)
            empty_ln("xTf0", 0, 1)
            ffn(0)
            norm_root(1)
            empty_ln("xTb", 0, 2)
            for j in range(3):
                empty("b_k", j, (kT[:, 2 * j:2 * j + 2, :], pair, ACT.Copy))
            for i, (tb, at, n) in enumerate([(tb, at, n) for at, n in ((0, 256), (256, 512)) for tb in range(TB)]):
                empty("b_v", i, (vrow[:, tb, at:at + n], lambda b, n=n: b[:, 0:n], ACT.Copy))
            for j in range(3):
                empty("b_q", j, (qT[:, 2 * j:2 * j + 2, :], pair, ACT.Copy))
            empty("b_qm", 0, (qmT[:, :, :], pair, ACT.Copy))
            attend(1)
            norm_root(2)
            empty_ln("xTf1", 1, 1)
            ffn(1)
            norm_root(3)

        @block.vector
        def _(dve):
            step = chained(dve, dve_step)
            tt, ts, stt = dve.tensor_tensor, dve.tensor_scalar, dve.scalar_tensor_tensor

            def emptied_self():
                dve.wait_ge(emptied_v, emptied_self.count)
            emptied_self.count = 0

            def count_emptied(instruction):
                emptied_self.count += 1
                instruction.then_inc(emptied_v, 1)

            dve.memset(arena[BUCKETS:BUCKETS + 1, at_hgi + 900:at_hgi + 900 + HEADS], NEG).then_inc(dist_ready, 1)

            dve.wait_ge(sq_ready, 1)
            step(ts(sm(3, 2), sm(0, 2), 1.0 / D, EPS, ALU.mult, ALU.add))
            ts(small[0:META, 5:6], small[0:META, 2:3], 1.0 / D, EPS, ALU.mult, ALU.add).then_inc(stat_ready, 1)
            dve.wait_ge(sq_ready, 2)
            step(dve.reciprocal(sm(3, 3), sm(3, 3)))
            dve.wait_ge(job_done, jobs.number("memT", 3) + 1)
            ts(meta, meta, small[0:META, 5:6], None, ALU.mult)
            for tb in range(TB):
                last = ts(R[:, tb, :], X[:, tb, :], sm(3 + tb, 1), None, ALU.mult)
            last.then_inc(rows_ready, 1)

            wait_emptied(dve, "pack")
            l0, l1 = (cols[:, PACK["lb"][0] + 4 * i:PACK["lb"][0] + 4 * i + 4] for i in range(2))
            step(tt(sm(650, 4), l0, l1, ALU.max))
            tt(sm(16, 4), l0, sm(650, 4), ALU.subtract)
            tt(sm(20, 4), l1, sm(650, 4), ALU.subtract).then_inc(lbound_ready, 1)

            for k in range(KT):
                b = filled(dve, "aT", k)
                at = PACK["g_mix"][0] + k
                count_emptied(ts(XT[:, k, :], b[:, 0:S1], cols[:, at:at + 1], None, ALU.mult))

            dve.wait_ge(lbound_ready, 2)
            step(tt(sm(650, 4), sm(16, 4), sm(20, 4), ALU.add))
            step(dve.reciprocal(sm(650, 4), sm(650, 4)))
            step(tt(sm(16, 4), sm(16, 4), sm(650, 4), ALU.mult))
            step(ts(sm(20, 4), sm(16, 4), -1.0, 1.0, ALU.mult, ALU.add))

            for h in range(HG_HEADS):
                wait_emptied(dve, "hgf", h)
                ts(logf[:, h, :], logf[:, h, :], sm(20 + h, 1), sm(16 + h, 1), ALU.mult, ALU.add)
                last = ts(hgk[:, h, :], hgk[:, h, :], sm(20 + h, 1), None, ALU.mult)
            last.then_inc(hg_f, 1)
            dve.wait_ge(hg_log, 1)
            dve.wait_ge(pool_const, 3)
            for h in range(HG_HEADS):
                dve.tensor_tensor_scan(bmeta[:, h, :], ones[:, 0:META], logf[:, h, 0:META], 0.0, ALU.mult, ALU.add)
                for c in range(TB):
                    last = dve.tensor_tensor_scan(bcum[:, h, c * P:(c + 1) * P], ones[:, 0:P],
                                                  logf[:, h, META + c * P:META + (c + 1) * P], 0.0, ALU.mult, ALU.add)
            step(last)
            tt(fmeta[:, :, :], bmeta[:, :, META - 1:META].broadcast_to([P, 4, META]), bmeta[:, :, :], ALU.subtract).then_inc(hg_arg, 1)
            tt(lev[1][:, :, 0:P], bcum[:, :, P - 1:P].broadcast_to([P, 4, P]), bcum[:, :, 0:P], ALU.subtract).then_inc(hg_arg, 1)

            def sides(t, half):
                v = t.rearrange("p h (x two r) -> p h x two r", two=2, r=half)
                return v[:, :, :, 0, :], v[:, :, :, 1, :]

            def flat_sides(t, half):
                v = t.rearrange("p h t -> p (h t)").rearrange("p (x two r) -> p x two r", two=2, r=half)
                return v[:, :, 0, :], v[:, :, 1, :]

            def level_args(level):
                half = P >> (level + 1)
                left, right = flat_sides(bcum[:, :, :], half)
                to_left, to_right = flat_sides(lev[level % 2][:, :, :], half)
                shape = list(left.shape)
                ref = left[:, :, half - 1:half].broadcast_to(shape)
                tt(to_left, ref, left, ALU.subtract)
                tt(to_right, right, ref, ALU.subtract).then_inc(hg_arg, 1)

            def level_factors(level):
                half = P >> (level + 1)
                dve.wait_ge(hg_exp, level + 3)
                to_left, to_right = sides(lev[level % 2][:, :, :], half)
                tt(to_left, to_left, sides(hgk[:, :, META:S1], half)[0], ALU.mult)
                tt(to_right, to_right, sides(hgq[:, :, :], half)[1], ALU.mult).then_inc(hg_fac, 1)

            def level_scores(level):
                for i in range(2):
                    b = filled(dve, f"level{level}", i)
                    count_emptied(dve.copy_predicated(score[:, 4 * i:4 * i + 4, :],
                                                      level_mask[:, level:level + 1, :].broadcast_to([P, 4, P]),
                                                      b[:, :].rearrange("p (a t) -> p a t", t=P)))

            dve.wait_ge(hg_exp, 1)
            tt(fmeta[:, :, :], fmeta[:, :, :], hgk[:, :, 0:META], ALU.mult).then_inc(hg_fac, 1)
            level_args(0)
            dve.wait_ge(hg_exp, 2)
            tt(lev[1][:, :, 0:P], lev[1][:, :, 0:P], hgk[:, :, META:META + P], ALU.mult).then_inc(hg_fac, 1)
            wait_emptied(dve, "hgq", 1)
            b = filled(dve, "s1")
            wait_emptied(dve, "s0")
            dve.wait_ge(hg_q, 1)
            for h in range(HG_HEADS):
                cut = slice(h * P, (h + 1) * P)
                last = stt(S1t[:, cut], S0[:, cut], sm(24 + h, 1), b[:, cut], ALU.mult, ALU.add)
            count_emptied(last)
            dve.wait_ge(mask_ready, 1)
            for level in range(7):
                if level < 6:
                    if level == 0:
                        dve.wait_ge(job_done, jobs.number("k1T") + 1)
                    else:
                        dve.wait_ge(job_done, jobs.number(f"level{level - 1}", 1) + 1)
                    level_args(level + 1)
                level_factors(level)
                if level >= 1:
                    level_scores(level - 1)
                    emptied_self()
            level_scores(6)
            emptied_self()
            level_scores(7)
            dve.wait_ge(job_done, jobs.number("level6", 1) + 1)
            dve.tensor_copy(lev[0][:, :, :], bcum[:, :, :]).then_inc(hg_arg, 1)
            dve.wait_ge(hg_exp, 10)
            tt(lev[0][:, :, :], lev[0][:, :, :], hgq[:, :, :], ALU.mult).then_inc(hg_fac, 1)

            def sb_masked(i):
                tb = i // SB_HEADS
                w = META + (tb + 1) * P
                b = filled(dve, f"z{i}")
                count_emptied(stt(zm[i % 2][:, 0:w], b[:, 0:w], SCALE, sbmask[:, tb, 0:w], ALU.mult, ALU.add))

            def sb_shares(i):
                tb = i // SB_HEADS
                w = META + (tb + 1) * P
                if i % SB_HEADS < 2:
                    step(dve.memset(keep[i % 2][:, w:w + 1], 1.0))
                dve.wait_ge(sig_ready, i + 1)
                step(dve.tensor_tensor_scan(zm[i % 2][:, w - 1::-1], keep[i % 2][:, w:0:-1], ones[:, 0:w], 1.0, ALU.mult, ALU.mult))
                tt(beta[i % 2][:, 0:w], beta[i % 2][:, 0:w], zm[i % 2][:, 0:w], ALU.mult).then_inc(w_ready, 1)

            waiting = XT[:, :, :].rearrange("p k t -> p (k t)")[:, 0:4 * HALF].rearrange("p (a n) -> p a n", n=HALF)
            squares = logf[:, :, :].rearrange("p a b -> p (a b)")[:, 0:HALF]
            head_parts = ((SB_HEADS, SB_D, 30), (HG_HEADS, P, 38))

            def heads_arrived(part, tb):
                n, d, at = head_parts[part]
                rows = waiting[:, 2 * tb + part, :]
                if part == 1:
                    b = filled(dve, "ohg", tb)
                    wait_emptied(dve, "sbv", 2)
                    count_emptied(dve.tensor_copy(rows, b[:, :]))
                    emptied_self()
                else:
                    dve.wait_ge(wT_used, SB_HEADS * (tb + 1))
                    step(dve.tensor_copy(rows, bank[4 + tb][:, :]))
                step(tt(squares, rows, rows, ALU.mult))
                ms = sm(at + 12 * tb, n)
                step(dve.reduce_sum(ms, squares.rearrange("p (h d) -> p h d", d=d), axis=AX.X))
                last = ts(ms, ms, 1.0 / d, EPS, ALU.mult, ALU.add)
                if part == 1:
                    step(last)
                    last = tt(rows, rows, hgg[:, tb, :], ALU.mult)
                return last

            wait_emptied(dve, "hgg", 1)
            dve.wait_ge(mask_ready, 3)
            for i in range(17):
                if i < 16:
                    if i >= 2:
                        dve.wait_ge(w_ready, i - 1)
                    sb_masked(i)
                if i >= 1:
                    sb_shares(i - 1)
                if i in HG_OUT:
                    step(heads_arrived(1, HG_OUT.index(i)))
                if i == 12:
                    step(heads_arrived(0, 0))
            heads_arrived(0, 1).then_inc(stat_ready, 1)
            dve.wait_ge(sq_ready, 3)
            step(dve.reciprocal(sm(30, 24), sm(30, 24)))
            for part, (n, d, at) in enumerate(head_parts):
                for tb in range(TB):
                    split = lambda v: v.rearrange("p (h d) -> p h d", d=d)
                    last = tt(split(R[:, tb, part * HALF:(part + 1) * HALF]), split(waiting[:, 2 * tb + part, :]),
                              sm(at + 12 * tb, n).unsqueeze(2).broadcast_to([P, n, d]), ALU.mult)
            last.then_inc(rows_ready, 1)

            for tb in range(TB):
                for n in range(2):
                    b = filled(dve, "w_out", 2 * tb + n)
                    v = X[:, tb, n * HALF:(n + 1) * HALF]
                    count_emptied(tt(v, v, b[:, :], ALU.add))
                dve.wait_ge(sq_ready, 4 + 2 * tb)
                ts(sm(8 + tb, 1), sm(6 + tb, 1), 1.0 / D, EPS, ALU.mult, ALU.add).then_inc(stat_ready, 1)
                dve.wait_ge(sq_ready, 5 + 2 * tb)
                step(dve.reciprocal(sm(8 + tb, 1), sm(8 + tb, 1)))
                ts(R[:, tb, :], X[:, tb, :], sm(8 + tb, 1), None, ALU.mult).then_inc(rows_ready, 1)
            emptied_self()

            def empty_last(name, columns):
                b = filled(dve, name + "_last")
                gain, bias = columns
                for r in range(4):
                    k = 4 + r
                    dst, src = XT[:, k, P:2 * P], b[:, r * P:(r + 1) * P]
                    if bias is None:
                        last = ts(dst, src, cols[:, gain + k:gain + k + 1], None, ALU.mult)
                    else:
                        last = ts(dst, src, cols[:, gain + k:gain + k + 1], cols[:, bias + k:bias + k + 1], ALU.mult, ALU.add)
                count_emptied(last)

            empty_last("x2T", (PACK["g_ffn"][0], None))

            per_tb = lambda v: v.rearrange("p (b n) -> p b n", b=TB)
            dve.wait_ge(in_small, 16 * 6)
            b = filled(dve, "router")
            rl = per_tb(sm(650, 72))
            count_emptied(tt(rl, per_tb(b[:, 0:128])[:, :, 0:36], bias36[:, :].unsqueeze(1).broadcast_to([P, TB, 36]), ALU.add))
            emptied_self()
            wide = lambda v, n: v.unsqueeze(2).broadcast_to([P, TB, n])
            iota = lambda n: sm(900, n).unsqueeze(1).broadcast_to([P, TB, n])

            def first_best(dst, src, best, n, scratch, index):
                step(tt(per_tb(scratch), src, wide(best, n), ALU.is_lt))
                step(stt(per_tb(scratch), per_tb(scratch), 100.0, iota(n), ALU.mult, ALU.add))
                step(dve.tensor_reduce(index, per_tb(scratch), axis=AX.X, op=ALU.min))
                step(tt(dst, iota(n), wide(index, n), ALU.is_equal))

            step(dve.reduce_max(sm(722, 2), rl[:, :, 0:GROUPS], axis=AX.X))
            tt(per_tb(sm(200, 8)), rl[:, :, 0:GROUPS], wide(sm(722, 2), GROUPS), ALU.subtract).then_inc(router_arg, 1)
            first_best(per_tb(sm(736, 8)), rl[:, :, 0:GROUPS], sm(722, 2), GROUPS, sm(726, 8), sm(734, 2))
            step(ts(sm(736, 8), sm(736, 8), -1.0, -NEG, ALU.add, ALU.mult))
            el = sm(744, 64).rearrange("p (b g e) -> p b g e", b=TB, g=GROUPS)
            for tb in range(TB):
                last = tt(el[:, tb], rl[:, tb, GROUPS:36].rearrange("p (g e) -> p g e", g=GROUPS),
                          sm(736 + 4 * tb, 4).unsqueeze(2).broadcast_to([P, GROUPS, PER_GROUP]), ALU.add)
            step(last)
            elf = per_tb(sm(744, 64))
            step(dve.reduce_max(sm(808, 2), elf, axis=AX.X))
            oh1, oh2 = per_tb(sm(64, 64)), per_tb(sm(128, 64))
            first_best(oh1, elf, sm(808, 2), EXPERTS, sm(128, 64), sm(810, 2))
            step(stt(elf, oh1, 3 * NEG, elf, ALU.mult, ALU.add))
            step(dve.reduce_max(sm(812, 2), elf, axis=AX.X))
            tt(sm(240, 2), sm(812, 2), sm(808, 2), ALU.subtract).then_inc(router_arg, 1)
            first_best(oh2, elf, sm(812, 2), EXPERTS, sm(128, 64), sm(814, 2))
            tt(sm(650, 64), sm(64, 64), sm(128, 64), ALU.add).then_inc(gate_ready, 1)
            dve.wait_ge(router_exp, 1)
            step(dve.reduce_sum(sm(816, 2), per_tb(sm(200, 8)), axis=AX.X))
            step(dve.reciprocal(sm(816, 2), sm(816, 2)))
            dve.wait_ge(router_exp, 2)
            step(ts(sm(870, 2), sm(240, 2), 1.0, None, ALU.add))
            step(dve.reciprocal(sm(870, 2), sm(870, 2)))
            step(tt(sm(870, 2), sm(870, 2), sm(816, 2), ALU.mult))
            step(tt(sm(872, 2), sm(870, 2), sm(240, 2), ALU.mult))
            b = filled(dve, "pos")
            pos = sm(744, 64)
            count_emptied(dve.tensor_copy(sm(744, 96), b[:, 0:96]))
            emptied_self()
            step(ts(pos, pos, 1.0, None, ALU.add))
            step(tt(pos, pos, sm(650, 64), ALU.mult))
            step(ts(pos, pos, -1.0, None, ALU.add))

            def picks(experts):
                at = slice(experts.start * SLOTS, experts.stop * SLOTS)
                n = experts.stop - experts.start
                for tb in range(TB):
                    last = tt(pick[:, tb, at].rearrange("p (e s) -> p e s", s=SLOTS),
                              sm(900, SLOTS).unsqueeze(1).broadcast_to([P, n, SLOTS]),
                              pos[:, tb * EXPERTS + experts.start:tb * EXPERTS + experts.stop].unsqueeze(2).broadcast_to([P, n, SLOTS]),
                              ALU.is_equal)
                return last

            picks(slice(0, 2)).then_inc(moe["picks"], 1)
            picks(slice(2, EXPERTS)).then_inc(moe["picks"], 1)
            weight = sm(200, 64)
            for tb in range(TB):
                last = ts(sm(200 + EXPERTS * tb, EXPERTS), sm(64 + EXPERTS * tb, EXPERTS), sm(870 + tb, 1), None, ALU.mult)
            step(last)
            for tb in range(TB):
                at = EXPERTS * tb
                last = stt(sm(200 + at, EXPERTS), sm(128 + at, EXPERTS), sm(872 + tb, 1), sm(200 + at, EXPERTS), ALU.mult, ALU.add)
            step(last)
            step(dve.reduce_max(sm(840, 1), sm(808, 32), axis=AX.X))
            step(ts(sm(841, 1), sm(840, 1), SLOTS + 0.5, None, ALU.is_ge))
            for c in range(2, PASSES):
                step(stt(sm(841, 1), sm(840, 1), c * SLOTS + 0.5, sm(841, 1), ALU.is_ge, ALU.add))
            dve.tensor_copy(extra[:, :], sm(841, 1)).then_inc(moe["extra_known"], 1)

            gains = cols[:, PACK["g_ffn"][0]:PACK["g_ffn"][0] + KT]

            def take_gathered(j):
                dst = xg[:, :, :].rearrange("p r (k s) -> p k r s", s=SLOTS)
                for r in range(2):
                    last = tt(dst[:, 4 * j:4 * j + 4, r, :],
                              bank[2 + j][:, :].rearrange("p (k r s) -> p k r s", r=2, s=SLOTS)[:, :, r, :],
                              gains[:, 4 * j:4 * j + 4].unsqueeze(2).broadcast_to([P, 4, SLOTS]), ALU.mult)
                return last

            def hidden(e):
                return tt(hid[e % 2], gact[e % 2], bank[e % 2][:, 256:512], ALU.mult)

            def row(e):
                return dve.tensor_copy(yrow[e % 2], bank[e % 2][:, :])

            def gates_of(i):
                for tb in range(TB):
                    last = tt(gated[:, tb, :].rearrange("p (r c s) -> p r c s", r=2, c=2),
                              pair_pick(tb, i).rearrange("p (r s) -> p r s", r=2).unsqueeze(2).broadcast_to([P, 2, 2, SLOTS]),
                              weight[:, bass.ds(i * 2 + tb * EXPERTS, 2)].unsqueeze(2).unsqueeze(3).broadcast_to([P, 2, 2, SLOTS]),
                              ALU.mult)
                return last

            def moe_taken(pair, i):
                dve.wait_ge(moe["gathered"], i + (pair + 1))
                for j in range(2):
                    take_gathered(j).then_inc(moe["taken"], 1)

            def moe_gated(pair, i):
                dve.wait_ge(moe["turned"], i * 2 + 2 * pair)
                gates_of(i + pair).then_inc(moe["gated"], 1)

            def moe_hidden(e, i, first=False):
                dve.wait_ge(moe["silu"], i * 2 + (e + 1))
                if not first:
                    dve.wait_ge(moe["turned"], i * 2 + (e - 1))
                hidden(e).then_inc(moe["hidden"], 1)

            def moe_row(e, i, first=False):
                dve.wait_ge(moe["down"], i * 2 + (e + 1))
                if not first:
                    dve.wait_ge(moe["combined"], i * 2 + (e - 1))
                row(e).then_inc(moe["row"], 1)

            def moe_pair(i, first=False):
                moe_hidden(1, i, first)
                moe_row(0, i, first)
                moe_taken(1, i)
                moe_gated(1, i)
                moe_hidden(2, i)
                moe_row(1, i, first)

            moe_taken(0, 0)
            gates_of(0).then_inc(moe["gated"], 1)
            moe_hidden(0, 0, first=True)
            moe_pair(0, first=True)
            with dve.Fori(1, EXPERTS // 2 - 1) as i:
                moe_pair(i)
            e = EXPERTS - 1
            moe_hidden(e, 0)
            moe_row(e - 1, 0)
            moe_row(e, 0)

            dve.wait_ge(moe["combined"], EXPERTS)
            more = dve.value_load(extra[0:1, 0:1], min_val=0, max_val=PASSES - 1)
            with dve.If(more > 0):
                dve.memset(sm(860, 1), 0.0).then_inc(ov["done"], 1)
                with dve.Fori(0, more) as p:
                    dve.wait_ge(ov["done"], p * EXPERTS + 1)
                    ts(pos, pos, -float(SLOTS), None, ALU.add).then_inc(ov_places, 1)
                    dve.wait_ge(ov_places, p + 1)
                    picks(slice(0, EXPERTS)).then_inc(ov["picks"], 1)
                    with dve.Fori(0, EXPERTS // 2) as i:
                        dve.wait_ge(ov["gathered"], p * (EXPERTS // 2) + i + 1)
                        take_gathered(0)
                        take_gathered(1).then_inc(ov["taken"], 1)
                        dve.wait_ge(ov["picks"], p + 1)
                        dve.wait_ge(ov["done"], p * EXPERTS + i * 2 + 1)
                        gates_of(i).then_inc(ov["gated"], 1)
                        for r in range(2):
                            count = p * EXPERTS + i * 2 + (r + 1)
                            dve.wait_ge(ov["silu"], count)
                            hidden(r).then_inc(ov["hidden"], 1)
                            dve.wait_ge(ov["down"], count)
                            row(r).then_inc(ov["row"], 1)
                dve.wait_ge(ov["done"], more * EXPERTS + 1)
                dve.memset(sm(861, 1), 0.0).then_inc(ov_through, 1)
            dve.wait_ge(sums_ready, 1)

            for tb in range(TB):
                for n in range(2):
                    v = X[:, tb, n * HALF:(n + 1) * HALF]
                    last = tt(v, v, bank[4 + 2 * tb + n][:, :], ALU.add)
                last.then_inc(y_used, 1)

            for tb in range(TB):
                dve.wait_ge(sq_ready, 8 + tb)
                ts(sm(12 + tb, 1), sm(10 + tb, 1), 1.0 / D, EPS, ALU.mult, ALU.add).then_inc(stat_ready, 1)
            for tb in range(TB):
                dve.wait_ge(sq_ready, 10 + tb)
                step(dve.reciprocal(sm(12 + tb, 1), sm(12 + tb, 1)))
                ts(X[:, tb, :], X[:, tb, :], sm(12 + tb, 1), None, ALU.mult).then_inc(normed, 1)
            dve.wait_ge(rowvec_in, 16)
            empty_last("xTa", (PACK["g_final"][0], None))
            for tb in range(TB):
                last = tt(X[:, tb, :], X[:, tb, :], rowvec[:, 0, :], ALU.mult)
            last.then_inc(ln_done, 1)

            wait_emptied(dve, "a_kv", 0)
            for kv, pe_at in enumerate((PACK["pe_k"][0], PACK["pe_v"][0])):
                v = shift2[:, kv, :]
                v = bass.AP(tensor=v.tensor, offset=v.offset, ap=[list(v.ap[0]), [2, 16], [CMP_STRIDE, N_CMP]])
                last = tt(logit[2][:, kv, 0:16 * N_CMP].rearrange("p (j n) -> p j n", n=N_CMP), v,
                          cols[:, pe_at:pe_at + 16].unsqueeze(2).broadcast_to([P, 16, N_CMP]), ALU.add)
            last.then_inc(cmp_in, 1)
            dve.wait_ge(pool_step, 1)
            wait_emptied(dve, "a_v", 0)
            for tb in range(TB):
                heads = lambda v: v.rearrange("p (h n) -> p h n", n=CMP_PAD)
                lc = sm(340, HEADS * CMP_PAD)
                b = filled(dve, "cmp_l", tb)
                count_emptied(stt(lc, b[:, 0:HEADS * CMP_PAD], SCALE, cbias[:, tb, :], ALU.mult, ALU.add))
                emptied_self()
                step(dve.reduce_max(sm(564, HEADS), heads(lc), axis=AX.X))
                tt(heads(lc), heads(lc), sm(564, HEADS).unsqueeze(2).broadcast_to([P, HEADS, CMP_PAD]), ALU.subtract).then_inc(cmp_e, 1)
                dve.wait_ge(cmp_e, 2 * tb + 2)
                step(stt(lc, cbias[:, tb, :], NEG / 10, lc, ALU.is_gt, ALU.mult))
                step(dve.reduce_sum(sm(576, HEADS), heads(lc), axis=AX.X))
                step(ts(sm(576, HEADS), sm(576, HEADS), TINY, None, ALU.max))
                step(dve.reciprocal(sm(576, HEADS), sm(576, HEADS)))
                gates = sm(260 + 36 * tb, 36).rearrange("p (h g) -> p h g", g=3)
                step(tt(sm(576, HEADS), sm(576, HEADS), gates[:, :, 0], ALU.mult))
                tt(pc[:, tb, :].rearrange("p (h n) -> p h n", n=32)[:, :, 0:CMP_PAD], heads(lc),
                   sm(576, HEADS).unsqueeze(2).broadcast_to([P, HEADS, CMP_PAD]), ALU.mult).then_inc(cmp_x, 1)
                dve.wait_ge(cmp_x, tb + 1)

            def attend(layer):
                mine = [u for u, key in enumerate(att) if key[0] == layer]

                def biased(u):
                    _, kind, pair, tb, h = att[u]
                    w = width(u)
                    if u >= LOGITS:
                        dve.wait_ge(at_t, u - (LOGITS - 1))
                    done = halves_by(u)
                    if kind == "nsa":
                        dve.wait_ge(at_l, done)
                        stt(logit[u % LOGITS][:, :, 0:w], bank[u % 4][:, 0:2 * w].rearrange("p (s n) -> p s n", s=2), SCALE,
                            btab[:, h, T - w:T].unsqueeze(1).broadcast_to([P, 2, w]), ALU.mult, ALU.add).then_inc(at_m, 1)
                    else:
                        for seg in range(2):
                            dve.wait_ge(at_l, done - 1 + seg)
                            dst, src = logit[u % LOGITS][:, seg, 0:w], bank[2 * (u % 2) + seg][:, 0:w]
                            if kind == "mem":
                                last = ts(dst, src, SCALE, None, ALU.mult)
                            else:
                                last = stt(dst, src, SCALE, btab[:, h + seg, T - w:T], ALU.mult, ALU.add)
                            last.then_inc(at_m, 1)
                    dve.wait_ge(at_m, done)
                    dve.tensor_reduce(sm(540 + 8 * (u % LOGITS), 2), logit[u % LOGITS][:, :, 0:w], axis=AX.X, op=ALU.max,
                                      negate=True).then_inc(at_x, 1)

                def row_scale(u):
                    _, kind, pair, tb, h = att[u]
                    dve.wait_ge(at_e, u + 1)
                    r = sm(544 + 8 * (u % LOGITS), 2)
                    ins = dve.reciprocal(r, sm(542 + 8 * (u % LOGITS), 2))
                    if kind == "nsa":
                        step(ins)
                        ins = tt(r, r, sm(260 + 36 * tb + 3 * h + 1, 2), ALU.mult)
                    ins.then_inc(at_r, 1)

                def outputs(u):
                    g, _ = group_of(u)
                    if groups[g][-1] != u:
                        return
                    _, kind, pair, _, _ = att[u]
                    dve.wait_ge(at_o, u + 1)
                    k = (PAIRS if kind == "mem" else 0) + pair
                    dve.tensor_copy(mixT[:, k, :], bank[6 + g % 2][:, 0:T]).then_inc(at_oc, 1)

                n = len(mine)
                for i in range(n + LOGITS + 1):
                    if i < n:
                        biased(mine[i])
                    if 1 <= i < n + 1:
                        row_scale(mine[i - 1])
                    if i >= LOGITS + 1:
                        outputs(mine[i - (LOGITS + 1)])

            def layer_norm(k, add, turned=None):
                mean = lambda tb: sm(628 + 2 * tb, 1)
                root = lambda tb: sm(600 + tb, 1)

                def centred(tb):
                    dve.wait_ge(sq_ready, 12 + 2 * k + tb)
                    step(dve.reciprocal(root(tb), root(tb)))
                    return ts(X[:, tb, :], X[:, tb, :], mean(tb), root(tb), ALU.subtract, ALU.mult)

                def gained(tb):
                    v = X[:, tb, :]
                    dve.wait_ge(rowvec_in, 16 * (3 + 2 * k))
                    step(tt(v, v, rowvec[:, 0, :], ALU.mult))
                    tt(v, v, rowvec[:, 1, :], ALU.add).then_inc(ln_done, 1)

                for tb in range(TB):
                    for n in range(2):
                        add(tb, n)
                        last = dve.bn_stats(sm(604 + 12 * tb + 6 * n, 6), X[:, tb, n * HALF:(n + 1) * HALF])
                    step(last)
                    step(dve.bn_aggr(sm(628 + 2 * tb, 2), sm(604 + 12 * tb, 12).rearrange("p (a s) -> p a s", s=6)))
                    ts(root(tb), sm(629 + 2 * tb, 1), LN_EPS, None, ALU.add).then_inc(stat_ready, 1)
                    centred(tb).then_inc(normed, 1)
                    if turned is None:
                        dve.wait_ge(normed, 3 + 2 * k + tb)
                        gained(tb)
                if turned is not None:
                    empty_last(*turned)
                    for tb in range(TB):
                        gained(tb)

            def ln_cols(name, layer, which):
                at = PACK_ROWS + layer * LAYER_ROWS
                return name, (at + LAYER_PACK[f"ln{which}_g"][0], at + LAYER_PACK[f"ln{which}_b"][0])

            def add_row(name):
                def add(tb, n):
                    b = filled(dve, name, 2 * tb + n)
                    v = X[:, tb, n * HALF:(n + 1) * HALF]
                    count_emptied(stt(v, v, ALPHA, b[:, :], ALU.mult, ALU.add))
                    emptied_self()
                return add

            def add_y(name):
                def add(tb, n):
                    if tb == 0:
                        dve.wait_ge(phase_sems[name]["first"], 1)
                    else:
                        dve.wait_ge(phase_sems[name]["used"], STEPS_F)
                    v = X[:, tb, n * HALF:(n + 1) * HALF]
                    step(stt(v, v, ALPHA, bank[4 + 2 * tb + n][:, :], ALU.mult, ALU.add))
                return add

            def ffn(layer):
                name = f"ffn{layer}"
                ph = phase_sems[name]
                at_w = PACK_ROWS + layer * LAYER_ROWS

                def conv_step(j, k):
                    tap = lambda t, q: cols[:, bass.ds(k * 8 + (at_w + t * FFT + 2 * j + q), 1)]
                    for q in range(2):
                        w, a = work[(2 * j + q) % 4], bank[2 * (j % 2) + q]
                        dve.wait_ge(ph["act"], k * 8 + (2 * j + q + 1))
                        stt(w[:, 1:T], a[:, 0:T - 1], tap(1, q), w[:, 1:T], ALU.mult, ALU.add).then_inc(conv1[name], 1)
                        dve.wait_ge(conv1[name], k * 8 + (2 * j + q + 1))
                        stt(w[:, 2:T], a[:, 0:T - 2], tap(0, q), w[:, 2:T], ALU.mult, ALU.add).then_inc(mulp[name], 1)
                    for q in range(2):
                        dve.wait_ge(act2[name], k * 8 + (2 * j + q + 1))
                        if j >= 1:
                            dve.wait_ge(ph["used"], k * 4 + max(j - 1, 1))
                        tt(hb[j % 2][:, q, :], work[(2 * j + q) % 4], bank[2 * (j % 2) + q][:, T:2 * T], ALU.mult).then_inc(ph["hidden"], 1)

                conv_step(0, 0)
                with dve.Fori(0, 2) as i:
                    for u in range(4):
                        conv_step(u + 1, i)
                for j in (9, 10):
                    conv_step(j, 0)

            attend(0)
            layer_norm(0, add_row("a_out"), ln_cols("xTf0", 0, 1))
            ffn(0)
            layer_norm(1, add_y("ffn0"), ln_cols("xTb", 0, 2))
            attend(1)
            layer_norm(2, add_row("b_out"), ln_cols("xTf1", 1, 1))
            ffn(1)
            layer_norm(3, add_y("ffn1"))

        @block.gpsimd
        def _(pool):
            step = chained(pool, pool_chain)

            pool.memset(small[:, :], 1.0).then_inc(pool_const, 1)
            step(pool.memset(ident[:, :], 0.0))
            pool.affine_select(out=ident[:, :], in_=ident[:, :], compare_op=ALU.not_equal, fill=1.0, base=0,
                               pattern=[[-1, P]], channel_multiplier=1).then_inc(pool_const, 1)
            pool.memset(ones[:, :], 1.0).then_inc(pool_const, 1)
            pool.memset(zeros[:, :], 0.0).then_inc(zero_ready, 1)
            step(pool.memset(tri[:, :], 1.0))
            step(pool.affine_select(out=tri[:, :], in_=tri[:, :], compare_op=ALU.is_ge, fill=0.0, base=-1,
                                    pattern=[[1, P]], channel_multiplier=-1))
            pool.wait_ge(pool_const, 3)
            pool.iota(iota_i[:, :], pattern=[[1, SLOTS]], base=0, channel_multiplier=0).then_inc(iota_done, 1)
            pool.wait_ge(iota_done, 1)
            step(pool.tensor_copy(sm(900, SLOTS), iota_i[:, :]))
            for level in range(7):
                half = P >> (level + 1)
                nb = P // (2 * half)
                v = level_maskf[:, :].rearrange("p (b r) -> p b r", b=nb)
                step(pool.memset(level_maskf[:, :], 1.0))
                for base, pattern, mult in ((0, [[-2 * half, nb], [0, 2 * half]], 1),
                                            (half - 1, [[2 * half, nb], [0, 2 * half]], -1),
                                            (-half, [[0, nb], [1, 2 * half]], 0)):
                    step(pool.affine_select(out=v, in_=v, compare_op=ALU.is_ge, fill=0.0, base=base,
                                            pattern=pattern, channel_multiplier=mult))
                step(pool.tensor_copy(level_mask[:, level, :], level_maskf[:, :]))
            step(pool.tensor_copy(level_mask[:, 7, :], ident[:, :]))
            wait_emptied(pool, "pack")
            pool.memset(score[:, :, :], 0.0).then_inc(mask_ready, 1)

            wait_emptied(pool, "dist", 1)
            pool.dma_start(by_dist, dist_out).then_inc(dist_stored, 16)
            pool.wait_ge(dist_stored, 16)
            row = DIST_REV + DIST_FWD
            pool.dma_start(by_token, bass.AP(tensor=by_dist.tensor, offset=P - 1,
                                             ap=[[row, HEADS], [-1, P], [1, T]])).then_inc(expanded, 16)
            pool.dma_start(by_block, bass.AP(tensor=by_dist.tensor, offset=DIST_REV + FWD_ZERO - (CMP_LEN - 1),
                                             ap=[[row, HEADS], [-CMP_STRIDE, CMP_PAD], [1, T]])).then_inc(expanded, 16)
            pool.wait_ge(job_done, jobs.number("aT", KT - 1) + 1)
            step(pool.memset(sbmask[:, :, :], 0.0))
            for tb in range(TB):
                v = sbmask[:, tb, META:S1]
                pool.affine_select(out=v, in_=v, compare_op=ALU.is_ge, fill=NEG, base=tb * P - 1,
                                   pattern=[[-1, T]], channel_multiplier=1).then_inc(mask_ready, 1)

            pool.wait_ge(job_done, jobs.number("mT", 3) + 1)
            pool.wait_ge(rows_ready, 2)
            pool.wait_ge(expanded, 32)
            pool.dma_start(btab[:, :, :], by_token.rearrange("h p j -> p h j")).then_inc(tables_in, 16)
            blocks_flat = by_block.rearrange("h n t -> (h n) t")
            pool.dma_start(ctmp[:, 0, :], blocks_flat[0:P, :]).then_inc(tables_in, 16)
            pool.dma_start(ctmp[0:64, 1, :], blocks_flat[P:P + 64, :]).then_inc(tables_in, 16)

            def load_rowvec(*vectors):
                for i, v in enumerate(vectors):
                    src = bass.AP(tensor=v.tensor, offset=v.offset, ap=[[0, P], [1, D]])
                    pool.dma_start(rowvec[:, i, :], src).then_inc(rowvec_in, 16)

            load_rowvec(g_final)

            pool.wait_ge(y_used, 1)
            for t in (pc, vz, hidT):
                pool.memset(t[:, :, :], 0.0)
            pool.memset(kz[:, :, :], 0.0).then_inc(pool_step, 1)
            pool.wait_ge(ln_done, 1)
            load_rowvec(ln1_g_2[0], ln1_b_2[0])

            def attend(layer):
                for u in [u for u, key in enumerate(att) if key[0] == layer]:
                    pool.wait_ge(at_r, u + 1)
                    w = width(u)
                    v = logit[u % LOGITS][:, :, 0:w]
                    pool.tensor_tensor(v, v, sm(544 + 8 * (u % LOGITS), 2).unsqueeze(2).broadcast_to([P, 2, w]), ALU.mult).then_inc(at_p, 1)

            attend(0)
            pool.wait_ge(ln_done, 3)
            load_rowvec(ln2_g_2[0], ln2_b_2[0])
            pool.wait_ge(ln_done, 5)
            load_rowvec(ln1_g_2[1], ln1_b_2[1])
            attend(1)
            pool.wait_ge(ln_done, 7)
            load_rowvec(ln2_g_2[1], ln2_b_2[1])
    return nc


_INS = ("x", "meta_tokens", "lb_logits", "g_mix", "w_in", "sb_gain", "hg_gain", "w_out", "g_ffn", "w_router_group",
        "b_router_group", "w_router_expert", "b_router_expert", "w_expert_gate", "w_expert_up", "w_expert_down",
        "g_final", "mem_2", "rel_bias_2", "a_w_in_2", "a_cmp_pe_k_2", "a_cmp_w1_k_2", "a_cmp_w2_k_2", "a_cmp_pe_v_2",
        "a_cmp_w1_v_2", "a_cmp_w2_v_2", "a_w_mem_kv_2", "a_w_out_2", "shared_w_kv_2", "b_w_in_2", "b_w_mem_kv_2",
        "b_w_out_2", "ln1_g_2", "ln1_b_2", "ln2_g_2", "ln2_b_2", "ffn_w_in_2", "ffn_conv_w_2", "ffn_conv_b_2",
        "ffn_w_out_2")


def kernel(**inputs):
    import numpy as _np
    import concourse.bacc as _bacc
    from concourse import mybir as _mybir
    from concourse.bass_utils import run_bass_kernel_spmd as _run

    nc = _bacc.Bacc("TRN2", target_bir_lowering=False, num_devices=1)
    arrays, args = {}, {}
    for name in _INS + ("dist_onehot",):
        a = bucket_table() if name == "dist_onehot" else _np.ascontiguousarray(inputs[name])
        arrays[f"in_{name}"] = a
        args[name] = nc.dram_tensor(f"in_{name}", a.shape, _mybir.dt.from_np(a.dtype), kind="ExternalInput").ap()
    args["out"] = nc.dram_tensor("out_0", (1, T, D), F32, kind="ExternalOutput").ap()
    build(nc, **args)
    r = _run(nc, [arrays], core_ids=[0])
    return r.results[0]["out_0"]
```
